# Optimizing a Trainium2 kernel written in Bass

```python
import jax, jax.numpy as jnp
from jax import lax
import numpy as np

D_MODEL = 1024
BATCH = 1
SEQ = 512
DEPTH = 2

N_MIXERS = 2
ALPHA = (2 * DEPTH) ** 0.25
BETA = (8 * DEPTH) ** -0.25
LN_EPS = 1e-5
N_A = (DEPTH + 1) // 2
N_B = DEPTH // 2
D_FF = 2816
ML_HEADS = 4
ML_DQK = D_MODEL // (2 * ML_HEADS)
ML_DV = D_MODEL // ML_HEADS
ML_QK = ML_HEADS * ML_DQK
ML_PROJ = 2 * ML_QK + 2 * D_MODEL + 4 * ML_HEADS
CHUNK = 64
HEAD_DIM = 64
N_Q_HEADS = D_MODEL // HEAD_DIM
N_KV_HEADS = 4
GROUP = N_Q_HEADS // N_KV_HEADS
WINDOW = 128
BLOCK = 128
AT_PROJ = (N_Q_HEADS + 2 * N_KV_HEADS) * HEAD_DIM
MASK_VALUE = -1e30


def layer_norm(x, g, b):
    xf = x.astype(jnp.float32)
    mu = jnp.mean(xf, axis=-1, keepdims=True)
    var = jnp.mean(jnp.square(xf - mu), axis=-1, keepdims=True)
    return ((xf - mu) * lax.rsqrt(var + LN_EPS) * g + b).astype(x.dtype)

def swiglu(x, w_in, w_out):
    gu = x @ w_in
    g, u = gu[..., :D_FF], gu[..., D_FF:]
    return (jax.nn.silu(g) * u) @ w_out

def mlstm_chunkwise(q, k, v, i_pre, f_pre):
    B, H, S, dk = q.shape
    dv = v.shape[-1]
    nc = S // CHUNK
    q = q.astype(jnp.float32).reshape(B, H, nc, CHUNK, dk)
    k = k.astype(jnp.float32).reshape(B, H, nc, CHUNK, dk)
    v = v.astype(jnp.float32).reshape(B, H, nc, CHUNK, dv)
    logf = jax.nn.log_sigmoid(f_pre.astype(jnp.float32)).reshape(B, H, nc, CHUNK)
    ig = i_pre.astype(jnp.float32).reshape(B, H, nc, CHUNK)
    g = jnp.cumsum(logf, axis=-1)
    G = g[..., -1]
    w_end = G[..., None] - g + ig
    a = jnp.max(w_end, axis=-1)
    e_end = jnp.exp(w_end - a[..., None])
    K_c = jnp.einsum('bhcl,bhclv,bhclk->bhcvk', e_end, v, k)
    N_c = jnp.einsum('bhcl,bhclk->bhck', e_end, k)

    def step(carry, inp):
        C, n, m = carry
        Gc, ac, Kc, Nc = inp
        m_new = jnp.maximum(Gc + m, ac)
        sp = jnp.exp(Gc + m - m_new)
        sc = jnp.exp(ac - m_new)
        C_new = sp[..., None, None] * C + sc[..., None, None] * Kc
        n_new = sp[..., None] * n + sc[..., None] * Nc
        return (C_new, n_new, m_new), (C, n, m)

    init = (jnp.zeros((B, H, dv, dk), jnp.float32), jnp.zeros((B, H, dk), jnp.float32),
            jnp.zeros((B, H), jnp.float32))
    xs = (jnp.moveaxis(G, 2, 0), jnp.moveaxis(a, 2, 0), jnp.moveaxis(K_c, 2, 0), jnp.moveaxis(N_c, 2, 0))
    _, (C0, n0, m0) = lax.scan(step, init, xs)
    C0 = jnp.moveaxis(C0, 0, 2)
    n0 = jnp.moveaxis(n0, 0, 2)
    m0 = jnp.moveaxis(m0, 0, 2)

    tril = jnp.tril(jnp.ones((CHUNK, CHUNK), dtype=bool))
    dmat = g[..., :, None] - g[..., None, :] + ig[..., None, :]
    dmat = jnp.where(tril, dmat, MASK_VALUE)
    inter_log = g + m0[..., None]
    m_out = jnp.maximum(inter_log, jnp.max(dmat, axis=-1))
    wts = jnp.exp(dmat - m_out[..., None])
    s_inter = jnp.exp(inter_log - m_out)
    s_qk = jnp.einsum('bhcjd,bhcsd->bhcjs', q, k) * wts
    num = jnp.einsum('bhcjs,bhcsv->bhcjv', s_qk, v) + s_inter[..., None] * jnp.einsum('bhcvd,bhcjd->bhcjv', C0, q)
    den = jnp.sum(s_qk, axis=-1) + s_inter * jnp.einsum('bhcd,bhcjd->bhcj', n0, q)
    den = jnp.maximum(jnp.abs(den), jnp.exp(-m_out))
    h = num / den[..., None]
    return h.reshape(B, H, S, dv)

def mlstm_mixer(x, w_in, gate_b, norm_g, w_out):
    B, S, _ = x.shape
    p = x @ w_in
    q = p[..., :ML_QK].reshape(B, S, ML_HEADS, ML_DQK).transpose(0, 2, 1, 3)
    k = p[..., ML_QK:2 * ML_QK].reshape(B, S, ML_HEADS, ML_DQK).transpose(0, 2, 1, 3) * (ML_DQK ** -0.5)
    v = p[..., 2 * ML_QK:2 * ML_QK + D_MODEL].reshape(B, S, ML_HEADS, ML_DV).transpose(0, 2, 1, 3)
    o = p[..., 2 * ML_QK + D_MODEL:2 * ML_QK + 2 * D_MODEL]
    gates = (p[..., 2 * ML_QK + 2 * D_MODEL:] + gate_b).reshape(B, S, 4, ML_HEADS).transpose(2, 0, 3, 1)
    h_f = mlstm_chunkwise(q, k, v, gates[0], gates[1])
    flip = lambda a: jnp.flip(a, axis=2)
    h_b = flip(mlstm_chunkwise(flip(q), flip(k), flip(v), flip(gates[2]), flip(gates[3])))
    h = h_f + h_b
    mu = jnp.mean(h, axis=-1, keepdims=True)
    var = jnp.mean(jnp.square(h - mu), axis=-1, keepdims=True)
    h = (h - mu) * lax.rsqrt(var + LN_EPS)
    h = h.transpose(0, 2, 1, 3).reshape(B, S, D_MODEL) * norm_g
    out = jax.nn.sigmoid(o.astype(jnp.float32)) * h
    return out.astype(x.dtype) @ w_out

def alibi_slopes():
    return jnp.exp2(-8.0 * jnp.arange(1, N_Q_HEADS + 1, dtype=jnp.float32) / N_Q_HEADS)

def window_attention(x, w_in, sink, w_out):
    B, S, _ = x.shape
    nb = S // BLOCK
    p = x @ w_in
    nq = N_Q_HEADS * HEAD_DIM
    nk = N_KV_HEADS * HEAD_DIM
    q = p[..., :nq].reshape(B, nb, BLOCK, N_KV_HEADS, GROUP, HEAD_DIM)
    k = p[..., nq:nq + nk].reshape(B, S, N_KV_HEADS, HEAD_DIM)
    v = p[..., nq + nk:].reshape(B, S, N_KV_HEADS, HEAD_DIM)
    pad = ((0, 0), (BLOCK, BLOCK), (0, 0), (0, 0))
    kp = jnp.pad(k, pad).reshape(B, nb + 2, BLOCK, N_KV_HEADS, HEAD_DIM)
    vp = jnp.pad(v, pad).reshape(B, nb + 2, BLOCK, N_KV_HEADS, HEAD_DIM)
    kw = jnp.concatenate([kp[:, :-2], kp[:, 1:-1], kp[:, 2:]], axis=2)
    vw = jnp.concatenate([vp[:, :-2], vp[:, 1:-1], vp[:, 2:]], axis=2)
    s = jnp.einsum('bnqkgd,bnskd->bnkgqs', q, kw).astype(jnp.float32) * (HEAD_DIM ** -0.5)
    qi = jnp.arange(BLOCK)[:, None]
    kj = jnp.arange(3 * BLOCK)[None, :]
    rel = qi - kj + BLOCK
    dist = jnp.abs(rel).astype(jnp.float32)
    key_pos = jnp.arange(nb)[:, None] * BLOCK - BLOCK + jnp.arange(3 * BLOCK)[None, :]
    valid = (jnp.abs(rel) <= WINDOW)[None] & ((key_pos >= 0) & (key_pos < S))[:, None, :]
    slopes = alibi_slopes().reshape(N_KV_HEADS, GROUP)
    s = s - slopes[:, :, None, None] * dist
    s = jnp.where(valid[None, :, None, None], s, MASK_VALUE)
    sink_l = sink.astype(jnp.float32).reshape(N_KV_HEADS, GROUP)[None, None, :, :, None, None]
    m = jnp.maximum(jnp.max(s, axis=-1, keepdims=True), sink_l)
    pe = jnp.exp(s - m)
    attn = pe / (jnp.sum(pe, axis=-1, keepdims=True) + jnp.exp(sink_l - m))
    o = jnp.einsum('bnkgqs,bnskd->bnqkgd', attn, vw.astype(jnp.float32)).reshape(B, S, nq)
    return o.astype(x.dtype) @ w_out

def first_inputs(seed: int = 0) -> dict:
    key = jax.random.key(seed)
    ks = jax.random.split(key, 16)
    nrm = jax.random.normal
    x = nrm(ks[0], (BATCH, SEQ, D_MODEL), jnp.float32)
    ffn_w_in = nrm(ks[1], (DEPTH, 2, D_MODEL, 2 * D_FF), jnp.float32) * D_MODEL ** -0.5
    ffn_w_out = nrm(ks[2], (DEPTH, 2, D_FF, D_MODEL), jnp.float32) * (D_FF ** -0.5 * BETA)
    ln_g = 1.0 + 0.02 * nrm(ks[3], (DEPTH, 3, D_MODEL), jnp.float32)
    ln_b = 0.02 * nrm(ks[4], (DEPTH, 3, D_MODEL), jnp.float32)
    ml_w_in = nrm(ks[5], (N_A, D_MODEL, ML_PROJ), jnp.float32) * D_MODEL ** -0.5
    ml_w_in = ml_w_in.at[..., 2 * ML_QK:2 * ML_QK + D_MODEL].multiply(BETA)
    f_off = jnp.linspace(3.0, 6.0, ML_HEADS, dtype=jnp.float32)
    zero = jnp.zeros((ML_HEADS,), jnp.float32)
    gate_off = jnp.stack([zero, f_off, zero, f_off])
    ml_gate_b = (0.1 * nrm(ks[6], (N_A, 4, ML_HEADS), jnp.float32) + gate_off).reshape(N_A, 4 * ML_HEADS)
    ml_norm_g = 1.0 + 0.02 * nrm(ks[7], (N_A, D_MODEL), jnp.float32)
    ml_w_out = nrm(ks[8], (N_A, D_MODEL, D_MODEL), jnp.float32) * (D_MODEL ** -0.5 * BETA)
    at_w_in = nrm(ks[9], (N_B, D_MODEL, AT_PROJ), jnp.float32) * D_MODEL ** -0.5
    at_w_in = at_w_in.at[..., (N_Q_HEADS + N_KV_HEADS) * HEAD_DIM:].multiply(BETA)
    at_sink = 0.5 * nrm(ks[10], (N_B, N_Q_HEADS), jnp.float32)
    at_w_out = nrm(ks[11], (N_B, D_MODEL, D_MODEL), jnp.float32) * (D_MODEL ** -0.5 * BETA)
    return {"x": x, "ffn_w_in": ffn_w_in, "ffn_w_out": ffn_w_out, "ln_g": ln_g, "ln_b": ln_b,
            "ml_w_in": ml_w_in, "ml_gate_b": ml_gate_b, "ml_norm_g": ml_norm_g, "ml_w_out": ml_w_out,
            "at_w_in": at_w_in, "at_sink": at_sink, "at_w_out": at_w_out}

def first_block(x, ffn_w_in, ffn_w_out, ln_g, ln_b, ml_w_in, ml_gate_b, ml_norm_g, ml_w_out,
              at_w_in, at_sink, at_w_out):
    for l in range(DEPTH):
        x = layer_norm(ALPHA * x + 0.5 * swiglu(x, ffn_w_in[l, 0], ffn_w_out[l, 0]), ln_g[l, 0], ln_b[l, 0])
        j = l // N_MIXERS
        if l % N_MIXERS == 0:
            y = mlstm_mixer(x, ml_w_in[j], ml_gate_b[j], ml_norm_g[j], ml_w_out[j])
        else:
            y = window_attention(x, at_w_in[j], at_sink[j], at_w_out[j])
        x = layer_norm(ALPHA * x + y, ln_g[l, 1], ln_b[l, 1])
        x = layer_norm(ALPHA * x + 0.5 * swiglu(x, ffn_w_in[l, 1], ffn_w_out[l, 1]), ln_g[l, 2], ln_b[l, 2])
    return x


HG_HEADS = 4
HG_DIM = 128
HG_WIDTH = HG_HEADS * HG_DIM
HG_CHUNK = 64
NSA_HEADS = 8
NSA_KV_HEADS = 2
NSA_GROUP = NSA_HEADS // NSA_KV_HEADS
NSA_DIM = 64
NSA_WIDTH = NSA_HEADS * NSA_DIM
NSA_KV_WIDTH = NSA_KV_HEADS * NSA_DIM
CMP_LEN = 32
CMP_STRIDE = 16
CMP_HIDDEN = 256
SLC_LEN = 64
SLC_TOP = 16
SLC_QBLOCK = 32
WINDOW_2 = 512
SWA_QBLOCK = 128
N_BRANCH = 3
MIX_WIDTH = HG_WIDTH + NSA_WIDTH
D_FF_2 = ((8 * D_MODEL + 3 * 256 - 1) // (3 * 256)) * 256
ROPE_THETA = 10000.0
RMS_EPS = 1e-6
NEG = -1e30
FORCED_SCORE = 1e9
IN_SPLITS = (HG_WIDTH, HG_WIDTH, HG_WIDTH, HG_WIDTH, NSA_WIDTH,
             NSA_KV_WIDTH, NSA_KV_WIDTH, NSA_KV_WIDTH, NSA_KV_WIDTH, NSA_KV_WIDTH, NSA_KV_WIDTH,
             NSA_HEADS * N_BRANCH)
IN_WIDTH = sum(IN_SPLITS)
IN_SPLIT_POINTS = tuple(int(v) for v in np.cumsum(IN_SPLITS)[:-1])


def rms_norm(x, gain):
    xf = x.astype(jnp.float32)
    y = xf * lax.rsqrt(jnp.mean(xf * xf, axis=-1, keepdims=True) + RMS_EPS)
    return (y * gain.astype(jnp.float32)).astype(x.dtype)

def rope(x, pos):
    half = x.shape[-1] // 2
    freqs = ROPE_THETA ** (-jnp.arange(half, dtype=jnp.float32) / half)
    ang = pos.astype(jnp.float32)[:, None] * freqs[None, :]
    cos = jnp.cos(ang)[:, None, :]
    sin = jnp.sin(ang)[:, None, :]
    xf = x.astype(jnp.float32)
    x1, x2 = xf[..., :half], xf[..., half:]
    return jnp.concatenate([x1 * cos - x2 * sin, x1 * sin + x2 * cos], axis=-1).astype(x.dtype)

def hgrn2_mixer(q, f_logit, i, g, lower_bound, g_norm):
    B, T, _ = q.shape
    dt = q.dtype
    n_chunk = T // HG_CHUNK
    lb = lower_bound.astype(jnp.float32)
    f = lb + (1.0 - lb) * jax.nn.sigmoid(f_logit.astype(jnp.float32))
    log_f = jnp.log(f)
    k = 1.0 - f
    qf = jax.nn.silu(q.astype(jnp.float32))
    v = i.astype(jnp.float32)

    def to_chunks(a):
        return a.reshape(B, n_chunk, HG_CHUNK, HG_HEADS, HG_DIM).transpose(1, 0, 3, 2, 4)

    causal = jnp.tril(jnp.ones((HG_CHUNK, HG_CHUNK), dtype=bool))[:, :, None]

    def step(S, xs):
        qc, kc, vc, lfc = xs
        b = jnp.cumsum(lfc, axis=2)
        diff = b[:, :, :, None, :] - b[:, :, None, :, :]
        decay = jnp.exp(jnp.where(causal, diff, -jnp.inf))
        A = jnp.einsum('bhtd,bhsd,bhtsd->bhts', qc, kc, decay)
        o = (jnp.einsum('bhts,bhsv->bhtv', A, vc)
             + jnp.einsum('bhtd,bhdv->bhtv', qc * jnp.exp(b), S))
        b_last = b[:, :, -1:, :]
        S = (jnp.exp(b_last[:, :, 0, :])[..., None] * S
             + jnp.einsum('bhsd,bhsv->bhdv', kc * jnp.exp(b_last - b), vc))
        return S, o

    S0 = jnp.zeros((B, HG_HEADS, HG_DIM, HG_DIM), jnp.float32)
    _, o = lax.scan(step, S0, (to_chunks(qf), to_chunks(k), to_chunks(v), to_chunks(log_f)))
    o = o.transpose(1, 0, 3, 2, 4).reshape(B, T, HG_HEADS, HG_DIM)
    o = rms_norm(o, g_norm) * jax.nn.silu(g.astype(jnp.float32).reshape(B, T, HG_HEADS, HG_DIM))
    return o.reshape(B, T, HG_WIDTH).astype(dt)

def compress(a, pe, w1, w2):
    B, T, G, d = a.shape
    R = CMP_LEN // CMP_STRIDE
    n_cmp = (T - CMP_LEN) // CMP_STRIDE + 1
    seg = a.reshape(B, T // CMP_STRIDE, CMP_STRIDE, G, d)
    blocks = jnp.concatenate([seg[:, r:r + n_cmp] for r in range(R)], axis=2)
    blocks = blocks + pe[None, None, :, None, :]
    flat = blocks.transpose(0, 1, 3, 2, 4).reshape(B, n_cmp, G, CMP_LEN * d)
    return jax.nn.silu(flat @ w1) @ w2

def cmp_to_slc_matrix(T):
    n_cmp = (T - CMP_LEN) // CMP_STRIDE + 1
    n_slc = T // SLC_LEN
    c_start = np.arange(n_cmp) * CMP_STRIDE
    c_end = c_start + CMP_LEN - 1
    s_start = np.arange(n_slc) * SLC_LEN
    s_end = s_start + SLC_LEN - 1
    M = (c_start[:, None] <= s_end[None, :]) & (c_end[:, None] >= s_start[None, :])
    return jnp.asarray(M.astype(np.float32))

def nsa_mixer(q, k_cmp, v_cmp, k_slc, v_slc, k_swa, v_swa, gate_logit, q_gain, k_gain,
              pe_k, w1_k, w2_k, pe_v, w1_v, w2_v):
    B, T, _ = q.shape
    dt = q.dtype
    H, G, Hg, d = NSA_HEADS, NSA_KV_HEADS, NSA_GROUP, NSA_DIM
    pos = jnp.arange(T)
    scale = d ** -0.5
    qr = rope(rms_norm(q.reshape(B, T, H, d), q_gain), pos)
    qg = qr.reshape(B, T, G, Hg, d)

    def kv_heads(a):
        return a.reshape(B, T, G, d)

    kc = compress(kv_heads(k_cmp), pe_k, w1_k, w2_k)
    vc = compress(kv_heads(v_cmp), pe_v, w1_v, w2_v)
    n_cmp = kc.shape[1]
    cmp_end = jnp.arange(n_cmp) * CMP_STRIDE + CMP_LEN - 1
    kc = rope(rms_norm(kc, k_gain[0]), cmp_end)
    s = jnp.einsum('btghd,bngd->bghtn', qg, kc).astype(jnp.float32) * scale
    m_cmp = cmp_end[None, :] <= pos[:, None]
    p_cmp = jax.nn.softmax(jnp.where(m_cmp, s, NEG), axis=-1) * m_cmp
    o_cmp = jnp.einsum('bghtn,bngd->btghd', p_cmp.astype(dt), vc)

    n_slc = T // SLC_LEN
    imp = jnp.einsum('bghtn,nj->bgtj', p_cmp, cmp_to_slc_matrix(T))
    blk = jnp.arange(n_slc)
    cur = pos // SLC_LEN
    forced = (blk[None, :] == 0) | (blk[None, :] == cur[:, None]) | (blk[None, :] == cur[:, None] - 1)
    causal_blk = blk[None, :] <= cur[:, None]
    score = jnp.where(forced, FORCED_SCORE, jnp.where(causal_blk, imp, NEG))
    top = min(SLC_TOP, n_slc)
    _, idx = lax.top_k(score, top)

    ks = rope(rms_norm(kv_heads(k_slc), k_gain[1]), pos)
    kb = ks.reshape(B, n_slc, SLC_LEN, G, d).transpose(0, 3, 1, 2, 4)
    vb = kv_heads(v_slc).reshape(B, n_slc, SLC_LEN, G, d).transpose(0, 3, 1, 2, 4)
    nq = T // SLC_QBLOCK
    q_blocks = qg.reshape(B, nq, SLC_QBLOCK, G, Hg, d).transpose(1, 0, 3, 4, 2, 5)
    idx_blocks = idx.reshape(B, G, nq, SLC_QBLOCK, top).transpose(2, 0, 1, 3, 4)
    t_blocks = pos.reshape(nq, SLC_QBLOCK)
    bi = jnp.arange(B)[:, None, None, None]
    gi = jnp.arange(G)[None, :, None, None]
    tok = jnp.arange(SLC_LEN)

    def slc_block(xs):
        qb, ib, tb = xs
        kg = kb[bi, gi, ib]
        vg = vb[bi, gi, ib]
        sb = jnp.einsum('bghqd,bgqnsd->bghqns', qb, kg).astype(jnp.float32) * scale
        kpos = ib[..., None] * SLC_LEN + tok
        mb = (kpos <= tb[None, None, :, None, None])[:, :, None]
        sb = jnp.where(mb, sb, NEG)
        pb = jax.nn.softmax(sb.reshape(B, G, Hg, SLC_QBLOCK, -1), axis=-1).reshape(sb.shape)
        return jnp.einsum('bghqns,bgqnsd->bghqd', pb.astype(dt), vg)

    o_slc = lax.map(slc_block, (q_blocks, idx_blocks, t_blocks))
    o_slc = o_slc.transpose(1, 0, 4, 2, 3, 5).reshape(B, T, G, Hg, d)

    kw = rope(rms_norm(kv_heads(k_swa), k_gain[2]), pos)
    vw = kv_heads(v_swa)
    kpad = jnp.pad(kw, ((0, 0), (WINDOW_2, 0), (0, 0), (0, 0)))
    vpad = jnp.pad(vw, ((0, 0), (WINDOW_2, 0), (0, 0), (0, 0)))
    nw = T // SWA_QBLOCK
    span = WINDOW_2 + SWA_QBLOCK
    qw_blocks = qg.reshape(B, nw, SWA_QBLOCK, G, Hg, d).transpose(1, 0, 3, 4, 2, 5)

    def swa_block(xs):
        qb, n = xs
        start = n * SWA_QBLOCK
        kblk = lax.dynamic_slice_in_dim(kpad, start, span, axis=1)
        vblk = lax.dynamic_slice_in_dim(vpad, start, span, axis=1)
        tq = start + jnp.arange(SWA_QBLOCK)
        tk = start - WINDOW_2 + jnp.arange(span)
        mw = (tk[None, :] <= tq[:, None]) & (tk[None, :] > tq[:, None] - WINDOW_2) & (tk[None, :] >= 0)
        sw = jnp.einsum('bghqd,bkgd->bghqk', qb, kblk).astype(jnp.float32) * scale
        pw = jax.nn.softmax(jnp.where(mw, sw, NEG), axis=-1)
        return jnp.einsum('bghqk,bkgd->bghqd', pw.astype(dt), vblk)

    o_swa = lax.map(swa_block, (qw_blocks, jnp.arange(nw)))
    o_swa = o_swa.transpose(1, 0, 4, 2, 3, 5).reshape(B, T, G, Hg, d)

    gate = jax.nn.sigmoid(gate_logit.astype(jnp.float32)).reshape(B, T, G, Hg, N_BRANCH)
    o = (gate[..., 0:1] * o_cmp.astype(jnp.float32)
         + gate[..., 1:2] * o_slc.astype(jnp.float32)
         + gate[..., 2:3] * o_swa.astype(jnp.float32))
    return o.reshape(B, T, NSA_WIDTH).astype(dt)

def second_inputs(seed: int = 0) -> dict:
    key = jax.random.key(seed)
    ks = jax.random.split(key, 20)

    def dense(k, shape, fan_in):
        return jax.random.normal(k, shape, jnp.float32) * fan_in ** -0.5

    def gain(k, shape):
        return 1.0 + 0.05 * jax.random.normal(k, shape, jnp.float32)

    return {
        'x': jax.random.normal(ks[0], (BATCH, SEQ, D_MODEL), jnp.float32),
        'w_in': dense(ks[1], (DEPTH, D_MODEL, IN_WIDTH), D_MODEL),
        'w_out': dense(ks[2], (DEPTH, MIX_WIDTH, D_MODEL), MIX_WIDTH),
        'hg_lb_logits': 0.1 * jax.random.normal(ks[3], (DEPTH, HG_WIDTH), jnp.float32),
        'hg_gnorm': gain(ks[4], (DEPTH, HG_DIM)),
        'q_gain': gain(ks[5], (DEPTH, NSA_DIM)),
        'k_gain': gain(ks[6], (DEPTH, N_BRANCH, NSA_DIM)),
        'cmp_pe_k': 0.1 * jax.random.normal(ks[7], (DEPTH, CMP_LEN, NSA_DIM), jnp.float32),
        'cmp_w1_k': dense(ks[8], (DEPTH, CMP_LEN * NSA_DIM, CMP_HIDDEN), CMP_LEN * NSA_DIM),
        'cmp_w2_k': dense(ks[9], (DEPTH, CMP_HIDDEN, NSA_DIM), CMP_HIDDEN),
        'cmp_pe_v': 0.1 * jax.random.normal(ks[10], (DEPTH, CMP_LEN, NSA_DIM), jnp.float32),
        'cmp_w1_v': dense(ks[11], (DEPTH, CMP_LEN * NSA_DIM, CMP_HIDDEN), CMP_LEN * NSA_DIM),
        'cmp_w2_v': dense(ks[12], (DEPTH, CMP_HIDDEN, NSA_DIM), CMP_HIDDEN),
        'w_ffn_in': dense(ks[13], (DEPTH, D_MODEL, 2 * D_FF_2), D_MODEL),
        'w_ffn_out': dense(ks[14], (DEPTH, D_FF_2, D_MODEL), D_FF_2),
        'norm_mix': gain(ks[15], (DEPTH, D_MODEL)),
        'norm_ffn': gain(ks[16], (DEPTH, D_MODEL)),
    }

def second_block(x, w_in, w_out, hg_lb_logits, hg_gnorm, q_gain, k_gain,
              cmp_pe_k, cmp_w1_k, cmp_w2_k, cmp_pe_v, cmp_w1_v, cmp_w2_v,
              w_ffn_in, w_ffn_out, norm_mix, norm_ffn):
    lb = jnp.cumsum(jax.nn.softmax(hg_lb_logits.astype(jnp.float32), axis=0), axis=0)
    lb = lb - lb[0:1]
    h = x
    for l in range(DEPTH):
        xn = rms_norm(h, norm_mix[l])
        proj = xn @ w_in[l]
        (hq, hf, hi, hg, nq, kc, vc, ksl, vsl, ksw, vsw, ngate) = jnp.split(proj, IN_SPLIT_POINTS, axis=-1)
        o_hg = hgrn2_mixer(hq, hf, hi, hg, lb[l], hg_gnorm[l])
        o_nsa = nsa_mixer(nq, kc, vc, ksl, vsl, ksw, vsw, ngate, q_gain[l], k_gain[l],
                          cmp_pe_k[l], cmp_w1_k[l], cmp_w2_k[l], cmp_pe_v[l], cmp_w1_v[l], cmp_w2_v[l])
        mix = jnp.concatenate([o_hg, o_nsa], axis=-1)
        h = h + mix @ w_out[l]
        xn = rms_norm(h, norm_ffn[l])
        gu = xn @ w_ffn_in[l]
        g_ff, u_ff = gu[..., :D_FF_2], gu[..., D_FF_2:]
        h = h + (jax.nn.silu(g_ff) * u_ff) @ w_ffn_out[l]
    return h


def setup_inputs(seed=0):
    out = dict(first_inputs(seed))
    for name, value in second_inputs(seed + 1).items():
        if name != "x":
            out[name + "_2"] = value
    return out


def reference(
    x, ffn_w_in, ffn_w_out, ln_g, ln_b, ml_w_in, ml_gate_b, ml_norm_g, ml_w_out, at_w_in,
    at_sink, at_w_out, w_in_2, w_out_2, hg_lb_logits_2, hg_gnorm_2, q_gain_2, k_gain_2,
    cmp_pe_k_2, cmp_w1_k_2, cmp_w2_k_2, cmp_pe_v_2, cmp_w1_v_2, cmp_w2_v_2, w_ffn_in_2,
    w_ffn_out_2, norm_mix_2, norm_ffn_2,
):
    x = first_block(
        x, ffn_w_in, ffn_w_out, ln_g, ln_b, ml_w_in, ml_gate_b, ml_norm_g, ml_w_out, at_w_in,
        at_sink, at_w_out,
    )
    return second_block(
        x, w_in_2, w_out_2, hg_lb_logits_2, hg_gnorm_2, q_gain_2, k_gain_2, cmp_pe_k_2,
        cmp_w1_k_2, cmp_w2_k_2, cmp_pe_v_2, cmp_w1_v_2, cmp_w2_v_2, w_ffn_in_2, w_ffn_out_2,
        norm_mix_2, norm_ffn_2,
    )


_drawn_inputs = setup_inputs


def setup_inputs(seed=0):
    import zlib

    import numpy as np

    out = dict(_drawn_inputs(seed))
    spreads = {}
    factors = {'ml_norm_g': 8.0,
     'at_sink': 8.0,
     'hg_lb_logits_2': 8.0,
     'q_gain_2': 7.082,
     'k_gain_2': 7.718,
     'cmp_pe_k_2': 7.852}
    for name, (base, spread) in spreads.items():
        noise = np.random.default_rng([zlib.crc32(name.encode()), seed]).standard_normal(out[name].shape)
        drawn = base * np.exp(spread * noise) if base else spread * noise
        out[name] = __import__('jax').numpy.asarray(drawn.astype(out[name].dtype))
    for name, factor in factors.items():
        out[name] = (out[name] * factor).astype(out[name].dtype)
    return out
```

```python
from contextlib import ExitStack

import numpy as np

import concourse.bass as bass
from concourse import mybir

P = 128
T = 512
D = 1024
KD = D // P
FF = 2816
KF = FF // P
ALPHA = 4 ** 0.25
LN_EPS = 1e-5
RMS_EPS = 1e-6
NEG = -1e30
UT = 8
NRAW = 5
NW = 4
AHEAD = 2

ALU = mybir.AluOpType
ACT = mybir.ActivationFunctionType
AX = mybir.AxisListType.X
F32 = mybir.dt.float32
F32R = mybir.dt.float32r
U32 = mybir.dt.uint32

V_LNG, V_LNB = 0, 48
V_EPS = 96
V_GB = 100
V_MNG = 104
V_SINK = 112
V_LB = 128
V_HGN = 144
V_QG, V_KG = 146, 148
V_NM, V_NF = 156, 172
V_N = 192


def lay_tables():
    p = np.arange(P)[:, None]
    f = np.arange(P)[None, :]
    one = np.ones((P, P), np.float32)
    t = {"ident": (p == f), "mean1024": one / 1024, "mean256": one / 256, "mean128": one / 128,
         "one": one, "mean64": (p // 64 == f // 64) / 64.0,
         "le": np.where(f <= p, 0.0, NEG), "ge": np.where(f >= p, 0.0, NEG)}
    rot = np.zeros((P, P))
    for i in range(P):
        if i % 64 < 32:
            rot[i + 32, i] = -1.0
        else:
            rot[i - 32, i] = 1.0
    t["rot"] = rot
    for h in (16, 8, 4, 2, 1):
        t[f"lv{h}"] = (p // (2 * h) == f // (2 * h)) & (p % (2 * h) < h) & (f % (2 * h) >= h)
    kj = np.arange(3 * P)[None, :]
    rel = p - kj + P
    t["dist"] = np.where(np.abs(rel) <= P, np.abs(rel), 1e30)
    ends = np.arange(31) * 16 + 31
    tok = np.arange(4)[None, :, None] * P + p[:, :, None]
    seen = np.zeros((P, 4, 32), bool)
    seen[:, :, :31] = ends[None, None, :] <= tok
    t["cneg"] = np.where(seen, 0.0, NEG).reshape(P, P)
    t["cone"] = seen.reshape(P, P).astype(np.float32)
    half = 32
    freqs = np.float32(10000.0) ** (-np.arange(half, dtype=np.float32) / np.float32(half))
    ang = np.arange(T, dtype=np.float32)[None, :] * freqs[np.arange(P) % half][:, None]
    t["cos"] = np.cos(ang.astype(np.float32))
    t["sin"] = np.sin(ang.astype(np.float32))
    t["keep"] = np.broadcast_to((np.arange(T) % P != 0)[None, :], (P, T))
    return {k: np.ascontiguousarray(v, np.float32) for k, v in t.items()}


def table_spans():
    at, spans = 0, {}
    for k, v in lay_tables().items():
        spans[k] = (at, v.shape[1])
        at += v.shape[1]
    return spans, at


SPANS, TABLE_N = table_spans()


class Queue:

    def __init__(self, sem):
        self.sem = sem
        self.n = 0
        self.items = []
        self.seen = {}

    def wait(self, waits):
        for w in waits:
            if w is None:
                continue
            if isinstance(w, list):
                self.wait(w)
                continue
            sem, value = w
            if self.seen.get(sem, 0) < value:
                self.seen[sem] = value
                self.items.append(("wait", sem, value))

    def put(self, fn, waits, signal=True):
        self.wait(waits)
        if not signal:
            self.items.append(("do", fn, None))
            return None
        self.n += 1
        self.items.append(("do", fn, self.sem))
        return (self.sem, self.n)

    def play(self, eng, sems):
        for kind, a, b in self.items:
            if kind == "wait":
                eng.wait_ge(sems[a], b)
            else:
                ins = a(eng)
                if b is not None:
                    ins.then_inc(sems[b], 1)


class Vec(Queue):
    def tt(self, out, a, b, op, *w):
        return self.put(lambda e: e.tensor_tensor(out, a, b, op), w)

    def ts(self, out, a, s1, op0, *w, s2=None, op1=None):
        if op1 is None:
            return self.put(lambda e: e.tensor_scalar(out, a, s1, None, op0), w)
        return self.put(lambda e: e.tensor_scalar(out, a, s1, s2, op0, op1), w)

    def stt(self, out, a, s, b, op0, op1, *w):
        return self.put(lambda e: e.scalar_tensor_tensor(out=out, in0=a, scalar=s, in1=b, op0=op0, op1=op1), w)

    def copy(self, out, a, *w):
        return self.put(lambda e: e.tensor_copy(out, a), w)

    def recip(self, out, a, *w):
        return self.put(lambda e: e.reciprocal(out, a), w)

    def scan(self, out, a, b, op0, op1, *w):
        return self.put(lambda e: e.tensor_tensor_scan(out, a, b, 0.0, op0, op1), w)

    def maxneg(self, out, a, *w):
        return self.put(lambda e: e.tensor_reduce(out, a, AX, ALU.max, negate=True), w)

    def pick(self, out, mask, a, *w):
        return self.put(lambda e: e.copy_predicated(out, mask, a), w)

    def fill(self, out, v, *w):
        return self.put(lambda e: e.memset(out, v), w)


class Act(Queue):
    def act(self, out, a, func, *w, scale=1.0, bias=0.0, total=None):
        if total is None:
            return self.put(lambda e: e.activation(out, a, func, bias=bias, scale=scale), w)
        return self.put(lambda e: e.activation(out, a, func, bias=bias, scale=scale, accum_out=total), w)

    def copy(self, out, a, *w):
        return self.put(lambda e: e.activation(out, a, ACT.Copy), w)


class Pe(Queue):
    def mm(self, out, l, r, start, stop, *w, signal=False):
        return self.put(lambda e: e.matmul(out, l, r, start=start, stop=stop), w, signal)

    def turn(self, out, a, ident, *w, signal=False):
        return self.put(lambda e: e.transpose(out, a, ident), w, signal)


class Buf:

    def __init__(self, ap):
        self.ap = ap
        self.free = []


def f32(ap):
    return ap.bitcast(F32)


def interleave(main, side, ratio):
    owed = 0.0
    for _ in main:
        owed += ratio
        while owed >= 1.0:
            owed -= 1.0
            if next(side, "end") == "end":
                owed = -1e9
    for _ in side:
        pass


def run_all(g):
    for _ in g:
        pass


def build(nc, xin, wst, vec, tab, mats_in, out, plan):
    with ExitStack() as ctx:
        def sem(name):
            return ctx.enter_context(nc.semaphore(name))

        def sb(name, shape, dt=F32, scope=ctx):
            return scope.enter_context(nc.sbuf_tensor(name, shape, dt))

        sems = {k: sem("s_" + k) for k in ("pe", "dve", "act", "pool", "ld", "cst", "out")}
        for i in range(NRAW):
            sems[f"raw{i}"] = sem(f"s_raw{i}")
        pe, dve, act, pool = Pe("pe"), Vec("dve"), Act("act"), Vec("pool")
        sp = Queue("sp")

        ps = ctx.enter_context(nc.psum_tensor("ps", [P, 8, 512], F32))
        bank = [Buf(ps[:, i, :]) for i in range(8)]

        raw = [sb(f"raw{i}", [P, UT * P]) for i in range(NRAW)]
        whi = [sb(f"whi{i}", [P, UT * P], F32R) for i in range(NW)]
        wlo = [sb(f"wlo{i}", [P, UT * P], F32R) for i in range(NW)]
        xr = sb("xr", [P, KD, T])
        xh = sb("xh", [P, KD, T], F32R)
        xl = sb("xl", [P, KD, T], F32R)
        vc = sb("vc", [P, V_N])
        res = sb("res", [P, 2 * P])
        tmp = [Buf(sb(f"tmp{i}", [P, T])[:, :]) for i in range(5)]
        ident, mean1024 = res[:, 0:P], res[:, P:2 * P]

        def table(tile, at, name):
            a, n = SPANS[name]
            return load(tile[:, at:at + n], tab[:, a:a + n])

        loads = [0]

        def load(dst, src, *w):
            sp.wait(w)
            loads[0] += 16
            sp.items.append(("dma", lambda e: e.dma_start(dst, src), "ld"))
            sp.items.append(("wait", "ld", loads[0]))
            return ("ld", loads[0])

        n_units = wst.shape[0]
        unit = [0]
        prepared = [0]
        ready = {}
        spent = {}
        rawfree = {}

        def prep(u):
            if u >= n_units:
                return
            r, s = u % NRAW, u % NW
            sp.wait([rawfree.get(u - NRAW)])
            sp.items.append(("dma", lambda e: e.dma_start(raw[r][:, :], wst[u, :, :]), f"raw{r}"))
            landed = (f"raw{r}", 16 * (u // NRAW + 1))
            prepared[0] = u + 1
            return landed

        landed = {}
        fetched = [0]

        def fetch(u):
            while fetched[0] <= u and fetched[0] < n_units:
                landed[fetched[0]] = prep(fetched[0])
                fetched[0] += 1

        split_n = [0]

        def split(u):
            while split_n[0] <= u and split_n[0] < n_units:
                v = split_n[0]
                fetch(v + NRAW - 1)
                r, s = v % NRAW, v % NW
                a = act.copy(whi[s][:, :], raw[r][:, :], landed[v], spent.get(v - NW))
                d = dve.tt(wlo[s][:, :], raw[r][:, :], f32(whi[s][:, :]), ALU.subtract, landed[v], a, spent.get(v - NW))
                ready[v] = [a, d]
                rawfree[v] = d
                split_n[0] += 1

        tile_n = [0]

        def gemm(kt, hi, lo, out, waits, *w, first=True, last=True, n=None):
            tok = None
            for k in range(kt):
                u, j = divmod(tile_n[0], UT)
                need = []
                if j == 0 or k == 0:
                    split(u + AHEAD)
                    need = ready[u]
                s = u % NW
                wh, wl = whi[s][:, j * P:(j + 1) * P], wlo[s][:, j * P:(j + 1) * P]
                a = first and k == 0
                b = last and k == kt - 1
                pe.mm(out, wh, hi(k), a, False, need, waits(k), *(w if k == 0 else ()))
                pe.mm(out, wh, lo(k), False, False)
                tok = pe.mm(out, wl, hi(k), False, b, signal=(j == UT - 1 or k == kt - 1))
                if j == UT - 1:
                    spent[u] = tok
                tile_n[0] += 1
            return tok

        st = {"xr": [None] * KD, "x": [[] for _ in range(KD)], "xused": None}
        rot = [0]

        def next_bank(k=4):
            b = bank[rot[0] % k]
            rot[0] += 1
            return b

        def xk(k):
            return st["x"][k]

        def project(b):
            t = gemm(KD, lambda k: xh[:, k, :], lambda k: xl[:, k, :], b.ap, xk, b.free)
            st["xused"] = t
            return t

        c0 = load(vc[:, :], vec)
        c0 = table(res, 0, "ident")
        c0 = table(res, P, "mean1024")
        xt = load(xr[:, :, :], xin.rearrange("(k p) t -> p k t", p=P))
        for k in range(KD):
            a = act.copy(xh[:, k, :], xr[:, k, :], xt)
            d = dve.tt(xl[:, k, :], xr[:, k, :], f32(xh[:, k, :]), ALU.subtract, a)
            st["x"][k] = [a, d]
            st["xr"][k] = d
        dve.wait([c0])
        act.wait([c0])
        pe.wait([c0])

        def prescale():
            for k in range(KD):
                st["xr"][k] = pool.ts(xr[:, k, :], xr[:, k, :], ALPHA, ALU.mult, st["xr"][k], s2=1.0, op1=ALU.mult)

        class Norm:

            def __init__(self, square):
                self.square = square
                self.acc = tmp[4]
                self.tok = None

            def add(self, k, t):
                z = xr[:, k, :]
                if self.square:
                    if k == 0:
                        self.tok = act.act(self.acc.ap, z, ACT.Square, t, self.acc.free)
                    else:
                        s = tmp[k % 2]
                        a = act.act(s.ap, z, ACT.Square, t, s.free)
                        self.tok = pool.tt(self.acc.ap, self.acc.ap, s.ap, ALU.add, a, self.tok)
                        s.free = [self.tok]
                elif k == 0:
                    self.tok = pool.put(lambda e: e.tensor_copy(self.acc.ap, z), [t, self.acc.free])
                else:
                    self.tok = pool.tt(self.acc.ap, self.acc.ap, z, ALU.add, t, self.tok)

        def layer_norm(nm, l, scale_next):
            b = next_bank()
            m = pe.mm(b.ap, mean1024, nm.acc.ap, True, True, nm.tok, b.free, signal=True)
            nm.acc.free = [m]
            b2 = next_bank()
            t = None
            dt = []
            for k in range(KD):
                d = dve.tt(xr[:, k, :], xr[:, k, :], b.ap, ALU.subtract, m, st["xr"][k])
                dt.append(d)
                s = tmp[k % 2]
                a = act.act(s.ap, xr[:, k, :], ACT.Square, d, s.free)
                t = pe.mm(b2.ap, mean1024, s.ap, k == 0, k == KD - 1, a, b2.free if k == 0 else None, signal=True)
                s.free = [t]
            b.free = [dt[-1]]
            sd, rc = tmp[2], tmp[3]
            a = act.act(sd.ap, b2.ap, ACT.Sqrt, t, sd.free, bias=vc[:, V_EPS:V_EPS + 1])
            b2.free = [a]
            r = dve.recip(rc.ap, sd.ap, a, rc.free)
            sd.free = [r]
            for k in range(KD):
                g, o = vc[:, V_LNG + 8 * l + k:V_LNG + 8 * l + k + 1], vc[:, V_LNB + 8 * l + k:V_LNB + 8 * l + k + 1]
                n = dve.tt(xr[:, k, :], xr[:, k, :], rc.ap, ALU.mult, r)
                a = act.act(xh[:, k, :], xr[:, k, :], ACT.Identity, n, st["xused"], scale=g, bias=o)
                y = dve.ts(xr[:, k, :], xr[:, k, :], g, ALU.mult, a, n, s2=o, op1=ALU.add)
                d = dve.tt(xl[:, k, :], xr[:, k, :], f32(xh[:, k, :]), ALU.subtract, y, st["xused"])
                st["x"][k] = [a, d]
                st["xr"][k] = d
            rc.free = [d]
            if scale_next:
                prescale()

        def rms_norm(nm, col):
            b = next_bank()
            m = pe.mm(b.ap, mean1024, nm.acc.ap, True, True, nm.tok, b.free, signal=True)
            nm.acc.free = [m]
            sd, rc = tmp[2], tmp[3]
            a = act.act(sd.ap, b.ap, ACT.Sqrt, m, sd.free, bias=vc[:, V_EPS + 1:V_EPS + 2])
            b.free = [a]
            r = dve.recip(rc.ap, sd.ap, a, rc.free)
            sd.free = [r]
            for k in range(KD):
                g = vc[:, col + k:col + k + 1]
                s = tmp[k % 2]
                n = dve.tt(s.ap, xr[:, k, :], rc.ap, ALU.mult, r, st["xr"][k], s.free)
                a = act.act(xh[:, k, :], s.ap, ACT.Copy, n, st["xused"], scale=g)
                d = dve.stt(xl[:, k, :], s.ap, g, f32(xh[:, k, :]), ALU.mult, ALU.subtract, a, n, st["xused"])
                s.free = [d]
                st["x"][k] = [a, d]
            rc.free = [d]

        def residual(k, b, t, by, nm):
            d = dve.stt(xr[:, k, :], b.ap, by, xr[:, k, :], ALU.mult, ALU.add, t, st["xr"][k])
            b.free = [d]
            st["xr"][k] = d
            if nm is not None:
                nm.add(k, d)

        mem_free = []

        def ffn(by, nm):
            scope = ExitStack()
            hh = sb(f"hh{unit[0]}", [P, KF, T], F32R, scope)
            hl = sb(f"hl{unit[0]}", [P, KF, T], F32R, scope)
            unit[0] += 1
            free = list(mem_free)
            hready = []
            for j in range(KF):
                bg, bu = next_bank(), next_bank()
                tg = project(bg)
                tu = project(bu)
                s, h = tmp[j % 2], tmp[2 + j % 2]
                a = act.act(s.ap, bg.ap, ACT.Silu, tg, s.free)
                d = dve.tt(h.ap, s.ap, bu.ap, ALU.mult, a, tu, h.free)
                bg.free, bu.free, s.free = [a], [d], [d]
                a = act.copy(hh[:, j, :], h.ap, d, free)
                d = dve.tt(hl[:, j, :], h.ap, f32(hh[:, j, :]), ALU.subtract, a, free)
                h.free = [d]
                hready.append([a, d])
            for f in range(KD):
                b = next_bank()
                t = gemm(KF, lambda k: hh[:, k, :], lambda k: hl[:, k, :], b.ap, lambda k: hready[k], b.free)
                residual(f, b, t, by, nm)
            mem_free[:] = [t]
            scope.close()

        def out_proj(nm):
            for f in range(KD):
                b = next_bank()
                t = project(b)
                residual(f, b, t, 1.0, nm)

        def to_tokens(dst, src, b, *w):
            for i in range(4):
                t = pe.turn(b.ap[:, i * P:(i + 1) * P], src[:, i * P:(i + 1) * P], ident, *(list(w) + b.free if i == 0 else []), signal=(i == 3))
            c = dve.copy(dst, b.ap.rearrange("p (i f) -> p i f", i=4), t)
            b.free = [c]
            return t, c

        def fence():
            last = [(q.sem, q.n) for q in (pe, act, dve, pool) if q.n]
            for q in (pe, act, dve, pool, sp):
                q.wait(last)
            return last

        def col(c, n=1, rows=slice(0, P)):
            return vc[rows, c:c + n]

        def over(ap, n):
            return ap[:, None, :].broadcast_to([ap.shape[0], n, ap.shape[1]])

        def along(ap, n):
            return ap[:, :, None].broadcast_to([ap.shape[0], ap.shape[1], n])

        def store_parts(k, src, *w):
            a = act.copy(xh[:, k, :], src, *w)
            d = dve.tt(xl[:, k, :], src, f32(xh[:, k, :]), ALU.subtract, a, *w)
            st["x"][k] = [a, d]
            return d

        def mlstm():
            fence()
            scope = ExitStack()
            q = sb("mq", [P, 4, T], F32, scope)
            kk = sb("mk", [P, 4, T], F32, scope)
            vt = sb("mv", [P, 4, D], F32, scope)
            og = sb("mo", [P, 8, T], F32, scope)
            hs = sb("mh", [P, 8, T], F32, scope)
            tb = sb("mtb", [P, 4 * P], F32, scope)
            le, ge, one, mean256 = (tb[:, i * P:(i + 1) * P] for i in range(4))
            for i, n in enumerate(("le", "ge", "one", "mean256")):
                ct = table(tb, i * P, n)
            rows = [sb(f"mr{i}", [64, T], F32, scope) for i in range(3)]
            nM, nm, fx = (r[:, :] for r in rows)
            at = sb("mat", [P, 4 * 64], F32, scope)
            nb = [Buf(sb(f"mn{i}", [P, T], F32, scope)[:, :]) for i in range(2)]
            nkb = [Buf(sb(f"mnk{i}", [P, T], F32, scope)[:, :]) for i in range(2)]
            eb = [Buf(sb(f"me{i}", [P, T], F32, scope)[:, :]) for i in range(2)]
            wt = [Buf(sb(f"mw{i}", [P, T], F32, scope)[:, :]) for i in range(2)]
            pt = [Buf(sb(f"mp{i}", [P, T], F32, scope)[:, :]) for i in range(2)]

            b = next_bank()
            t = project(b)
            g, f, e1, e2 = tmp[0].ap, tmp[1].ap, tmp[2].ap, tmp[3].ap
            a = act.act(g, b.ap, ACT.Identity, t, [x.free for x in tmp], bias=col(V_GB))
            b.free = [a]
            d = dve.copy(f[0:64, :], g[64:128, :], a)
            a = act.act(e1[0:64, :], f[0:64, :], ACT.Abs, d)
            a = act.act(e2[0:64, :], e1[0:64, :], ACT.Exp, a, scale=-1.0)
            d = dve.ts(e2[0:64, :], e2[0:64, :], 1.0, ALU.add, a)
            a = act.act(e1[0:64, :], e2[0:64, :], ACT.Ln, d)
            d = dve.stt(f[0:64, :], f[0:64, :], 0.0, e1[0:64, :], ALU.min, ALU.subtract, a)
            d1 = dve.fill(e2[0:64, :], 1.0)
            dve.scan(e1[0:32, :], e2[0:32, :], f[0:32, :], ALU.mult, ALU.add, d, d1)
            d = dve.scan(e1[32:64, ::-1], e2[32:64, :], f[32:64, ::-1], ALU.mult, ALU.add)
            d = dve.tt(fx, g[0:64, :], e1[0:64, :], ALU.subtract, d)
            dve.scan(f[0:32, :], fx[0:32, :], fx[0:32, :], ALU.max, ALU.max, d)
            d = dve.scan(f[32:64, ::-1], fx[32:64, ::-1], fx[32:64, ::-1], ALU.max, ALU.max)
            d = dve.ts(nM, f[0:64, :], -1.0, ALU.mult, d, s2=1.0, op1=ALU.mult)
            rows_ok = dve.tt(nm, nM, e1[0:64, :], ALU.subtract, d)
            for x in tmp:
                x.free = [rows_ok]
            b = next_bank()
            for i in range(4):
                t = pe.turn(b.ap[:, i * 64:(i + 1) * 64], fx[:, i * P:(i + 1) * P], ident[0:64, 0:64], rows_ok, b.free, signal=True)
            at_ok = act.copy(at[:, :], b.ap[:, 0:256], t)
            b.free = [at_ok]

            for h in range(4):
                b = next_bank()
                t = project(b)
                b.free = [act.copy(q[:, h, :], b.ap, t)]
            for h in range(4):
                b = next_bank()
                t = project(b)
                b.free = [act.act(kk[:, h, :], b.ap, ACT.Copy, t, scale=P ** -0.5)]
            for c in range(8):
                b = next_bank()
                t = project(b)
                s = tmp[c % 2]
                a = act.copy(s.ap, b.ap, t, s.free)
                b.free = [a]
                t, d = to_tokens(vt[:, :, c * P:(c + 1) * P], s.ap, bank[4 + c % 2], a)
                s.free = [t]
            for c in range(8):
                b = next_bank()
                t = project(b)
                a = act.act(og[:, c, :], b.ap, ACT.Sigmoid, t)
                b.free = [a]
            qkv = [a, d, ct]
            pe.wait(qkv)
            dve.wait([ct])

            units = [(h, r) for h in range(4) for r in range(2)]
            order = [range(4), range(3, -1, -1)]
            span = [lambda s: (s * P, T), lambda s: (0, (s + 1) * P)]
            stage = {}

            def first(n):
                h, r = units[n]
                b = bank[7]
                one_row = ident[0:64, 32 * r + h:32 * r + h + 1].broadcast_to([64, P])
                t = pe.mm(b.ap, one_row, nM, True, True, b.free, signal=True)
                m, nk = nb[n % 2], nkb[n % 2]
                a = act.copy(m.ap, b.ap, t, m.free)
                b.free = [a]
                t = pe.mm(b.ap, one_row, nm, True, True, b.free, signal=True)
                e = eb[n % 2]
                a2 = act.act(e.ap, b.ap, ACT.Exp, t, e.free)
                b.free = [a2]
                blocks = lambda x: x.rearrange("p (i f) -> p i f", i=4)
                d = dve.tt(blocks(nk.ap), blocks(m.ap), over(ge if r == 0 else le, 4), ALU.add, a, nk.free)
                if r == 0:
                    for s in range(4):
                        t = pe.mm(bank[s].ap, kk[:, h, s * P:(s + 1) * P], q[:, h, :], True, True, bank[s].free, signal=True)
                        stage["s", h, s] = t
                stage[n] = (a, a2, d)

            def second(n):
                h, r = units[n]
                a, a2, d = stage[n]
                m, e, nk = nb[n % 2], eb[n % 2], nkb[n % 2]
                acc = [bank[4], bank[5], bank[6]]
                for i, s in enumerate(order[r]):
                    lo, hi = span[r](s)
                    w, p = wt[i % 2], pt[i % 2]
                    bias = at[:, s * 64 + 32 * r + h:s * 64 + 32 * r + h + 1]
                    x = act.act(w.ap[:, s * P:(s + 1) * P], nk.ap[:, s * P:(s + 1) * P], ACT.Exp, d, at_ok, w.free, bias=bias)
                    olo, ohi = ((s + 1) * P, T) if r == 0 else (0, s * P)
                    if ohi > olo:
                        x = act.act(w.ap[:, olo:ohi], m.ap[:, olo:ohi], ACT.Exp, bias=bias)
                    y = dve.tt(p.ap[:, lo:hi], bank[s].ap[:, lo:hi], w.ap[:, lo:hi], ALU.mult, x, stage["s", h, s], p.free)
                    w.free = [y]
                    if r == 1:
                        bank[s].free = [y]
                    for c in range(3):
                        l = one if c == 2 else vt[:, s, (2 * h + c) * P:(2 * h + c + 1) * P]
                        t = pe.mm(acc[c].ap[:, lo:hi], l, p.ap[:, lo:hi], i == 0, i == 3, y, acc[c].free if i == 0 else None, signal=(c == 2))
                    p.free = [t]
                nk.free = m.free = [x]
                s0, s1 = tmp[2], tmp[3]
                x = act.act(s0.ap, acc[2].ap, ACT.Abs, t, s0.free)
                acc[2].free = [x]
                y = dve.tt(s1.ap, s0.ap, e.ap, ALU.max, x, a2, s1.free)
                e.free = [y]
                s0.free = [y]
                y = dve.recip(s1.ap, s1.ap, y)
                for c in range(2):
                    o = hs[:, 2 * h + c, :]
                    if r == 0:
                        y2 = dve.tt(o, acc[c].ap, s1.ap, ALU.mult, y)
                        acc[c].free = [y2]
                    else:
                        s = tmp[c]
                        y2 = dve.tt(s.ap, acc[c].ap, s1.ap, ALU.mult, y, s.free)
                        acc[c].free = [y2]
                        g = pool.tt(o, o, s.ap, ALU.add, y2)
                        s.free = [g]
                        stage["h", 2 * h + c] = g
                s1.free = [y2]

            first(0)
            for n in range(8):
                if n + 1 < 8:
                    first(n + 1) if units[n + 1][1] == 1 else None
                second(n)
                if n + 1 < 8 and units[n + 1][1] == 0:
                    first(n + 1)

            for h in range(4):
                b, b2 = bank[h % 2], bank[2 + h % 2]
                w = [stage["h", 2 * h], stage["h", 2 * h + 1]]
                pe.mm(b.ap, mean256, hs[:, 2 * h, :], True, False, w, b.free)
                t = pe.mm(b.ap, mean256, hs[:, 2 * h + 1, :], False, True, signal=True)
                for c in range(2):
                    d = dve.tt(hs[:, 2 * h + c, :], hs[:, 2 * h + c, :], b.ap, ALU.subtract, t)
                    s = tmp[c]
                    a = act.act(s.ap, hs[:, 2 * h + c, :], ACT.Square, d, s.free)
                    t2 = pe.mm(b2.ap, mean256, s.ap, c == 0, c == 1, a, b2.free if c == 0 else None, signal=True)
                    s.free = [t2]
                b.free = [d]
                sd, rc = tmp[2], tmp[3]
                a = act.act(sd.ap, b2.ap, ACT.Sqrt, t2, sd.free, bias=col(V_EPS))
                b2.free = [a]
                r = dve.recip(rc.ap, sd.ap, a, rc.free)
                sd.free = [r]
                for c in range(2):
                    k = 2 * h + c
                    n = dve.tt(hs[:, k, :], hs[:, k, :], rc.ap, ALU.mult, r)
                    n = dve.stt(hs[:, k, :], hs[:, k, :], col(V_MNG + k), og[:, k, :], ALU.mult, ALU.mult, n)
                    d = store_parts(k, hs[:, k, :], n, st["xused"])
                rc.free = [d]
            scope.close()
            mem_free[:] = [d, st["x"][7]]

        def window():
            fence()
            scope = ExitStack()
            q = sb("wq", [P, 8, T], F32, scope)
            kk = sb("wk", [P, 2, T], F32, scope)
            vt = sb("wv", [P, 4, 2 * P], F32, scope)
            dist = sb("wd", [P, 3 * P], F32, scope)
            ct = table(dist, 0, "dist")
            sx = [Buf(sb(f"ws{i}", [P, 2, 3 * P], F32, scope)) for i in range(2)]
            pp = [Buf(sb(f"wp{i}", [P, 2, 3 * P], F32, scope)) for i in range(2)]
            pt = [Buf(sb(f"wt{i}", [P, 2, 3 * P], F32, scope)) for i in range(2)]
            nsink = sb("wns", [P, 16], F32, scope)
            small = [Buf(sb(f"wm{i}", [P, 16], F32, scope)) for i in range(2)]
            ns = dve.ts(nsink[:, :], col(V_SINK, 16), -1.0, ALU.mult, s2=1.0, op1=ALU.mult)
            for c in range(2):
                b = next_bank()
                t = project(b)
                b.free = [act.copy(kk[:, c, :], b.ap, t)]
            for c in range(2):
                b = next_bank()
                t = project(b)
                s = tmp[c % 2]
                a = act.copy(s.ap, b.ap, t, s.free)
                b.free = [a]
                t, d = to_tokens(vt[:, :, c * P:(c + 1) * P], s.ap, bank[4 + c % 2], a)
                s.free = [t]
            for c in range(8):
                b = next_bank()
                t = project(b)
                a = act.act(q[:, c, :], b.ap, ACT.Copy, t, scale=0.125)
                b.free = [a]
            pe.wait([a, d])
            dve.wait([ct, ns])
            units = [(t, i) for t in range(8) for i in range(4)]
            stage = {}

            def first(n):
                t, i = units[n]
                j0, j1 = max(0, i - 1), min(3, i + 1)
                for g in range(2):
                    b = bank[2 * (n % 2) + g]
                    x = pe.mm(b.ap[:, 0:(j1 - j0 + 1) * P], q[64 * g:64 * g + 64, t, i * P:(i + 1) * P],
                              kk[64 * g:64 * g + 64, t // 4, j0 * P:(j1 + 1) * P], True, True, b.free, signal=True)
                stage[n] = x

            def second(n):
                t, i = units[n]
                j0, j1 = max(0, i - 1), min(3, i + 1)
                w = (j1 - j0 + 1) * P
                at = (j0 - i + 1) * P
                s, p, m = sx[n % 2], pp[n % 2], small[n % 2]
                for g in range(2):
                    slope = float(np.float32(2.0 ** (-8.0 * (WIN_ORDER[2 * t + g] + 1) / 16)))
                    b = bank[2 * (n % 2) + g]
                    d = dve.stt(s.ap[:, g, 0:w], dist[:, at:at + w], -slope, b.ap[:, 0:w], ALU.mult, ALU.add, stage[n], s.free)
                    b.free = [d]
                nm, sums, es = m.ap[:, 0:2], m.ap[:, 2:4], m.ap[:, 4:6]
                d = dve.maxneg(nm, s.ap[:, :, 0:w], d, m.free)
                d = dve.tt(nm, nm, nsink[:, 2 * t:2 * t + 2], ALU.min, d)
                d2 = dve.tt(es, nm, col(V_SINK + 2 * t, 2), ALU.add, d)
                for g in range(2):
                    a = act.act(p.ap[:, g, 0:w], s.ap[:, g, 0:w], ACT.Exp, d, p.free, bias=nm[:, g:g + 1], total=sums[:, g:g + 1])
                s.free = [a]
                a = act.act(es, es, ACT.Exp, d2)
                d = dve.tt(sums, sums, es, ALU.add, a)
                d = dve.recip(sums, sums, d)
                for g in range(2):
                    d2 = dve.ts(p.ap[:, g, 0:w], p.ap[:, g, 0:w], sums[:, g:g + 1], ALU.mult, d, s2=1.0, op1=ALU.mult)
                m.free = [d2]
                stage[n] = d2

            def third(n):
                t, i = units[n]
                nk = min(3, i + 1) - max(0, i - 1) + 1
                p, y = pp[n % 2], pt[n % 2]
                for g in range(2):
                    b = bank[4 + g]
                    for j in range(nk):
                        x = pe.turn(b.ap[:, j * P:(j + 1) * P], p.ap[:, g, j * P:(j + 1) * P], ident, stage[n], b.free, signal=(j == nk - 1))
                    if g:
                        z = dve.copy(y.ap[:, g, 0:nk * P], b.ap[:, 0:nk * P], x, y.free)
                    else:
                        z = act.copy(y.ap[:, g, 0:nk * P], b.ap[:, 0:nk * P], x, y.free)
                    b.free = [z]
                    stage[n, g] = z
                p.free = [x]

            def fourth(n):
                t, i = units[n]
                j0, j1 = max(0, i - 1), min(3, i + 1)
                b, y = bank[6 + t % 2], pt[n % 2]
                for g in range(2):
                    for j in range(j0, j1 + 1):
                        at = (t // 4) * P + 64 * g
                        x = pe.mm(b.ap[64 * g:64 * g + 64, i * P:(i + 1) * P], vt[:, j, at:at + 64],
                                  y.ap[:, g, (j - j0) * P:(j - j0 + 1) * P], j == j0, j == j1, stage[n, g],
                                  b.free, signal=(g == 1 and j == j1))
                y.free = [x]
                if i == 3:
                    b.free = [store_parts(t, b.ap, x, st["xused"])]
                    b.free += st["x"][t]

            for n in range(len(units) + 3):
                if n < len(units):
                    first(n)
                    second(n)
                if 0 <= n - 1 < len(units):
                    third(n - 1)
                if 0 <= n - 2 < len(units):
                    fourth(n - 2)
            scope.close()
            mem_free[:] = b.free

        def hgrn(l, hres, scope):
            q = sb(f"hq{l}", [P, 4, T], F32, scope)
            kk = sb(f"hk{l}", [P, 4, T], F32, scope)
            bb = sb(f"hb{l}", [P, 4, T], F32, scope)
            vt = sb(f"hv{l}", [P, 4, T], F32, scope)
            tb = sb(f"htb{l}", [P, 6 * P], F32, scope)
            keep = sb(f"hkeep{l}", [P, T], F32, scope)
            lbs = sb(f"hlb{l}", [P, 40], F32, scope)
            dd = [Buf(sb(f"hd{l}{i}", [P, T], F32, scope)[:, :]) for i in range(2)]
            ee = [Buf(sb(f"he{l}{i}", [P, T], F32, scope)[:, :]) for i in range(2)]
            qe = [Buf(sb(f"hqe{l}{i}", [P, T], F32, scope)[:, :]) for i in range(2)]
            ke = [Buf(sb(f"hke{l}{i}", [P, T], F32, scope)[:, :]) for i in range(2)]
            ad = [Buf(sb(f"had{l}{i}", [P, T], F32, scope)[:, :]) for i in range(2)]
            ao = [Buf(sb(f"hao{l}{i}", [P, 6 * P], F32, scope)[:, :]) for i in range(2)]
            for i, n in enumerate(("lv16", "lv8", "lv4", "lv2", "lv1", "mean128")):
                ct = table(tb, i * P, n)
            ct = table(keep, 0, "keep")
            mask = {h: tb[:, i * P:(i + 1) * P].bitcast(U32) for i, h in enumerate((16, 8, 4, 2, 1))}
            mask[0] = ident.bitcast(U32)
            mean128 = tb[:, 5 * P:6 * P]

            l0, l1 = col(V_LB, 4), col(V_LB + 4, 4)
            c = [lbs[:, 4 * i:4 * i + 4] for i in range(10)]
            d = dve.tt(c[0], l0, l1, ALU.max)
            d = dve.tt(c[1], l0, c[0], ALU.subtract, d)
            d = dve.tt(c[2], l1, c[0], ALU.subtract, d)
            a = act.act(lbs[:, 4:12], lbs[:, 4:12], ACT.Exp, d)
            d = dve.tt(c[3], c[1], c[2], ALU.add, a)
            d = dve.recip(c[3], c[3], d)
            d = dve.tt(c[4], c[1], c[3], ALU.mult, d)
            d = dve.tt(c[5], c[2], c[3], ALU.mult, d)
            d = dve.tt(c[5], c[4], c[5], ALU.add, d)
            d = dve.tt(c[6], c[4 + l], c[4], ALU.subtract, d)
            lb_ok = dve.ts(c[7], c[6], -1.0, ALU.mult, d, s2=1.0, op1=ALU.add)
            for i in range(2):
                z = dve.fill(ad[i].ap, 0.0)

            done = {}
            for h in range(4):
                b = next_bank()
                t = project(b)
                b.free = [act.act(q[:, h, :], b.ap, ACT.Silu, t)]
                yield
            for h in range(4):
                b = next_bank()
                t = project(b)
                s = tmp[h % 2]
                a = act.act(s.ap, b.ap, ACT.Sigmoid, t, s.free)
                b.free = [a]
                f = dve.ts(bb[:, h, :], s.ap, c[7][:, h:h + 1], ALU.mult, a, lb_ok, s2=c[6][:, h:h + 1], op1=ALU.add)
                s.free = [f]
                done["k", h] = dve.ts(kk[:, h, :], bb[:, h, :], -1.0, ALU.mult, f, s2=1.0, op1=ALU.add)
                yield
            dve.wait([ct])
            for h in range(4):
                a = act.act(bb[:, h, :], bb[:, h, :], ACT.Ln, done["k", h])
                done["b", h] = dve.scan(bb[:, h, :], keep[:, :], bb[:, h, :], ALU.mult, ALU.add, a)
            for h in range(4):
                b = next_bank()
                t = project(b)
                s = tmp[h % 2]
                a = act.copy(s.ap, b.ap, t, s.free)
                b.free = [a]
                t, done["v"] = to_tokens(vt[:, :, h * P:(h + 1) * P], s.ap, bank[4 + h % 2], a)
                s.free = [t]
                yield
            for h in range(4):
                b = next_bank()
                t = project(b)
                done["g", h] = act.act(hres[:, h, :], b.ap, ACT.Silu, t)
                b.free = [done["g", h]]
                yield
            pe.wait([done["g", 3], done["k", 3], done["v"], ct])
            n = 0
            for h in range(4):
                pd, po, y = ad[h % 2], ao[h % 2], None
                bh = bb[:, h, :]
                dve.wait([done["b", h]])
                act.wait([done["b", h]])
                for half in (64, 32, 16, 8, 4, 2, 1, 0):
                    x, e, qq, ek = dd[n % 2], ee[n % 2], qe[n % 2], ke[n % 2]
                    pb = bank[4 + n % 2]
                    n += 1
                    if half:
                        v = lambda y: y.rearrange("p (i f) -> p i f", f=2 * half)
                        ref = along(v(bh)[:, :, half - 1], 2 * half)
                        d = dve.tt(v(x.ap), v(bh), ref, ALU.subtract, x.free)
                        act.act(v(e.ap)[:, :, 0:half], v(x.ap)[:, :, 0:half], ACT.Exp, d, e.free, scale=-1.0)
                        a = act.act(v(e.ap)[:, :, half:], v(x.ap)[:, :, half:], ACT.Exp)
                        x.free = [a]
                        d1 = dve.tt(qq.ap, q[:, h, :], e.ap, ALU.mult, a, qq.free)
                        d2 = pool.tt(ek.ap, kk[:, h, :], e.ap, ALU.mult, a, ek.free)
                        e.free = [d1, d2]
                        kx, qx = ek.ap, qq.ap
                        w = [d1, d2]
                    else:
                        kx, qx, w = kk[:, h, :], q[:, h, :], []
                    step = half if half >= 32 else P
                    if half >= 32:
                        for i in range(T // (2 * half)):
                            lo = 2 * half * i
                            r = lo % P
                            t = pe.mm(pb.ap[r:r + half, lo + half:lo + 2 * half], kx[:, lo:lo + half], qx[:, lo + half:lo + 2 * half],
                                      True, True, w, pb.free, signal=True)
                        for r in range(0, P, 2 * half):
                            src = pb.ap.rearrange("p (i f) -> p i f", f=P)[r:r + half, :, r + half:r + 2 * half]
                            dst = pd.ap.rearrange("p (i f) -> p i f", f=P)[r:r + half, :, r + half:r + 2 * half]
                            y = dve.copy(dst, src, t, pd.free, z, y)
                    else:
                        for i in range(4):
                            t = pe.mm(pb.ap[:, i * P:(i + 1) * P], kx[:, i * P:(i + 1) * P], qx[:, i * P:(i + 1) * P],
                                      True, True, w, pb.free, signal=(i == 3))
                        v4 = lambda y: y.rearrange("p (i f) -> p i f", f=P)
                        y = dve.pick(v4(pd.ap), over(mask[half], 4), v4(pb.ap), t, pd.free, z, y)
                    pb.free = [y]
                    if half:
                        qq.free = ek.free = [t]
                    yield
                diag_ok = y
                x, e, qq, ek = dd[n % 2], ee[n % 2], qe[n % 2], ke[n % 2]
                x2 = dd[(n + 1) % 2]
                n += 1
                ends = v4(bh)[:, 0:3, P - 1]
                d = dve.tt(v4(x.ap)[:, 0:3, :], along(ends, P), v4(bh)[:, 0:3, :], ALU.subtract, x.free)
                act.act(e.ap[:, 0:384], x.ap[:, 0:384], ACT.Exp, d, e.free)
                a = act.act(x2.ap[:, 0:384], bh[:, P:T], ACT.Exp, x2.free)
                a2 = act.act(lbs[:, 32:35], ends, ACT.Exp, done.get("lbs"))
                d1 = dve.tt(ek.ap[:, 0:384], kk[:, h, 0:384], e.ap[:, 0:384], ALU.mult, a, ek.free)
                d2 = dve.tt(qq.ap[:, 0:384], q[:, h, P:T], x2.ap[:, 0:384], ALU.mult, a, qq.free)
                d3 = dve.ts(ek.ap[:, 384:T], ek.ap[:, 0:P], lbs[:, 33:34], ALU.mult, d1, a2, s2=1.0, op1=ALU.mult)
                d4 = dve.ts(qq.ap[:, 384:T], qq.ap[:, 256:384], lbs[:, 34:35], ALU.mult, d2, s2=1.0, op1=ALU.mult)
                e.free = x.free = x2.free = [d4, a]
                done["lbs"] = d4
                b0, b1 = bank[6], bank[7]
                K = lambda i: ek.ap[:, i * P:(i + 1) * P]
                Q = lambda i: qq.ap[:, i * P:(i + 1) * P]
                pairs = [(0, 0, K(0), Q(0)), (0, 1, K(3), Q(1)), (0, 2, K(3), Q(3)), (1, 0, K(1), Q(1)), (1, 1, K(1), Q(3)), (1, 2, K(2), Q(2))]
                for bi, at, kx, qx in pairs:
                    o = (b0, b1)[bi]
                    t = pe.mm(o.ap[:, at * P:(at + 1) * P], kx, qx, True, True, d3, d4, o.free, signal=True)
                qq.free = ek.free = [t]
                y1 = act.copy(po.ap[:, 0:384], b0.ap[:, 0:384], t, po.free)
                y2 = act.copy(po.ap[:, 384:768], b1.ap[:, 0:384], t)
                b0.free, b1.free = [y1], [y2]
                yield
                ob = bank[6]
                off = {0: (0, 384), 1: (384, 640), 2: (640, 768)}
                for j in range(4):
                    v = vt[:, j, h * P:(h + 1) * P]
                    t = pe.mm(ob.ap[:, j * P:(j + 1) * P], v, pd.ap[:, j * P:(j + 1) * P], j == 0, j == 3, diag_ok, y2, ob.free if j == 0 else None, signal=True)
                    if j < 3:
                        t = pe.mm(ob.ap[:, (j + 1) * P:T], v, po.ap[:, off[j][0]:off[j][1]], False, False, signal=True)
                pd.free = po.free = [t]
                s, r = tmp[2], tmp[3]
                mb = bank[7]
                a = act.act(s.ap, ob.ap, ACT.Square, t, s.free)
                t2 = pe.mm(mb.ap, mean128, s.ap, True, True, a, mb.free, signal=True)
                a = act.act(r.ap, mb.ap, ACT.Sqrt, t2, r.free, bias=col(V_EPS + 1))
                mb.free = [a]
                d = dve.recip(r.ap, r.ap, a)
                d = dve.tt(s.ap, ob.ap, r.ap, ALU.mult, d, t2)
                ob.free = [d]
                r.free = [d]
                d = dve.stt(hres[:, h, :], s.ap, col(V_HGN + l), hres[:, h, :], ALU.mult, ALU.mult, d)
                s.free = [d]
                done["o", h] = d
                yield

        def attention(l, scope):
            q = sb(f"nq{l}", [P, 4, T], F32, scope)
            ks = sb(f"nk{l}", [P, 2, T], F32, scope)
            vt = sb(f"nv{l}", [P, 2, 4, P], F32, scope)
            cc = sb(f"nc{l}", [P, 2, T], F32, scope)
            rope = sb(f"nr{l}", [P, 2, T], F32, scope)
            tb = sb(f"ntb{l}", [P, 5 * P], F32, scope)
            mats = sb(f"nm{l}", [P, 2, 160], F32, scope)
            xx = sb(f"nx{l}", [P, 16, 62], F32, scope)
            xxh = sb(f"nxh{l}", [P, 16, 62], F32R, scope)
            xxl = sb(f"nxl{l}", [P, 16, 62], F32R, scope)
            hid = sb(f"nh{l}", [P, 2, 62], F32, scope)
            kc = sb(f"nkc{l}", [P, 32], F32, scope)
            vcm = sb(f"nvc{l}", [32, P], F32, scope)
            gt = sb(f"ng{l}", [P, 4, 24], F32, scope)
            pc = sb(f"npc{l}", [P, 32, 31], F32, scope)
            pct = sb(f"npt{l}", [32, 32, P], F32, scope)
            st1 = sb(f"ns{l}", [P, 112], F32, scope)
            pp = [Buf(sb(f"np{l}{i}", [P, 2, T], F32, scope)) for i in range(2)]
            pt = [Buf(sb(f"nt{l}{i}", [P, 2, T], F32, scope)) for i in range(1)]
            small = [Buf(sb(f"nsm{l}{i}", [P, 16], F32, scope)) for i in range(2)]
            names = ("le", "rot", "mean64", "cneg", "cone")
            le, rotm, mean64, cneg, cone = (tb[:, i * P:(i + 1) * P] for i in range(5))
            for i, n in enumerate(names):
                table(tb, i * P, n)
            for i, n in enumerate(("cos", "sin")):
                table(rope[:, i, :], 0, n)
            ct = None
            for i in range(2):
                ct = load(mats[:, i, :], mats_in[l, i, :, :])
            for x in (pe, act, dve):
                x.wait([ct])
            cos, sin = rope[:, 0, :], rope[:, 1, :]
            qg = dve.ts(st1[:, 0:1], col(V_QG + l), 0.125, ALU.mult, s2=1.0, op1=ALU.mult)
            dve.wait([qg])

            def head_norm(dst, src, gain, c, s, n, t, b):
                s0, s1, s2 = tmp[0], tmp[1], tmp[2]
                b2, b3 = bank[4], bank[5]
                a = act.act(s0.ap[:, 0:n], src, ACT.Square, t, s0.free)
                m = pe.mm(b2.ap[:, 0:n], mean64, s0.ap[:, 0:n], True, True, a, b2.free, signal=True)
                a = act.act(s1.ap[:, 0:n], b2.ap[:, 0:n], ACT.Sqrt, m, s1.free, bias=col(V_EPS + 1))
                b2.free = [a]
                d = dve.recip(s1.ap[:, 0:n], s1.ap[:, 0:n], a)
                d = dve.stt(s0.ap[:, 0:n], src, gain, s1.ap[:, 0:n], ALU.mult, ALU.mult, d, m)
                b.free = [d]
                m = pe.mm(b3.ap[:, 0:n], rotm, s0.ap[:, 0:n], True, True, d, b3.free, signal=True)
                d1 = dve.tt(s2.ap[:, 0:n], s0.ap[:, 0:n], c, ALU.mult, d, s2.free)
                d2 = dve.tt(s1.ap[:, 0:n], b3.ap[:, 0:n], s, ALU.mult, m)
                b3.free = [d2]
                d = dve.tt(dst, s2.ap[:, 0:n], s1.ap[:, 0:n], ALU.add, d1, d2)
                s0.free = s1.free = s2.free = [d]
                return d

            def tokens(c, b, t):
                a = act.copy(tmp[3].ap, b.ap, t, tmp[3].free)
                b.free = [a]
                t, d = to_tokens(vt[:, c, :, :], tmp[3].ap, bank[6 + c], a)
                tmp[3].free = [t]
                return d

            done = {}
            for c in range(2):
                b = next_bank()
                t = project(b)
                done["c", c] = act.copy(cc[:, c, :], b.ap, t)
                b.free = [done["c", c]]
                yield
            for c in range(2):
                b = next_bank()
                t = project(b)
                done["k", c] = head_norm(ks[:, c, :], b.ap, col(V_KG + 4 * l + 1 + c), cos, sin, T, t, b)
                yield
                b = next_bank()
                t = project(b)
                done["v", c] = tokens(c, b, t)
                yield
            b = next_bank()
            t = project(b)
            s = tmp[4]
            a = act.act(s.ap[0:32, :], b.ap[0:32, :], ACT.Sigmoid, t, s.free)
            b.free = [a]
            b = bank[6]
            for i in range(4):
                t = pe.turn(b.ap[:, i * 32:(i + 1) * 32], s.ap[0:32, i * P:(i + 1) * P], ident[0:32, 0:32], a, b.free, signal=(i == 3))
            gt_ok = dve.copy(gt[:, :, :], b.ap[:, 0:P].rearrange("p (i f) -> p i f", f=32)[:, :, 0:24], t)
            b.free = [gt_ok]
            s.free = [t]
            yield
            for c in range(4):
                b = next_bank()
                t = project(b)
                done["q", c] = head_norm(q[:, c, :], b.ap, st1[:, 0:1], cos, sin, T, t, b)
                yield
            used = None
            for c in range(2):
                d = done["c", c]
                for g in range(2):
                    rg = slice(64 * g, 64 * g + 64)
                    src = cc[rg, c, :].rearrange("p (n c) -> p c n", c=16)
                    pos = mats[rg, c, 0:32]
                    for par in range(2):
                        for up in range(2):
                            o = xx[64 * par:64 * par + 64, 8 * up:8 * up + 8, 31 * g:31 * g + 31]
                            y = dve.tt(o, src[:, par::2, up:up + 31], along(pos[:, 16 * up + par:16 * up + 16:2], 31), ALU.add, d, used)
                a = act.copy(xxh[:, :, :], xx[:, :, :], y, used)
                y = dve.tt(xxl[:, :, :], xx[:, :, :], f32(xxh[:, :, :]), ALU.subtract, a, used)
                for hh in range(2):
                    b = next_bank()
                    t = gemm(16, lambda k: xxh[:, k, :], lambda k: xxl[:, k, :], b.ap[:, 0:62], lambda k: [a, y], b.free)
                    h = act.act(hid[:, hh, :], b.ap[:, 0:62], ACT.Silu, t, done.get("hid"))
                    b.free = [h]
                    yield
                used = t
                b = next_bank()
                w2 = mats[:, c, 32:160].rearrange("p (h f) -> p h f", h=2)
                for g in range(2):
                    for hh in range(2):
                        t = pe.mm(b.ap[64 * g:64 * g + 64, 0:31], w2[:, hh, :], hid[:, hh, 31 * g:31 * g + 31], hh == 0, hh == 1, h, b.free, signal=True)
                done["hid"] = t
                if c == 0:
                    done["kc"] = head_norm(kc[:, 0:31], b.ap[:, 0:31], col(V_KG + 4 * l), cos[:, 31::16], sin[:, 31::16], 31, t, b)
                else:
                    s = tmp[3]
                    a = act.copy(s.ap[:, 0:31], b.ap[:, 0:31], t, s.free)
                    b.free = [a]
                    t = pe.turn(bank[6].ap[0:31, 0:P], s.ap[:, 0:31], ident, a, bank[6].free, signal=True)
                    vcm_ok = dve.copy(vcm[0:31, :], bank[6].ap[0:31, 0:P], t)
                    bank[6].free = [vcm_ok]
                    s.free = [t]
                yield
            pe.wait([done["q", 3], done["k", 1], done["v", 1], done["kc"], vcm_ok])

            nmx, sm = st1[:, 8:40], st1[:, 40:72]
            for hf in range(2):
                b = bank[hf]
                rg = slice(64 * hf, 64 * hf + 64)
                for t in range(4):
                    for i in range(4):
                        at = 4 * t + i
                        x = pe.mm(b.ap[:, 32 * at:32 * at + 31], q[rg, t, i * P:(i + 1) * P], kc[rg, 0:31], True, True, b.free, signal=True)
                p3 = pc[:, 16 * hf:16 * hf + 16, :]
                s3 = b.ap.rearrange("p (u n) -> p u n", n=32)[:, :, 0:31]
                cn = cneg.rearrange("p (i n) -> p i n", n=32)[:, :, 0:31]
                for u in range(4):
                    y = dve.tt(p3[:, 4 * u:4 * u + 4, :], s3[:, 4 * u:4 * u + 4, :], cn, ALU.add, x)
                b.free = [y]
                m, s = nmx[:, 16 * hf:16 * hf + 16], sm[:, 16 * hf:16 * hf + 16]
                y = dve.maxneg(m, p3, y)
                y = dve.tt(p3, p3, along(m, 31), ALU.add, y)
                a = act.act(p3, p3, ACT.Exp, y)
                y = dve.put(lambda e, s=s, p3=p3: e.tensor_reduce(s, p3, AX, ALU.add), [a])
                y = dve.recip(s, s, y)
                for u in range(4):
                    head = 4 * hf + u
                    w = dve.tt(s[:, 4 * u:4 * u + 4], s[:, 4 * u:4 * u + 4], gt[:, :, 3 * head], ALU.mult, y, gt_ok)
                y = dve.tt(p3, p3, along(s, 31), ALU.mult, w)
                c1 = cone.rearrange("p (i n) -> p i n", n=32)[:, :, 0:31]
                for u in range(4):
                    y2 = dve.tt(p3[:, 4 * u:4 * u + 4, :], p3[:, 4 * u:4 * u + 4, :], c1, ALU.mult, y)
                for u in range(4):
                    b = bank[4 + u]
                    for i in range(4):
                        x = pe.turn(b.ap[0:31, i * P:(i + 1) * P], p3[:, 4 * u + i, :], ident, y2, b.free, signal=True)
                    z = act.copy(pct[0:31, 16 * hf + 4 * u:16 * hf + 4 * u + 4, :], b.ap[0:31, :].rearrange("p (i f) -> p i f", i=4), x)
                    b.free = [z]
                yield
            pe.wait([z])
            units = [(t, g, i) for t in range(4) for i in range(4) for g in range(2)]
            stage = {}

            def first(n):
                t, g, i = units[n]
                for br in range(2):
                    b = bank[2 * (n % 2) + br]
                    stage[n] = pe.mm(b.ap[:, 0:(i + 1) * P], q[64 * g:64 * g + 64, t, i * P:(i + 1) * P],
                                     ks[64 * g:64 * g + 64, br, 0:(i + 1) * P], True, True, b.free, signal=True)

            def second(n):
                t, g, i = units[n]
                head = t + 4 * g
                w = (i + 1) * P
                two = ps[:, 2 * (n % 2):2 * (n % 2) + 2, :]
                pair = (bank[2 * (n % 2)], bank[2 * (n % 2) + 1])
                p, m = pp[n % 2], small[n % 2]
                nm, sums = m.ap[:, 0:2], m.ap[:, 2:4]
                d = dve.tt(two[:, :, i * P:w], two[:, :, i * P:w], over(le, 2), ALU.add, stage[n])
                d = dve.maxneg(nm, two[:, :, 0:w], d, m.free)
                for br in range(2):
                    a = act.act(p.ap[:, br, 0:w], two[:, br, 0:w], ACT.Exp, d, p.free, bias=nm[:, br:br + 1], total=sums[:, br:br + 1])
                for b in pair:
                    b.free = [a]
                d = dve.recip(sums, sums, a)
                d = dve.tt(sums, sums, gt[:, i, 3 * head + 1:3 * head + 3], ALU.mult, d)
                for br in range(2):
                    d2 = dve.ts(p.ap[:, br, 0:w], p.ap[:, br, 0:w], sums[:, br:br + 1], ALU.mult, d, s2=1.0, op1=ALU.mult)
                m.free = [d2]
                stage[n] = d2

            def third(n):
                t, g, i = units[n]
                p, y = pp[n % 2], pt[0]
                for br in range(2):
                    b = bank[4 + br]
                    for j in range(i + 1):
                        x = pe.turn(b.ap[:, j * P:(j + 1) * P], p.ap[:, br, j * P:(j + 1) * P], ident, stage[n], b.free, signal=(j == i))
                    w = (i + 1) * P
                    z = (dve if br else act).copy(y.ap[:, br, 0:w], b.ap[:, 0:w], x, y.free)
                    b.free = [z]
                    stage[n, br] = z
                p.free = [x]

            def fourth(n):
                t, g, i = units[n]
                b, y = bank[6 + t % 2], pt[0]
                o = b.ap[64 * g:64 * g + 64, i * P:(i + 1) * P]
                pe.mm(o, vcm[0:31, 64 * g:64 * g + 64], pct[0:31, 16 * g + 4 * t + i, :], True, False, b.free)
                for br in range(2):
                    for j in range(i + 1):
                        end = br == 1 and j == i
                        x = pe.mm(o, vt[:, br, j, 64 * g:64 * g + 64], y.ap[:, br, j * P:(j + 1) * P], False, end, stage[n, br], signal=end)
                y.free = [x]
                if i == 3 and g == 1:
                    b.free = [store_parts(4 + t, b.ap, x, st["xused"])]
                    b.free += st["x"][4 + t]

            for n in range(len(units) + 2):
                if n < len(units):
                    first(n)
                    second(n)
                if 0 <= n - 2:
                    fourth(n - 2)
                if 0 <= n - 1 < len(units):
                    third(n - 1)
                yield

        def nsa(l):
            fence()
            outer = ExitStack()
            hres = sb(f"hres{l}", [P, 4, T], F32, outer)
            scope = ExitStack()
            run_all(hgrn(l, hres, scope))
            fence()
            scope.close()
            scope = ExitStack()
            run_all(attention(l, scope))
            for h in range(4):
                d = store_parts(h, hres[:, h, :], st["xused"])
            fence()
            scope.close()
            outer.close()
            mem_free[:] = [d]


        for step in plan:
            kind, args = step[0], step[1:]
            nm = None
            if kind == "scale":
                prescale()
            elif kind == "ffn_ln":
                nm = Norm(False)
                ffn(0.5, nm)
                layer_norm(nm, args[0], args[1])
            elif kind == "ffn_rms":
                nm = Norm(True)
                ffn(1.0, nm)
                rms_norm(nm, args[0])
            elif kind == "ffn_end":
                ffn(1.0, None)
            elif kind == "rms":
                nm = Norm(True)
                for k in range(KD):
                    nm.add(k, st["xr"][k])
                rms_norm(nm, args[0])
            elif kind == "mlstm":
                mlstm()
                nm = Norm(False)
                out_proj(nm)
                layer_norm(nm, args[0], True)
            elif kind == "window":
                window()
                nm = Norm(False)
                out_proj(nm)
                layer_norm(nm, args[0], True)
            elif kind == "nsa":
                nsa(args[0])
                nm = Norm(True)
                out_proj(nm)
                rms_norm(nm, args[1])
        assert tile_n[0] == n_units * UT, (tile_n[0], n_units * UT)
        outs = out.rearrange("(k p) t -> p k t", p=P)
        for k in range(KD):
            sp.wait([st["xr"][k]])
            sp.items.append(("dma", lambda e, k=k: e.dma_start(outs[:, k, :], xr[:, k, :]), "out"))
        sp.items.append(("wait", "out", 16 * KD))

        block = ctx.enter_context(nc.Block())

        @block.sync
        def _(e):
            for kind, a, b in sp.items:
                if kind == "wait":
                    e.wait_ge(sems[a], b)
                else:
                    a(e).then_inc(sems[b], 16)

        @block.tensor
        def _(e):
            pe.play(e, sems)

        @block.vector
        def _(e):
            dve.play(e, sems)

        @block.scalar
        def _(e):
            act.play(e, sems)

        @block.gpsimd
        def _(e):
            pool.play(e, sems)


PLAN = [("scale",), ("ffn_ln", 0, True), ("mlstm", 1), ("ffn_ln", 2, True), ("ffn_ln", 3, True), ("window", 4),
        ("ffn_ln", 5, False), ("rms", V_NM), ("nsa", 0, V_NF), ("ffn_rms", V_NM + 8), ("nsa", 1, V_NF + 8), ("ffn_end",)]


def columns(w, cols=None):
    w = np.asarray(w)
    if cols is None:
        cols = np.arange(w.shape[1])
    cols = np.asarray(cols)
    picked = w[:, np.maximum(cols, 0)]
    if (cols < 0).any():
        picked[:, cols < 0] = 0
    k, n = picked.shape
    return picked.reshape(k // P, P, n // P, P).transpose(2, 0, 1, 3).reshape(-1, P, P)


def head_pairs(order, dim=64):
    return np.concatenate([np.arange(h * dim, (h + 1) * dim) for h in order])


WIN_ORDER = [h for t in range(8) for h in ((t % 4) + 8 * (t // 4), (t % 4) + 4 + 8 * (t // 4))]
NSA_ORDER = [h for t in range(4) for h in (t, 4 + t)]


def stream(inp, plan):
    parts = []

    def ffn(w_in, w_out):
        w = columns(w_in).reshape(2, KF, KD, P, P)
        parts.append(w.transpose(1, 0, 2, 3, 4).reshape(-1, P, P))
        parts.append(columns(w_out))

    for step in plan:
        if step[0] == "ffn_ln":
            l, j = {0: (0, 0), 2: (0, 1), 3: (1, 0), 5: (1, 1)}[step[1]]
            ffn(inp["ffn_w_in"][l, j], inp["ffn_w_out"][l, j])
        elif step[0] in ("ffn_rms", "ffn_end"):
            l = 0 if step[0] == "ffn_rms" else 1
            ffn(inp["w_ffn_in_2"][l], inp["w_ffn_out_2"][l])
        elif step[0] == "mlstm":
            w = inp["ml_w_in"][0]
            g = np.full(P, -1)
            for q, at in enumerate((0, 64, 32, 96)):
                g[at:at + 4] = 3072 + 4 * q + np.arange(4)
            parts.append(columns(w, g))
            parts.append(columns(w, np.arange(3072)))
            parts.append(columns(inp["ml_w_out"][0]))
        elif step[0] == "window":
            order = head_pairs(WIN_ORDER)
            parts.append(columns(inp["at_w_in"][0], np.concatenate([np.arange(1024, 1536), order])))
            parts.append(columns(inp["at_w_out"][0][order, :]))
        elif step[0] == "nsa":
            l = step[1]
            w = inp["w_in_2"][l]
            gate = np.full(P, -1)
            gate[:24] = 2048 + 512 + 768 + np.arange(24)
            order = head_pairs(NSA_ORDER)
            parts.append(columns(w, np.arange(2048)))
            parts.append(columns(w, np.concatenate([np.arange(2560, 2560 + 768), gate, 2048 + order])))
            parts.append(columns(inp["cmp_w1_k_2"][l]))
            parts.append(columns(inp["cmp_w1_v_2"][l]))
            rows = np.concatenate([np.arange(512), 512 + order])
            parts.append(columns(inp["w_out_2"][l][rows, :]))
    w = np.concatenate(parts)
    return np.ascontiguousarray(w.reshape(-1, UT, P, P).transpose(0, 2, 1, 3)).reshape(-1, P, UT * P)


def vectors(inp):
    v = np.zeros((P, V_N), np.float32)

    def put(at, a):
        a = np.asarray(a).reshape(-1, P)
        v[:, at:at + a.shape[0]] = a.T

    put(V_LNG, inp["ln_g"])
    put(V_LNB, inp["ln_b"])
    v[:, V_EPS] = LN_EPS
    v[:, V_EPS + 1] = RMS_EPS
    for q, at in enumerate((0, 64, 32, 96)):
        v[at:at + 4, V_GB] = inp["ml_gate_b"][0][4 * q:4 * q + 4]
    put(V_MNG, inp["ml_norm_g"])
    v[:, V_SINK:V_SINK + 16] = inp["at_sink"][0][WIN_ORDER][None, :]
    for l in range(2):
        put(V_LB + 4 * l, inp["hg_lb_logits_2"][l])
        v[:, V_HGN + l] = inp["hg_gnorm_2"][l]
        v[:, V_QG + l] = np.tile(inp["q_gain_2"][l], 2)
        for b in range(3):
            v[:, V_KG + 4 * l + b] = np.tile(inp["k_gain_2"][l, b], 2)
    put(V_NM, inp["norm_mix_2"])
    put(V_NF, inp["norm_ffn_2"])
    return v


def small_mats(inp):
    m = np.zeros((2, 2, P, 32 + 128), np.float32)
    for l in range(2):
        for i, n in enumerate("kv"):
            m[l, i, :, :32] = np.tile(inp[f"cmp_pe_{n}_2"][l].T, (2, 1))
            m[l, i, :, 32:] = inp[f"cmp_w2_{n}_2"][l].reshape(2, P, 64).transpose(1, 0, 2).reshape(P, 128)
    return m


def arrange(inp, plan, x):
    t = lay_tables()
    return {
        "in_x": np.ascontiguousarray(np.asarray(x).reshape(T, D).T),
        "in_w": stream(inp, plan),
        "in_vec": vectors(inp),
        "in_tab": np.concatenate([t[k] for k in SPANS], axis=1),
        "in_mat": small_mats(inp),
    }


def kernel(**inputs):
    import numpy as _np
    import concourse.bacc as _bacc
    from concourse import mybir as _mybir
    from concourse.bass_utils import run_bass_kernel_spmd as _run

    inp = {k: _np.asarray(v) for k, v in inputs.items()}
    arrays = arrange(inp, PLAN, inp["x"])
    nc = _bacc.Bacc("TRN2", target_bir_lowering=False, num_devices=1)
    args = [nc.dram_tensor(k, a.shape, _mybir.dt.float32, kind="ExternalInput").ap() for k, a in arrays.items()]
    args.append(nc.dram_tensor("out_0", [D, T], _mybir.dt.float32, kind="ExternalOutput").ap())
    build(nc, *args, PLAN)
    r = _run(nc, [arrays], core_ids=[0])
    return _np.ascontiguousarray(r.results[0]["out_0"].T).reshape(1, T, D)
```

```python
from contextlib import ExitStack

import numpy as np

import concourse.bass as bass
from concourse import mybir

P = 128
T = 512
D = 1024
KD = D // P
FF = 2816
KF = FF // P
ALPHA = 4 ** 0.25
LN_EPS = 1e-5
RMS_EPS = 1e-6
NEG = -1e30
UT = 8
NRAW = 5
NW = 4
NLD = 4
AHEAD = 2

ALU = mybir.AluOpType
ACT = mybir.ActivationFunctionType
AX = mybir.AxisListType.X
F32 = mybir.dt.float32
F32R = mybir.dt.float32r
U32 = mybir.dt.uint32

V_LNG, V_LNB = 0, 48
V_EPS = 96
V_GB = 100
V_MNG = 104
V_SINK = 112
V_LB = 128
V_HGN = 144
V_QG, V_KG = 146, 148
V_NM, V_NF = 156, 172
V_N = 192


def lay_tables():
    p = np.arange(P)[:, None]
    f = np.arange(P)[None, :]
    one = np.ones((P, P), np.float32)
    causal = np.where(f >= p, 0.0, NEG)
    acausal = np.where(f <= p, 0.0, NEG)
    t = {"ident": (p == f), "mean1024": one / 1024}
    for h in (16, 8, 4, 2, 1):
        t[f"lv{h}"] = (p // (2 * h) == f // (2 * h)) & (p % (2 * h) < h) & (f % (2 * h) >= h)
    t["mean128"] = one / 128
    t["keep"] = np.broadcast_to((np.arange(T) % P != 0)[None, :], (P, T))
    t["le"] = acausal
    rot = np.zeros((P, P))
    for i in range(P):
        if i % 64 < 32:
            rot[i + 32, i] = -1.0
        else:
            rot[i - 32, i] = 1.0
    t["rot"] = rot
    t["mean64"] = (p // 64 == f // 64) / 64.0
    ends = np.arange(31) * 16 + 31
    tok = np.arange(4)[None, :, None] * P + p[:, :, None]
    seen = np.zeros((P, 4, 32), bool)
    seen[:, :, :31] = ends[None, None, :] <= tok
    t["cneg"] = np.where(seen, 0.0, NEG).reshape(P, P)
    t["cone"] = seen.reshape(P, P).astype(np.float32)
    half = 32
    freqs = np.float32(10000.0) ** (-np.arange(half, dtype=np.float32) / np.float32(half))
    ang = np.arange(T, dtype=np.float32)[None, :] * freqs[np.arange(P) % half][:, None]
    t["cos"] = np.cos(ang.astype(np.float32))
    t["sin"] = np.sin(ang.astype(np.float32))
    t["mle"] = acausal
    t["mge"] = causal
    t["one"] = one
    t["mean256"] = one / 256
    kj = np.arange(3 * P)[None, :]
    rel = p - kj + P
    t["dist"] = np.where(np.abs(rel) <= P, np.abs(rel), 1e30)
    return {k: np.ascontiguousarray(v, np.float32) for k, v in t.items()}


def table_spans():
    at, spans = 0, {}
    for k, v in lay_tables().items():
        spans[k] = (at, v.shape[1])
        at += v.shape[1]
    return spans, at


SPANS, TABLE_N = table_spans()


class Queue:

    def __init__(self, sem):
        self.sem = sem
        self.n = 0
        self.items = []
        self.seen = {}

    def wait(self, waits):
        for w in waits:
            if w is None:
                continue
            if isinstance(w, (list, tuple)) and not (len(w) == 2 and isinstance(w[0], str)):
                self.wait(w)
                continue
            sem, value = w
            if self.seen.get(sem, 0) < value:
                self.seen[sem] = value
                self.items.append(("wait", sem, value))

    def put(self, fn, waits, signal=True):
        self.wait(waits)
        if not signal:
            self.items.append(("do", fn, None))
            return None
        self.n += 1
        self.items.append(("do", fn, self.sem))
        return (self.sem, self.n)

    def play(self, eng, sems):
        for kind, a, b in self.items:
            if kind == "wait":
                eng.wait_ge(sems[a], b)
            else:
                ins = a(eng)
                if b is not None:
                    ins.then_inc(sems[b], 1)


class Vec(Queue):
    def tt(self, out, a, b, op, *w):
        return self.put(lambda e: e.tensor_tensor(out, a, b, op), w)

    def ts(self, out, a, s1, op0, *w, s2=None, op1=None):
        if op1 is None:
            return self.put(lambda e: e.tensor_scalar(out, a, s1, None, op0), w)
        return self.put(lambda e: e.tensor_scalar(out, a, s1, s2, op0, op1), w)

    def stt(self, out, a, s, b, op0, op1, *w):
        return self.put(lambda e: e.scalar_tensor_tensor(out=out, in0=a, scalar=s, in1=b, op0=op0, op1=op1), w)

    def copy(self, out, a, *w):
        return self.put(lambda e: e.tensor_copy(out, a), w)

    def recip(self, out, a, *w):
        return self.put(lambda e: e.reciprocal(out, a), w)

    def scan(self, out, a, b, op0, op1, *w):
        return self.put(lambda e: e.tensor_tensor_scan(out, a, b, 0.0, op0, op1), w)

    def maxneg(self, out, a, *w):
        return self.put(lambda e: e.tensor_reduce(out, a, AX, ALU.max, negate=True), w)

    def pick(self, out, mask, a, *w):
        return self.put(lambda e: e.copy_predicated(out, mask, a), w)

    def fill(self, out, v, *w):
        return self.put(lambda e: e.memset(out, v), w)


class Act(Queue):
    def act(self, out, a, func, *w, scale=1.0, bias=0.0, total=None):
        if total is None:
            return self.put(lambda e: e.activation(out, a, func, bias=bias, scale=scale), w)
        return self.put(lambda e: e.activation(out, a, func, bias=bias, scale=scale, accum_out=total), w)

    def copy(self, out, a, *w):
        return self.put(lambda e: e.activation(out, a, ACT.Copy), w)


class Pe(Queue):
    def mm(self, out, l, r, start, stop, *w, signal=False):
        return self.put(lambda e: e.matmul(out, l, r, start=start, stop=stop), w, signal)

    def turn(self, out, a, ident, *w, signal=False):
        return self.put(lambda e: e.transpose(out, a, ident), w, signal)


class Buf:

    def __init__(self, ap):
        self.ap = ap
        self.free = []


def f32(ap):
    return ap.bitcast(F32)


def interleave(main, side, ratio):
    owed = 0.0
    for _ in main:
        owed += ratio
        while owed >= 1.0:
            owed -= 1.0
            if next(side, "end") == "end":
                owed = -1e9
    for _ in side:
        pass


def run_all(g):
    for _ in g:
        pass


def build(nc, xin, wst, vec, tab, mats_in, out, plan):
    with ExitStack() as ctx:
        def sem(name):
            return ctx.enter_context(nc.semaphore(name))

        def sb(name, shape, dt=F32, scope=ctx):
            return scope.enter_context(nc.sbuf_tensor(name, shape, dt))

        sems = {k: sem("s_" + k) for k in ("pe", "dve", "act", "pool", "out")}
        for i in range(NLD):
            sems[f"ld{i}"] = sem(f"s_ld{i}")
        for i in range(NRAW):
            sems[f"raw{i}"] = sem(f"s_raw{i}")
        pe, dve, act, pool = Pe("pe"), Vec("dve"), Act("act"), Vec("pool")
        sp = Queue("sp")

        ps = ctx.enter_context(nc.psum_tensor("ps", [P, 8, 512], F32))
        bank = [Buf(ps[:, i, :]) for i in range(8)]

        raw = [sb(f"raw{i}", [P, UT * P]) for i in range(NRAW)]
        whi = [sb(f"whi{i}", [P, UT * P], F32R) for i in range(NW)]
        wlo = [sb(f"wlo{i}", [P, UT * P], F32R) for i in range(NW)]
        xr = sb("xr", [P, KD, T])
        xh = sb("xh", [P, KD, T], F32R)
        xl = sb("xl", [P, KD, T], F32R)
        vc = sb("vc", [P, V_N])
        res = sb("res", [P, 2 * P])
        tmp = [Buf(sb(f"tmp{i}", [P, T])[:, :]) for i in range(5)]
        ident, mean1024 = res[:, 0:P], res[:, P:2 * P]

        def table(tile, first, last=None):
            a = SPANS[first][0]
            z = sum(SPANS[last or first])
            return load(tile, tab[:, a:z])

        loads = [0]

        def load(dst, src, *w):
            i, n = loads[0] % NLD, loads[0] // NLD
            loads[0] += 1
            sp.wait([w, (f"ld{i}", 16 * n) if n else None])
            sp.items.append(("dma", lambda e: e.dma_start(dst, src), f"ld{i}"))
            return (f"ld{i}", 16 * (n + 1))

        n_units = wst.shape[0]
        unit = [0]
        prepared = [0]
        ready = {}
        spent = {}
        rawfree = {}

        def prep(u):
            if u >= n_units:
                return
            r, s = u % NRAW, u % NW
            sp.wait([rawfree.get(u - NRAW)])
            sp.items.append(("dma", lambda e: e.dma_start(raw[r][:, :], wst[u, :, :]), f"raw{r}"))
            landed = (f"raw{r}", 16 * (u // NRAW + 1))
            prepared[0] = u + 1
            return landed

        landed = {}
        fetched = [0]

        def fetch(u):
            while fetched[0] <= u and fetched[0] < n_units:
                landed[fetched[0]] = prep(fetched[0])
                fetched[0] += 1

        split_n = [0]

        def split(u):
            while split_n[0] <= u and split_n[0] < n_units:
                v = split_n[0]
                fetch(v + NRAW - 1)
                r, s = v % NRAW, v % NW
                a = act.copy(whi[s][:, :], raw[r][:, :], landed[v], spent.get(v - NW))
                d = dve.tt(wlo[s][:, :], raw[r][:, :], f32(whi[s][:, :]), ALU.subtract, landed[v], a, spent.get(v - NW))
                ready[v] = [a, d]
                rawfree[v] = d
                split_n[0] += 1

        tile_n = [0]

        def gemm(kt, hi, lo, out, waits, *w, first=True, last=True, n=None):
            tok = None
            for k in range(kt):
                u, j = divmod(tile_n[0], UT)
                need = []
                if j == 0 or k == 0:
                    split(u + AHEAD)
                    need = ready[u]
                s = u % NW
                wh, wl = whi[s][:, j * P:(j + 1) * P], wlo[s][:, j * P:(j + 1) * P]
                a = first and k == 0
                b = last and k == kt - 1
                pe.mm(out, wh, hi(k), a, False, need, waits(k), *(w if k == 0 else ()))
                pe.mm(out, wh, lo(k), False, False)
                tok = pe.mm(out, wl, hi(k), False, b, signal=(j == UT - 1 or k == kt - 1))
                if j == UT - 1:
                    spent[u] = tok
                tile_n[0] += 1
                if k % UT in st["ticks"]:
                    tick()
            return tok

        def pair(b0, b1):
            u = tile_n[0] // UT
            split(u + 1 + AHEAD)
            toks = [None, None]
            for k in range(KD):
                for i, b in enumerate((b0, b1)):
                    s = (u + i) % NW
                    wh, wl = whi[s][:, k * P:(k + 1) * P], wlo[s][:, k * P:(k + 1) * P]
                    pe.mm(b.ap, wh, xh[:, k, :], k == 0, False, ready[u + i], st["x"][k], b.free)
                    pe.mm(b.ap, wh, xl[:, k, :], False, False)
                    toks[i] = pe.mm(b.ap, wl, xh[:, k, :], False, k == KD - 1, signal=(k == KD - 1))
                if k in st["ticks"]:
                    tick()
            spent[u], spent[u + 1] = toks
            tile_n[0] += 2 * UT
            st["xused"] = toks[1]
            tick()
            return toks

        pending = []

        def spawn(g, now=False):
            if now:
                next(g, None)
            pending.append(g)

        def tick():
            for g in list(pending):
                if next(g, "end") == "end":
                    pending.remove(g)

        def drain():
            while pending:
                tick()

        def take(free):
            while not free:
                yield
            return free.pop(0)

        st = {"xr": [None] * KD, "x": [[] for _ in range(KD)], "xused": None, "ticks": (3,)}
        rot = [0]

        def next_bank(k=4):
            b = bank[rot[0] % k]
            rot[0] += 1
            return b

        def xk(k):
            return st["x"][k]

        def project(b):
            t = gemm(KD, lambda k: xh[:, k, :], lambda k: xl[:, k, :], b.ap, xk, b.free)
            st["xused"] = t
            tick()
            return t

        xs = xin.rearrange("(k p) t -> p k t", p=P)
        fetch(0)
        xt = [load(xr[:, 0:4, :], xs[:, 0:4, :]), load(xr[:, 4:8, :], xs[:, 4:8, :])]
        fetch(1)
        c0 = [load(vc[:, :], vec), table(res[:, :], "ident", "mean1024")]
        for k in range(KD):
            a = act.copy(xh[:, k, :], xr[:, k, :], xt[k // 4])
            d = dve.tt(xl[:, k, :], xr[:, k, :], f32(xh[:, k, :]), ALU.subtract, a)
            st["x"][k] = [a, d]
            st["xr"][k] = d
            if k == 1:
                split(1)
        dve.wait([c0])
        act.wait([c0])
        pe.wait([c0])

        def prescale():
            for k in range(KD):
                st["xr"][k] = pool.ts(xr[:, k, :], xr[:, k, :], ALPHA, ALU.mult, st["xr"][k], s2=1.0, op1=ALU.mult)

        class Norm:

            def __init__(self, square):
                self.square = square
                self.acc = tmp[4]
                self.tok = None

            def add(self, k, t):
                z = xr[:, k, :]
                if self.square:
                    if k == 0:
                        self.tok = act.act(self.acc.ap, z, ACT.Square, t, self.acc.free)
                    else:
                        s = tmp[k % 2]
                        a = act.act(s.ap, z, ACT.Square, t, s.free)
                        self.tok = pool.tt(self.acc.ap, self.acc.ap, s.ap, ALU.add, a, self.tok)
                        s.free = [self.tok]
                elif k == 0:
                    self.tok = pool.put(lambda e: e.tensor_copy(self.acc.ap, z), [t, self.acc.free])
                else:
                    self.tok = pool.tt(self.acc.ap, self.acc.ap, z, ALU.add, t, self.tok)

        def layer_norm(nm, l, scale_next):
            b = next_bank()
            m = pe.mm(b.ap, mean1024, nm.acc.ap, True, True, nm.tok, b.free, signal=True)
            nm.acc.free = [m]
            b2 = next_bank()
            t = None
            dt = []
            for k in range(KD):
                d = dve.tt(xr[:, k, :], xr[:, k, :], b.ap, ALU.subtract, m, st["xr"][k])
                dt.append(d)
                s = tmp[k % 2]
                a = act.act(s.ap, xr[:, k, :], ACT.Square, d, s.free)
                t = pe.mm(b2.ap, mean1024, s.ap, k == 0, k == KD - 1, a, b2.free if k == 0 else None, signal=True)
                s.free = [t]
            b.free = [dt[-1]]
            sd, rc = tmp[2], tmp[3]
            a = act.act(sd.ap, b2.ap, ACT.Sqrt, t, sd.free, bias=vc[:, V_EPS:V_EPS + 1])
            b2.free = [a]
            r = dve.recip(rc.ap, sd.ap, a, rc.free)
            sd.free = [r]
            for k in range(KD):
                g, o = vc[:, V_LNG + 8 * l + k:V_LNG + 8 * l + k + 1], vc[:, V_LNB + 8 * l + k:V_LNB + 8 * l + k + 1]
                n = dve.tt(xr[:, k, :], xr[:, k, :], rc.ap, ALU.mult, r)
                a = act.act(xh[:, k, :], xr[:, k, :], ACT.Identity, n, st["xused"], scale=g, bias=o)
                y = dve.ts(xr[:, k, :], xr[:, k, :], g, ALU.mult, a, n, s2=o, op1=ALU.add)
                d = dve.tt(xl[:, k, :], xr[:, k, :], f32(xh[:, k, :]), ALU.subtract, y, st["xused"])
                st["x"][k] = [a, d]
                st["xr"][k] = d
            rc.free = [d]
            if scale_next:
                prescale()

        def rms_norm(nm, col):
            b = next_bank()
            m = pe.mm(b.ap, mean1024, nm.acc.ap, True, True, nm.tok, b.free, signal=True)
            nm.acc.free = [m]
            sd, rc = tmp[2], tmp[3]
            a = act.act(sd.ap, b.ap, ACT.Sqrt, m, sd.free, bias=vc[:, V_EPS + 1:V_EPS + 2])
            b.free = [a]
            r = dve.recip(rc.ap, sd.ap, a, rc.free)
            sd.free = [r]
            for k in range(KD):
                g = vc[:, col + k:col + k + 1]
                s = tmp[k % 2]
                n = dve.tt(s.ap, xr[:, k, :], rc.ap, ALU.mult, r, st["xr"][k], s.free)
                a = act.act(xh[:, k, :], s.ap, ACT.Copy, n, st["xused"], scale=g)
                d = dve.stt(xl[:, k, :], s.ap, g, f32(xh[:, k, :]), ALU.mult, ALU.subtract, a, n, st["xused"])
                s.free = [d]
                st["x"][k] = [a, d]
            rc.free = [d]

        def residual(k, b, t, by, nm):
            d = dve.stt(xr[:, k, :], b.ap, by, xr[:, k, :], ALU.mult, ALU.add, t, st["xr"][k])
            b.free = [d]
            st["xr"][k] = d
            if nm is not None:
                nm.add(k, d)

        mem_free = []

        def ffn(by, nm):
            scope = ExitStack()
            hh = sb(f"hh{unit[0]}", [P, KF, T], F32R, scope)
            hl = sb(f"hl{unit[0]}", [P, KF, T], F32R, scope)
            unit[0] += 1
            free = list(mem_free)
            hready = []
            for j in range(KF):
                bg, bu = next_bank(), next_bank()
                tg, tu = pair(bg, bu)
                s, h = tmp[j % 2], tmp[2 + j % 2]
                a = act.act(s.ap, bg.ap, ACT.Silu, tg, s.free)
                d = dve.tt(h.ap, s.ap, bu.ap, ALU.mult, a, tu, h.free)
                bg.free, bu.free, s.free = [a], [d], [d]
                a = act.copy(hh[:, j, :], h.ap, d, free)
                d = dve.tt(hl[:, j, :], h.ap, f32(hh[:, j, :]), ALU.subtract, a, free)
                h.free = [d]
                hready.append([a, d])
            for f in range(KD):
                b = next_bank()
                t = gemm(KF, lambda k: hh[:, k, :], lambda k: hl[:, k, :], b.ap, lambda k: hready[k], b.free)
                residual(f, b, t, by, nm)
            mem_free[:] = [t]
            scope.close()

        def out_proj(nm):
            bs = [next_bank(), next_bank()]
            for f, t in enumerate(pair(*bs)):
                residual(f, bs[f], t, 1.0, nm)
            for f in range(2, KD):
                b = next_bank()
                t = project(b)
                residual(f, b, t, 1.0, nm)

        def to_tokens(dst, src, b, *w):
            for i in range(4):
                t = pe.turn(b.ap[:, i * P:(i + 1) * P], src[:, i * P:(i + 1) * P], ident, *(list(w) + b.free if i == 0 else []), signal=(i == 3))
            c = dve.copy(dst, b.ap.rearrange("p (i f) -> p i f", i=4), t)
            b.free = [c]
            return t, c

        def fence(last=None):
            if last is None:
                last = [(q.sem, q.n) for q in (pe, act, dve, pool) if q.n]
            for q in (pe, act, dve, pool, sp):
                q.wait(list(last))

        def col(c, n=1, rows=slice(0, P)):
            return vc[rows, c:c + n]

        def over(ap, n):
            return ap[:, None, :].broadcast_to([ap.shape[0], n, ap.shape[1]])

        def along(ap, n):
            return ap[:, :, None].broadcast_to([ap.shape[0], ap.shape[1], n])

        def store_parts(k, src, *w):
            a = act.copy(xh[:, k, :], src, *w)
            d = dve.tt(xl[:, k, :], src, f32(xh[:, k, :]), ALU.subtract, a, *w)
            st["x"][k] = [a, d]
            return d

        def mlstm():
            fence(mem_free)
            scope = ExitStack()

            def bufs(name, n, shape):
                return [Buf(sb(f"m{name}{i}", shape, F32, scope)) for i in range(n)]

            qb, kb, vb = bufs("q", 2, [P, T]), bufs("k", 2, [P, T]), bufs("v", 2, [P, 4, 2 * P])
            og = sb("mo", [P, 8, T], F32, scope)
            hs = sb("mh", [P, 8, T], F32, scope)
            tb = sb("mtb", [P, 4 * P], F32, scope)
            le, ge, one, mean256 = (tb[:, i * P:(i + 1) * P] for i in range(4))
            ct = table(tb[:, :], "mle", "mean256")
            rows = [sb(f"mr{i}", [64, T], F32, scope) for i in range(3)]
            nM, nm, fx = (r[:, :] for r in rows)
            at = sb("mat", [P, 4 * 64], F32, scope)
            nb, nkb, eb = bufs("n", 2, [P, T]), bufs("nk", 2, [P, T]), bufs("e", 2, [P, T])
            wt, pt = bufs("w", 2, [P, T]), bufs("p", 2, [P, T])
            banks, temps = bank[2:8], tmp[0:5]
            done = {}
            st["ticks"] = (2, 5)

            def gates(b, t):
                four = []
                for _ in range(4):
                    four.append((yield from take(temps)))
                g, f, e1, e2 = (x.ap for x in four)
                a = act.act(g, b.ap, ACT.Identity, t, [x.free for x in four], bias=col(V_GB))
                b.free = [a]
                d = dve.copy(f[0:64, :], g[64:128, :], a)
                yield
                a = act.act(e1[0:64, :], f[0:64, :], ACT.Abs, d)
                a = act.act(e2[0:64, :], e1[0:64, :], ACT.Exp, a, scale=-1.0)
                d = dve.ts(e2[0:64, :], e2[0:64, :], 1.0, ALU.add, a)
                a = act.act(e1[0:64, :], e2[0:64, :], ACT.Ln, d)
                d = dve.stt(f[0:64, :], f[0:64, :], 0.0, e1[0:64, :], ALU.min, ALU.subtract, a)
                d1 = dve.fill(e2[0:64, :], 1.0)
                yield
                dve.scan(e1[0:32, :], e2[0:32, :], f[0:32, :], ALU.mult, ALU.add, d, d1)
                d = dve.scan(e1[32:64, ::-1], e2[32:64, :], f[32:64, ::-1], ALU.mult, ALU.add)
                d = dve.tt(fx, g[0:64, :], e1[0:64, :], ALU.subtract, d)
                dve.scan(f[0:32, :], fx[0:32, :], fx[0:32, :], ALU.max, ALU.max, d)
                d = dve.scan(f[32:64, ::-1], fx[32:64, ::-1], fx[32:64, ::-1], ALU.max, ALU.max)
                d = dve.ts(nM, f[0:64, :], -1.0, ALU.mult, d, s2=1.0, op1=ALU.mult)
                r = dve.tt(nm, nM, e1[0:64, :], ALU.subtract, d)
                for x in four:
                    x.free = [r]
                temps.extend(four)
                yield
                yield
                b = yield from take(banks)
                for i in range(4):
                    t = pe.turn(b.ap[:, i * 64:(i + 1) * 64], fx[:, i * P:(i + 1) * P], ident[0:64, 0:64], r, b.free, signal=True)
                done["at"] = act.copy(at[:, :], b.ap[:, 0:256], t)
                b.free = [done["at"]]
                banks.append(b)
                done["rows"] = r
                spawn(bound(0, 0))

            def bound(h, r):
                n = 2 * h + r
                one_row = ident[0:64, 32 * r + h:32 * r + h + 1].broadcast_to([64, P])
                m, nk, e = nb[n % 2], nkb[n % 2], eb[n % 2]
                b = yield from take(banks)
                t = pe.mm(b.ap, one_row, nM, True, True, b.free, done["rows"], signal=True)
                a = act.copy(m.ap[:, :], b.ap, t, m.free)
                yield
                t = pe.mm(b.ap, one_row, nm, True, True, a, signal=True)
                a2 = act.act(e.ap[:, :], b.ap, ACT.Exp, t, e.free)
                b.free = [a2]
                banks.append(b)
                blocks = lambda x: x.rearrange("p (i f) -> p i f", i=4)
                d = dve.tt(blocks(nk.ap[:, :]), blocks(m.ap[:, :]), over(ge if r == 0 else le, 4), ALU.add, a, nk.free, ct)
                done["b", n] = (a, a2, d)

            def mix(h):
                need = [("q", h), ("k", h), ("v", h, 0), ("v", h, 1), "at"]
                while any(x not in done for x in need):
                    yield
                q, k, v = qb[h % 2], kb[h % 2], vb[h % 2]
                for r in range(2):
                    n = 2 * h + r
                    while ("b", n) not in done:
                        yield
                    if n < 7:
                        spawn(bound((n + 1) // 2, (n + 1) % 2))
                    a, a2, d = done["b", n]
                    m, e, nk = nb[n % 2], eb[n % 2], nkb[n % 2]
                    acc = None
                    for i, s in enumerate(range(4) if r == 0 else range(3, -1, -1)):
                        lo, hi = (s * P, T) if r == 0 else (0, (s + 1) * P)
                        b = yield from take(banks)
                        w, p = wt[i % 2], pt[i % 2]
                        t = pe.mm(b.ap[:, lo:hi], k.ap[:, s * P:(s + 1) * P], q.ap[:, lo:hi], True, True, b.free, done["q", h], done["k", h], signal=True)
                        bias = at[:, s * 64 + 32 * r + h:s * 64 + 32 * r + h + 1]
                        x = act.act(w.ap[:, s * P:(s + 1) * P], nk.ap[:, s * P:(s + 1) * P], ACT.Exp, d, done["at"], w.free, bias=bias)
                        olo, ohi = ((s + 1) * P, T) if r == 0 else (0, s * P)
                        if ohi > olo:
                            x = act.act(w.ap[:, olo:ohi], m.ap[:, olo:ohi], ACT.Exp, bias=bias)
                        y = dve.tt(p.ap[:, lo:hi], b.ap[:, lo:hi], w.ap[:, lo:hi], ALU.mult, x, t, p.free)
                        w.free = b.free = [y]
                        banks.append(b)
                        yield
                        if acc is None:
                            acc = []
                            for _ in range(3):
                                acc.append((yield from take(banks)))
                        for c in range(3):
                            l = one if c == 2 else v.ap[:, s, c * P:(c + 1) * P]
                            t = pe.mm(acc[c].ap[:, lo:hi], l, p.ap[:, lo:hi], i == 0, i == 3, y, ct, done["v", h, c % 2],
                                      acc[c].free if i == 0 else None, signal=(c == 2))
                        p.free = [t]
                    nk.free = m.free = [x]
                    if r == 1:
                        q.free = k.free = v.free = [t]
                    spawn(finish(h, r, acc, e, a2, t))
                    yield

            def finish(h, r, acc, e, a2, t):
                s1 = yield from take(temps)
                x = act.act(s1.ap, acc[2].ap, ACT.Abs, t, s1.free)
                acc[2].free = [x]
                banks.append(acc[2])
                y = dve.tt(s1.ap, s1.ap, e.ap[:, :], ALU.max, x, a2)
                e.free = [y]
                y = dve.recip(s1.ap, s1.ap, y)
                for c in range(2):
                    o = hs[:, 2 * h + c, :]
                    if r == 0:
                        y2 = dve.tt(o, acc[c].ap, s1.ap, ALU.mult, y)
                        done["h", 2 * h + c] = y2
                        acc[c].free = [y2]
                    else:
                        s = yield from take(temps)
                        y2 = dve.tt(s.ap, acc[c].ap, s1.ap, ALU.mult, y, s.free)
                        acc[c].free = [y2]
                        g = pool.tt(o, o, s.ap, ALU.add, y2, done["h", 2 * h + c])
                        s.free = [g]
                        temps.append(s)
                        done["h", 2 * h + c] = g
                s1.free = [y2]
                temps.append(s1)
                yield
                yield
                banks.extend(acc[0:2])
                if r == 0:
                    return
                yield
                b = yield from take(banks)
                w = [done["h", 2 * h], done["h", 2 * h + 1]]
                pe.mm(b.ap, mean256, hs[:, 2 * h, :], True, False, w, b.free)
                t = pe.mm(b.ap, mean256, hs[:, 2 * h + 1, :], False, True, signal=True)
                ss = []
                for c in range(2):
                    d = dve.tt(hs[:, 2 * h + c, :], hs[:, 2 * h + c, :], b.ap, ALU.subtract, t)
                    s = yield from take(temps)
                    ss.append(s)
                    a = act.act(s.ap, hs[:, 2 * h + c, :], ACT.Square, d, s.free)
                b.free = [d]
                yield
                for c in range(2):
                    t = pe.mm(b.ap, mean256, ss[c].ap, c == 0, c == 1, a, b.free, signal=True)
                s, s2 = ss
                s2.free = [t]
                temps.append(s2)
                a = act.act(s.ap, b.ap, ACT.Sqrt, t, bias=col(V_EPS))
                b.free = [a]
                banks.append(b)
                r = dve.recip(s.ap, s.ap, a)
                for c in range(2):
                    i = 2 * h + c
                    done["n", i] = dve.stt(hs[:, i, :], hs[:, i, :], col(V_MNG + i), s.ap, ALU.mult, ALU.mult, r)
                s.free = [done["n", i]]
                temps.append(s)

            def copied(b, t, dst, scale, key):
                done[key] = act.act(dst.ap[:, :], b.ap, ACT.Copy, t, dst.free, scale=scale)
                b.free = [done[key]]

            for h in range(4):
                bs = [next_bank(2), next_bank(2)]
                if h == 0:
                    tg, t = pair(*bs)
                    spawn(gates(bs[0], tg), now=True)
                    copied(bs[1], t, qb[0], 1.0, ("q", 0))
                    b = next_bank(2)
                    copied(b, project(b), kb[0], P ** -0.5, ("k", 0))
                else:
                    copied(bs[0], project(bs[0]), qb[h % 2], 1.0, ("q", h))
                    copied(bs[1], project(bs[1]), kb[h % 2], P ** -0.5, ("k", h))
                for c in range(2):
                    b = next_bank(2)
                    t = project(b)
                    v = vb[h % 2]
                    spawn(transposed(v, v.ap[:, :, c * P:(c + 1) * P], b, t, banks, temps, done, ("v", h, c)), now=True)
                if h:
                    while ("n", 2 * h - 1) not in done and len(pending) > 6:
                        tick()
                spawn(mix(h))
            for c in range(8):
                b = next_bank(2)
                t = project(b)
                a = act.act(og[:, c, :], b.ap, ACT.Sigmoid, t)
                b.free = [a]
                done["o", c] = a
                for x in range(c + 1):
                    if ("m", x) not in done and ("n", x) in done:
                        done["m", x] = pool.tt(hs[:, x, :], hs[:, x, :], og[:, x, :], ALU.mult, done["n", x], done["o", x])
            drain()
            for c in range(8):
                if ("m", c) not in done:
                    done["m", c] = dve.tt(hs[:, c, :], hs[:, c, :], og[:, c, :], ALU.mult, done["n", c], done["o", c])
                d = store_parts(c, hs[:, c, :], done["m", c], st["xused"])
            st["ticks"] = (3,)
            scope.close()
            mem_free[:] = [d, st["x"][7]]

        def window():
            fence(mem_free)
            scope = ExitStack()
            q = sb("wq", [P, 8, T], F32, scope)
            kk = sb("wk", [P, 2, T], F32, scope)
            vt = sb("wv", [P, 4, 2 * P], F32, scope)
            dist = sb("wd", [P, 3 * P], F32, scope)
            ct = table(dist[:, :], "dist")
            sx = [Buf(sb(f"ws{i}", [P, 2, 3 * P], F32, scope)) for i in range(2)]
            pp = [Buf(sb(f"wp{i}", [P, 2, 3 * P], F32, scope)) for i in range(2)]
            pt = [Buf(sb(f"wt{i}", [P, 2, 3 * P], F32, scope)) for i in range(2)]
            nsink = sb("wns", [P, 16], F32, scope)
            small = [Buf(sb(f"wm{i}", [P, 16], F32, scope)) for i in range(2)]
            ns = dve.ts(nsink[:, :], col(V_SINK, 16), -1.0, ALU.mult, s2=1.0, op1=ALU.mult)
            bs = [next_bank(), next_bank()]
            ts = pair(*bs)
            for c in range(2):
                bs[c].free = [act.copy(kk[:, c, :], bs[c].ap, ts[c])]
            for c in range(2):
                b = next_bank()
                t = project(b)
                s = tmp[c % 2]
                a = act.copy(s.ap, b.ap, t, s.free)
                b.free = [a]
                t, d = to_tokens(vt[:, :, c * P:(c + 1) * P], s.ap, bank[4 + c % 2], a)
                s.free = [t]
            for c in range(8):
                b = next_bank()
                t = project(b)
                a = act.act(q[:, c, :], b.ap, ACT.Copy, t, scale=0.125)
                b.free = [a]
            pe.wait([a, d])
            dve.wait([ct, ns])
            units = [(t, i) for t in range(8) for i in range(4)]
            stage = {}

            def first(n):
                t, i = units[n]
                j0, j1 = max(0, i - 1), min(3, i + 1)
                for g in range(2):
                    b = bank[2 * (n % 2) + g]
                    x = pe.mm(b.ap[:, 0:(j1 - j0 + 1) * P], q[64 * g:64 * g + 64, t, i * P:(i + 1) * P],
                              kk[64 * g:64 * g + 64, t // 4, j0 * P:(j1 + 1) * P], True, True, b.free, signal=True)
                stage[n] = x

            def second(n):
                t, i = units[n]
                j0, j1 = max(0, i - 1), min(3, i + 1)
                w = (j1 - j0 + 1) * P
                at = (j0 - i + 1) * P
                s, p, m = sx[n % 2], pp[n % 2], small[n % 2]
                for g in range(2):
                    slope = float(np.float32(2.0 ** (-8.0 * (WIN_ORDER[2 * t + g] + 1) / 16)))
                    b = bank[2 * (n % 2) + g]
                    d = dve.stt(s.ap[:, g, 0:w], dist[:, at:at + w], -slope, b.ap[:, 0:w], ALU.mult, ALU.add, stage[n], s.free)
                    b.free = [d]
                nm, sums, es = m.ap[:, 0:2], m.ap[:, 2:4], m.ap[:, 4:6]
                d = dve.maxneg(nm, s.ap[:, :, 0:w], d, m.free)
                d = dve.tt(nm, nm, nsink[:, 2 * t:2 * t + 2], ALU.min, d)
                d2 = dve.tt(es, nm, col(V_SINK + 2 * t, 2), ALU.add, d)
                for g in range(2):
                    a = act.act(p.ap[:, g, 0:w], s.ap[:, g, 0:w], ACT.Exp, d, p.free, bias=nm[:, g:g + 1], total=sums[:, g:g + 1])
                s.free = [a]
                a = act.act(es, es, ACT.Exp, d2)
                d = dve.tt(sums, sums, es, ALU.add, a)
                d = dve.recip(sums, sums, d)
                for g in range(2):
                    d2 = dve.ts(p.ap[:, g, 0:w], p.ap[:, g, 0:w], sums[:, g:g + 1], ALU.mult, d, s2=1.0, op1=ALU.mult)
                m.free = [d2]
                stage[n] = d2

            def third(n):
                t, i = units[n]
                nk = min(3, i + 1) - max(0, i - 1) + 1
                p, y = pp[n % 2], pt[n % 2]
                for g in range(2):
                    b = bank[4 + g]
                    for j in range(nk):
                        x = pe.turn(b.ap[:, j * P:(j + 1) * P], p.ap[:, g, j * P:(j + 1) * P], ident, stage[n], b.free, signal=(j == nk - 1))
                    if g:
                        z = dve.copy(y.ap[:, g, 0:nk * P], b.ap[:, 0:nk * P], x, y.free)
                    else:
                        z = act.copy(y.ap[:, g, 0:nk * P], b.ap[:, 0:nk * P], x, y.free)
                    b.free = [z]
                    stage[n, g] = z
                p.free = [x]

            def fourth(n):
                t, i = units[n]
                j0, j1 = max(0, i - 1), min(3, i + 1)
                b, y = bank[6 + t % 2], pt[n % 2]
                for g in range(2):
                    for j in range(j0, j1 + 1):
                        at = (t // 4) * P + 64 * g
                        x = pe.mm(b.ap[64 * g:64 * g + 64, i * P:(i + 1) * P], vt[:, j, at:at + 64],
                                  y.ap[:, g, (j - j0) * P:(j - j0 + 1) * P], j == j0, j == j1, stage[n, g],
                                  b.free, signal=(g == 1 and j == j1))
                y.free = [x]
                if i == 3:
                    b.free = [store_parts(t, b.ap, x, st["xused"])]
                    b.free += st["x"][t]

            for n in range(len(units) + 3):
                if n < len(units):
                    first(n)
                    second(n)
                if 0 <= n - 1 < len(units):
                    third(n - 1)
                if 0 <= n - 2 < len(units):
                    fourth(n - 2)
            scope.close()
            mem_free[:] = b.free

        class Hgrn:
            def __init__(self, l, hres, scope, banks, temps):
                self.l, self.hres, self.banks, self.temps = l, hres, banks, temps

                def bufs(name, n, shape):
                    return [Buf(sb(f"h{name}{l}{i}", shape, F32, scope)) for i in range(n)]

                self.q, self.k, self.b = bufs("q", 2, [P, T]), bufs("k", 2, [P, T]), bufs("b", 2, [P, T])
                self.v = bufs("v", 2, [P, 4, P])
                self.x, self.qe, self.ke = bufs("x", 3, [P, T]), bufs("qe", 2, [P, T]), bufs("ke", 2, [P, T])
                self.ad, self.ao = bufs("ad", 2, [P, T]), bufs("ao", 1, [P, 6 * P])
                tb = sb(f"htb{l}", [P, 6 * P + T], F32, scope)
                self.lbs = lbs = sb(f"hlb{l}", [P, 48], F32, scope)
                self.ct = table(tb[:, :], "lv16", "keep")
                self.keep = tb[:, 6 * P:]
                self.mask = {h: tb[:, i * P:(i + 1) * P].bitcast(U32) for i, h in enumerate((16, 8, 4, 2, 1))}
                self.mask[0] = ident.bitcast(U32)
                self.mean128 = tb[:, 5 * P:6 * P]
                l0, l1 = col(V_LB, 4), col(V_LB + 4, 4)
                self.c = c = [lbs[:, 4 * i:4 * i + 4] for i in range(8)]
                d = dve.tt(c[0], l0, l1, ALU.max)
                d = dve.tt(c[1], l0, c[0], ALU.subtract, d)
                d = dve.tt(c[2], l1, c[0], ALU.subtract, d)
                a = act.act(lbs[:, 4:12], lbs[:, 4:12], ACT.Exp, d)
                d = dve.tt(c[3], c[1], c[2], ALU.add, a)
                d = dve.recip(c[3], c[3], d)
                d = dve.tt(c[4], c[1], c[3], ALU.mult, d)
                d = dve.tt(c[5], c[2], c[3], ALU.mult, d)
                d = dve.tt(c[5], c[4], c[5], ALU.add, d)
                d = dve.tt(c[6], c[4 + l], c[4], ALU.subtract, d)
                self.lb_ok = dve.ts(c[7], c[6], -1.0, ALU.mult, d, s2=1.0, op1=ALU.add)
                self.chain = [dve.fill(x.ap[:, :], 0.0) for x in self.ad]
                self.off = [None] * 4
                self.count = [0] * 4
                self.done = {}

            def project(self, h):
                q, k, bb, v = self.q[h % 2], self.k[h % 2], self.b[h % 2], self.v[h % 2]
                bs = [next_bank(2), next_bank(2)]
                ts = pair(*bs) if h == 0 else (project(bs[0]), project(bs[1]))
                b, t = bs[0], ts[0]
                a = act.act(q.ap[:, :], b.ap, ACT.Silu, t, q.free)
                self.done["q", h] = a
                b.free = [a]
                b, t = bs[1], ts[1]
                a = act.act(bb.ap[:, :], b.ap, ACT.Sigmoid, t, bb.free)
                b.free = [a]
                d = dve.ts(bb.ap[:, :], bb.ap[:, :], self.c[7][:, h:h + 1], ALU.mult, a, self.lb_ok, s2=self.c[6][:, h:h + 1], op1=ALU.add)
                self.done["k", h] = dve.ts(k.ap[:, :], bb.ap[:, :], -1.0, ALU.mult, d, k.free, s2=1.0, op1=ALU.add)
                b = next_bank(2)
                t = project(b)
                a = act.act(bb.ap[:, :], bb.ap[:, :], ACT.Ln, self.done["k", h])
                self.done["b", h] = dve.scan(bb.ap[:, :], self.keep, bb.ap[:, :], ALU.mult, ALU.add, a, self.ct)
                spawn(transposed(v, v.ap[:, :, :], b, t, self.banks, self.temps, self.done, ("v", h)), now=True)
                b = next_bank(2)
                t = project(b)
                self.done["g", h] = act.act(self.hres[:, h, :], b.ap, ACT.Silu, t)
                b.free = [self.done["g", h]]
                spawn(self.mix(h))

            def mix(self, h):
                for half in (64, 32, 16, 8, 4, 2, 1):
                    x = yield from take(self.x)
                    spawn(self.level(h, half, x))
                    yield
                spawn(self.level(h, 0, None))
                yield
                x = yield from take(self.x)
                x2 = yield from take(self.x)
                spawn(self.between(h, x, x2))
                while self.count[h] < 9 or ("v", h) not in self.done:
                    yield
                spawn(self.values(h))

            def level(self, h, half, x):
                v = lambda y: y.rearrange("p (i f) -> p i f", f=2 * half)
                v4 = lambda y: y.rearrange("p (i f) -> p i f", f=P)
                bh, q, k = self.b[h % 2], self.q[h % 2], self.k[h % 2]
                pd = self.ad[h % 2]
                if half:
                    d = dve.tt(v(x.ap[:, :]), v(bh.ap[:, :]), along(v(bh.ap[:, :])[:, :, half - 1], 2 * half), ALU.subtract, self.done["b", h], x.free)
                    act.act(v(x.ap[:, :])[:, :, 0:half], v(x.ap[:, :])[:, :, 0:half], ACT.Exp, d, scale=-1.0)
                    a = act.act(v(x.ap[:, :])[:, :, half:], v(x.ap[:, :])[:, :, half:], ACT.Exp)
                    yield
                    qq = yield from take(self.qe)
                    ek = yield from take(self.ke)
                    d1 = dve.tt(qq.ap[:, :], q.ap[:, :], x.ap[:, :], ALU.mult, a, self.done["q", h], qq.free)
                    d2 = pool.tt(ek.ap[:, :], k.ap[:, :], x.ap[:, :], ALU.mult, a, self.done["k", h], ek.free)
                    x.free = [d1, d2]
                    self.x.append(x)
                    kx, qx, w = ek.ap, qq.ap, [d1, d2]
                else:
                    kx, qx, w = k.ap, q.ap, [self.done["q", h], self.done["k", h]]
                yield
                pb = yield from take(self.banks)
                if half >= 32:
                    for i in range(T // (2 * half)):
                        lo = 2 * half * i
                        r = lo % P
                        t = pe.mm(pb.ap[r:r + half, lo + half:lo + 2 * half], kx[:, lo:lo + half], qx[:, lo + half:lo + 2 * half],
                                  True, True, w, pb.free, signal=True)
                else:
                    for i in range(4):
                        t = pe.mm(pb.ap[:, i * P:(i + 1) * P], kx[:, i * P:(i + 1) * P], qx[:, i * P:(i + 1) * P],
                                  True, True, w, pb.free, signal=(i == 3))
                if half:
                    qq.free = ek.free = [t]
                    self.qe.append(qq)
                    self.ke.append(ek)
                yield
                free = pd.free if self.count[h] == 0 else None
                if half >= 32:
                    for r in range(0, P, 2 * half):
                        y = dve.copy(v4(pd.ap[:, :])[r:r + half, :, r + half:r + 2 * half], v4(pb.ap)[r:r + half, :, r + half:r + 2 * half],
                                     t, free, self.chain[h % 2])
                        self.chain[h % 2] = y
                else:
                    y = dve.pick(v4(pd.ap[:, :]), over(self.mask[half], 4), v4(pb.ap), t, free, self.chain[h % 2], self.ct)
                    self.chain[h % 2] = y
                pb.free = [y]
                self.banks.append(pb)
                self.count[h] += 1

            def between(self, h, x, x2):
                v4 = lambda y: y.rearrange("p (i f) -> p i f", f=P)
                bh, q, k, po, lbs = self.b[h % 2], self.q[h % 2], self.k[h % 2], self.ao[0], self.lbs
                ends = v4(bh.ap[:, :])[:, 0:3, P - 1]
                d = dve.tt(v4(x.ap[:, :])[:, 0:3, :], along(ends, P), v4(bh.ap[:, :])[:, 0:3, :], ALU.subtract, x.free, self.done["b", h])
                a0 = act.act(x.ap[:, 0:384], x.ap[:, 0:384], ACT.Exp, d)
                act.act(x2.ap[:, 0:384], bh.ap[:, P:T], ACT.Exp, x2.free, self.done["b", h])
                a = act.act(lbs[:, 32:35], ends, ACT.Exp, self.done.get("lbs"))
                yield
                qq = yield from take(self.qe)
                ek = yield from take(self.ke)
                d1 = pool.tt(ek.ap[:, 0:384], k.ap[:, 0:384], x.ap[:, 0:384], ALU.mult, a0, ek.free)
                d2 = dve.tt(qq.ap[:, 0:384], q.ap[:, P:T], x2.ap[:, 0:384], ALU.mult, a, qq.free)
                d3 = pool.ts(ek.ap[:, 384:T], ek.ap[:, 0:P], lbs[:, 33:34], ALU.mult, d1, a, s2=1.0, op1=ALU.mult)
                d4 = dve.ts(qq.ap[:, 384:T], qq.ap[:, 256:384], lbs[:, 34:35], ALU.mult, d2, s2=1.0, op1=ALU.mult)
                x.free = x2.free = [d3, d4]
                self.x += [x, x2]
                self.done["lbs"] = [d3, d4]
                yield
                b0 = yield from take(self.banks)
                b1 = yield from take(self.banks)
                K = lambda i: ek.ap[:, i * P:(i + 1) * P]
                Q = lambda i: qq.ap[:, i * P:(i + 1) * P]
                pairs = [(0, 0, K(0), Q(0)), (0, 1, K(3), Q(1)), (0, 2, K(3), Q(3)), (1, 0, K(1), Q(1)), (1, 1, K(1), Q(3)), (1, 2, K(2), Q(2))]
                for bi, at, kx, qx in pairs:
                    o = (b0, b1)[bi]
                    t = pe.mm(o.ap[:, at * P:(at + 1) * P], kx, qx, True, True, d3, d4, o.free, signal=True)
                qq.free = ek.free = [t]
                self.qe.append(qq)
                self.ke.append(ek)
                yield
                y1 = act.copy(po.ap[:, 0:384], b0.ap[:, 0:384], t, po.free)
                self.off[h] = act.copy(po.ap[:, 384:768], b1.ap[:, 0:384], t)
                b0.free, b1.free = [y1], [self.off[h]]
                self.banks += [b0, b1]
                self.count[h] += 1

            def values(self, h):
                pd, po, vt = self.ad[h % 2], self.ao[0], self.v[h % 2]
                ob = yield from take(self.banks)
                off = {0: (0, 384), 1: (384, 640), 2: (640, 768)}
                w = [self.chain[h % 2], self.off[h], self.done["v", h]]
                for j in range(4):
                    v = vt.ap[:, j, :]
                    t = pe.mm(ob.ap[:, j * P:(j + 1) * P], v, pd.ap[:, j * P:(j + 1) * P], j == 0, j == 3, w, ob.free, signal=True)
                    if j < 3:
                        t = pe.mm(ob.ap[:, (j + 1) * P:T], v, po.ap[:, off[j][0]:off[j][1]], False, False, signal=True)
                for x in (pd, po, vt, self.q[h % 2], self.k[h % 2], self.b[h % 2]):
                    x.free = [t]
                self.b[h % 2].free = self.q[h % 2].free = self.k[h % 2].free = [t, self.done["lbs"]]
                yield
                s = yield from take(self.temps)
                r = yield from take(self.temps)
                a = act.act(s.ap, ob.ap, ACT.Square, t, s.free)
                yield
                mb = yield from take(self.banks)
                t2 = pe.mm(mb.ap, self.mean128, s.ap, True, True, a, mb.free, self.ct, signal=True)
                yield
                a = act.act(r.ap, mb.ap, ACT.Sqrt, t2, r.free, bias=col(V_EPS + 1))
                mb.free = [a]
                self.banks.append(mb)
                d = dve.recip(r.ap, r.ap, a)
                d = dve.tt(s.ap, ob.ap, r.ap, ALU.mult, d, t2)
                ob.free = [d]
                self.banks.append(ob)
                r.free = [d]
                d = dve.stt(self.hres[:, h, :], s.ap, col(V_HGN + self.l), self.hres[:, h, :], ALU.mult, ALU.mult, d, self.done["g", h])
                s.free = [d]
                self.temps += [r, s]
                self.done["o", h] = d

        def transposed(dbuf, dst, b, t, banks, temps, done, key):
            s = yield from take(temps)
            a = act.copy(s.ap, b.ap, t, s.free)
            b.free = [a]
            yield
            pb = yield from take(banks)
            for i in range(4):
                t = pe.turn(pb.ap[:, i * P:(i + 1) * P], s.ap[:, i * P:(i + 1) * P], ident, a, pb.free, signal=(i == 3))
            s.free = [t]
            temps.append(s)
            yield
            c = dve.copy(dst, pb.ap.rearrange("p (i f) -> p i f", i=4), t, dbuf.free)
            pb.free = [c]
            banks.append(pb)
            done[key] = c

        class Attention:
            def __init__(self, l, scope, banks, temps):
                self.l, self.banks, self.temps = l, banks, temps
                self.q = sb(f"nq{l}", [P, 4, T], F32, scope)
                self.ks = sb(f"nk{l}", [P, 2, T], F32, scope)
                self.vt = sb(f"nv{l}", [P, 2, 4, P], F32, scope)
                self.cc = sb(f"nc{l}", [P, 2, T], F32, scope)
                tb = sb(f"ntb{l}", [P, 5 * P + 2 * T], F32, scope)
                self.mats = sb(f"nm{l}", [P, 2, 160], F32, scope)
                self.xx = sb(f"nx{l}", [P, 16, 62], F32, scope)
                self.xxh = sb(f"nxh{l}", [P, 16, 62], F32R, scope)
                self.xxl = sb(f"nxl{l}", [P, 16, 62], F32R, scope)
                self.hid = sb(f"nh{l}", [P, 2, 62], F32, scope)
                self.kc = sb(f"nkc{l}", [P, 32], F32, scope)
                self.vcm = sb(f"nvc{l}", [32, P], F32, scope)
                self.gt = sb(f"ng{l}", [P, 4, 24], F32, scope)
                self.st1 = sb(f"ns{l}", [P, 80], F32, scope)
                self.le, self.rotm, self.mean64, self.cneg, self.cone = (tb[:, i * P:(i + 1) * P] for i in range(5))
                self.ct = [table(tb[:, :], "le", "sin"), load(self.mats[:, :, :], mats_in[l].rearrange("c p n -> p c n"))]
                self.cos, self.sin = tb[:, 5 * P:5 * P + T], tb[:, 5 * P + T:]
                self.qg = dve.ts(self.st1[:, 0:1], col(V_QG + l), 0.125, ALU.mult, s2=1.0, op1=ALU.mult)
                self.done = {}

            def head_norm(self, dst, src, gain, c, s, n, t, b, home, key):
                s0 = yield from take(self.temps)
                s1 = yield from take(self.temps)
                a = act.act(s0.ap[:, 0:n], src, ACT.Square, t, s0.free)
                yield
                b2 = yield from take(self.banks)
                m = pe.mm(b2.ap[:, 0:n], self.mean64, s0.ap[:, 0:n], True, True, a, b2.free, self.ct, signal=True)
                yield
                a = act.act(s1.ap[:, 0:n], b2.ap[:, 0:n], ACT.Sqrt, m, s1.free, bias=col(V_EPS + 1))
                b2.free = [a]
                self.banks.append(b2)
                d = dve.recip(s1.ap[:, 0:n], s1.ap[:, 0:n], a)
                d = dve.stt(s0.ap[:, 0:n], src, gain, s1.ap[:, 0:n], ALU.mult, ALU.mult, d, m, self.qg)
                b.free = [d]
                if home is not None:
                    home.append(b)
                yield
                b3 = yield from take(self.banks)
                m = pe.mm(b3.ap[:, 0:n], self.rotm, s0.ap[:, 0:n], True, True, d, b3.free, signal=True)
                d1 = pool.tt(dst, s0.ap[:, 0:n], c, ALU.mult, d, self.ct)
                yield
                d2 = dve.tt(s1.ap[:, 0:n], b3.ap[:, 0:n], s, ALU.mult, m, self.ct)
                b3.free = [d2]
                self.banks.append(b3)
                d = dve.tt(dst, dst, s1.ap[:, 0:n], ALU.add, d1, d2)
                s0.free = s1.free = [d]
                self.temps += [s0, s1]
                self.done[key] = d

            def compress(self, c):
                while ("cfree", c) not in self.done:
                    yield
                used = self.done["cfree", c]
                d = self.done["c", c]
                for g in range(2):
                    rg = slice(64 * g, 64 * g + 64)
                    src = self.cc[rg, c, :].rearrange("p (n c) -> p c n", c=16)
                    pos = self.mats[rg, c, 0:32]
                    for par in range(2):
                        for up in range(2):
                            o = self.xx[64 * par:64 * par + 64, 8 * up:8 * up + 8, 31 * g:31 * g + 31]
                            y = dve.tt(o, src[:, par::2, up:up + 31], along(pos[:, 16 * up + par:16 * up + 16:2], 31), ALU.add, d, used, self.ct)
                    yield
                a = act.copy(self.xxh[:, :, :], self.xx[:, :, :], y, used)
                y = dve.tt(self.xxl[:, :, :], self.xx[:, :, :], f32(self.xxh[:, :, :]), ALU.subtract, a, used)
                self.done["x", c] = [a, y]

            def plain(self, c):
                b = next_bank(2)
                t = project(b)
                self.done["c", c] = act.copy(self.cc[:, c, :], b.ap, t)
                b.free = [self.done["c", c]]

            def key(self, c):
                b = next_bank(2)
                t = project(b)
                spawn(self.freed(b, self.ks[:, c, :], col(V_KG + 4 * self.l + 1 + c), t, ("k", c)), now=True)

            def query(self, c):
                b = next_bank(2)
                t = project(b)
                spawn(self.freed(b, self.q[:, c, :], self.st1[:, 0:1], t, ("q", c)), now=True)

            def freed(self, b, dst, gain, t, key):
                s = yield from take(self.temps)
                a = act.copy(s.ap, b.ap, t, s.free)
                b.free = [a]
                yield from self.head_norm(dst, s.ap, gain, self.cos, self.sin, T, a, s, self.temps, key)

            def value(self, c):
                b = next_bank(2)
                t = project(b)
                spawn(transposed(Buf(None), self.vt[:, c, :, :], b, t, self.banks, self.temps, self.done, ("v", c)), now=True)

            def gates(self):
                b = next_bank(2)
                t = project(b)
                spawn(self.gate_task(b, t), now=True)

            def gate_task(self, b, t):
                s = yield from take(self.temps)
                a = act.act(s.ap[0:32, :], b.ap[0:32, :], ACT.Sigmoid, t, s.free)
                b.free = [a]
                yield
                pb = yield from take(self.banks)
                for i in range(4):
                    t = pe.turn(pb.ap[:, i * 32:(i + 1) * 32], s.ap[0:32, i * P:(i + 1) * P], ident[0:32, 0:32], a, pb.free, signal=(i == 3))
                s.free = [t]
                self.temps.append(s)
                yield
                self.done["gt"] = dve.copy(self.gt[:, :, :], pb.ap[:, 0:P].rearrange("p (i f) -> p i f", f=32)[:, :, 0:24], t)
                pb.free = [self.done["gt"]]
                self.banks.append(pb)

            def hidden(self, c):
                while ("x", c) not in self.done:
                    tick()
                w = self.done["x", c]
                h = None
                for hh in range(2):
                    b = next_bank(2)
                    t = gemm(16, lambda k: self.xxh[:, k, :], lambda k: self.xxl[:, k, :], b.ap[:, 0:62], lambda k: w, b.free)
                    h = act.act(self.hid[:, hh, :], b.ap[:, 0:62], ACT.Silu, t, self.done.get("hid"))
                    b.free = [h]
                    tick()
                self.done["cfree", 1] = t
                spawn(self.second_layer(c, h))

            def second_layer(self, c, h):
                yield
                b = yield from take(self.banks)
                w2 = self.mats[:, c, 32:160].rearrange("p (h f) -> p h f", h=2)
                for g in range(2):
                    for hh in range(2):
                        t = pe.mm(b.ap[64 * g:64 * g + 64, 0:31], w2[:, hh, :], self.hid[:, hh, 31 * g:31 * g + 31], hh == 0, hh == 1, h, b.free, self.ct, signal=True)
                self.done["hid"] = t
                if c == 0:
                    yield from self.head_norm(self.kc[:, 0:31], b.ap[:, 0:31], col(V_KG + 4 * self.l), self.cos[:, 31::16], self.sin[:, 31::16], 31, t, b, self.banks, "kc")
                    return
                yield
                s = yield from take(self.temps)
                a = act.copy(s.ap[:, 0:31], b.ap[:, 0:31], t, s.free)
                b.free = [a]
                self.banks.append(b)
                yield
                b = yield from take(self.banks)
                t = pe.turn(b.ap[0:31, 0:P], s.ap[:, 0:31], ident, a, b.free, signal=True)
                s.free = [t]
                self.temps.append(s)
                yield
                self.done["vcm"] = dve.copy(self.vcm[0:31, :], b.ap[0:31, 0:P], t)
                b.free = [self.done["vcm"]]
                self.banks.append(b)

        def attend(o, scope):
            l, q, ks, vt, kc, vcm, gt, st1, le, cneg, cone = o.l, o.q, o.ks, o.vt, o.kc, o.vcm, o.gt, o.st1, o.le, o.cneg, o.cone
            pc = sb(f"npc{l}", [P, 32, 31], F32, scope)
            pct = sb(f"npt{l}", [32, 32, P], F32, scope)
            pp = [Buf(sb(f"np{l}{i}", [P, 2, T], F32, scope)) for i in range(2)]
            pt = [Buf(sb(f"nt{l}{i}", [P, 2, T], F32, scope)) for i in range(2)]
            small = [Buf(sb(f"nsm{l}{i}", [P, 16], F32, scope)) for i in range(2)]
            gt_ok = o.done["gt"]

            nmx, sm = st1[:, 8:40], st1[:, 40:72]
            for hf in range(2):
                b = bank[hf]
                rg = slice(64 * hf, 64 * hf + 64)
                for t in range(4):
                    for i in range(4):
                        at = 4 * t + i
                        x = pe.mm(b.ap[:, 32 * at:32 * at + 31], q[rg, t, i * P:(i + 1) * P], kc[rg, 0:31], True, True, b.free, signal=True)
                p3 = pc[:, 16 * hf:16 * hf + 16, :]
                s3 = b.ap.rearrange("p (u n) -> p u n", n=32)[:, :, 0:31]
                cn = cneg.rearrange("p (i n) -> p i n", n=32)[:, :, 0:31]
                for u in range(4):
                    y = dve.tt(p3[:, 4 * u:4 * u + 4, :], s3[:, 4 * u:4 * u + 4, :], cn, ALU.add, x)
                b.free = [y]
                m, s = nmx[:, 16 * hf:16 * hf + 16], sm[:, 16 * hf:16 * hf + 16]
                y = dve.maxneg(m, p3, y)
                y = dve.tt(p3, p3, along(m, 31), ALU.add, y)
                a = act.act(p3, p3, ACT.Exp, y)
                y = dve.put(lambda e, s=s, p3=p3: e.tensor_reduce(s, p3, AX, ALU.add), [a])
                y = dve.recip(s, s, y)
                for u in range(4):
                    head = 4 * hf + u
                    w = dve.tt(s[:, 4 * u:4 * u + 4], s[:, 4 * u:4 * u + 4], gt[:, :, 3 * head], ALU.mult, y, gt_ok)
                y = dve.tt(p3, p3, along(s, 31), ALU.mult, w)
                c1 = cone.rearrange("p (i n) -> p i n", n=32)[:, :, 0:31]
                for u in range(4):
                    y2 = dve.tt(p3[:, 4 * u:4 * u + 4, :], p3[:, 4 * u:4 * u + 4, :], c1, ALU.mult, y)
                for u in range(4):
                    b = bank[4 + u]
                    for i in range(4):
                        x = pe.turn(b.ap[0:31, i * P:(i + 1) * P], p3[:, 4 * u + i, :], ident, y2, b.free, signal=True)
                    z = act.copy(pct[0:31, 16 * hf + 4 * u:16 * hf + 4 * u + 4, :], b.ap[0:31, :].rearrange("p (i f) -> p i f", i=4), x)
                    b.free = [z]
            pe.wait([z])
            units = [(t, g, i) for t in range(4) for i in range(4) for g in range(2)]
            stage = {}

            def first(n):
                t, g, i = units[n]
                for br in range(2):
                    b = bank[2 * (n % 2) + br]
                    stage[n] = pe.mm(b.ap[:, 0:(i + 1) * P], q[64 * g:64 * g + 64, t, i * P:(i + 1) * P],
                                     ks[64 * g:64 * g + 64, br, 0:(i + 1) * P], True, True, b.free, signal=True)

            def second(n):
                t, g, i = units[n]
                head = t + 4 * g
                w = (i + 1) * P
                two = ps[:, 2 * (n % 2):2 * (n % 2) + 2, :]
                pair = (bank[2 * (n % 2)], bank[2 * (n % 2) + 1])
                p, m = pp[n % 2], small[n % 2]
                nm, sums = m.ap[:, 0:2], m.ap[:, 2:4]
                d = dve.tt(two[:, :, i * P:w], two[:, :, i * P:w], over(le, 2), ALU.add, stage[n])
                d = dve.maxneg(nm, two[:, :, 0:w], d, m.free)
                for br in range(2):
                    a = act.act(p.ap[:, br, 0:w], two[:, br, 0:w], ACT.Exp, d, p.free, bias=nm[:, br:br + 1], total=sums[:, br:br + 1])
                for b in pair:
                    b.free = [a]
                d = dve.recip(sums, sums, a)
                d = dve.tt(sums, sums, gt[:, i, 3 * head + 1:3 * head + 3], ALU.mult, d)
                for br in range(2):
                    d2 = dve.ts(p.ap[:, br, 0:w], p.ap[:, br, 0:w], sums[:, br:br + 1], ALU.mult, d, s2=1.0, op1=ALU.mult)
                m.free = [d2]
                stage[n] = d2

            def third(n):
                t, g, i = units[n]
                p, y = pp[n % 2], pt[n % 2]
                for br in range(2):
                    b = bank[4 + br]
                    for j in range(i + 1):
                        x = pe.turn(b.ap[:, j * P:(j + 1) * P], p.ap[:, br, j * P:(j + 1) * P], ident, stage[n], b.free, signal=(j == i))
                    w = (i + 1) * P
                    z = (dve if br else act).copy(y.ap[:, br, 0:w], b.ap[:, 0:w], x, y.free)
                    b.free = [z]
                    stage[n, br] = z
                p.free = [x]

            def fourth(n):
                t, g, i = units[n]
                b, y = bank[6 + t % 2], pt[n % 2]
                o = b.ap[64 * g:64 * g + 64, i * P:(i + 1) * P]
                pe.mm(o, vcm[0:31, 64 * g:64 * g + 64], pct[0:31, 16 * g + 4 * t + i, :], True, False, b.free)
                for br in range(2):
                    for j in range(i + 1):
                        end = br == 1 and j == i
                        x = pe.mm(o, vt[:, br, j, 64 * g:64 * g + 64], y.ap[:, br, j * P:(j + 1) * P], False, end, stage[n, br], signal=end)
                y.free = [x]
                if i == 3 and g == 1:
                    b.free = [store_parts(4 + t, b.ap, x, st["xused"])]
                    b.free += st["x"][4 + t]

            for n in range(len(units) + 2):
                if n < len(units):
                    first(n)
                    second(n)
                if 0 <= n - 2:
                    fourth(n - 2)
                if 0 <= n - 1 < len(units):
                    third(n - 1)

        def nsa(l):
            fence(mem_free)
            outer = ExitStack()
            hres = sb(f"hres{l}", [P, 4, T], F32, outer)
            banks, temps = bank[2:8], tmp[0:5]
            o = Attention(l, outer, banks, temps)
            scope = ExitStack()
            hg = Hgrn(l, hres, scope, banks, temps)
            o.done["cfree", 0] = None
            st["ticks"] = (2, 5)
            hg.project(0)
            o.plain(0)
            o.plain(1)
            spawn(o.compress(0))
            o.key(0)
            o.value(0)
            hg.project(1)
            o.key(1)
            o.value(1)
            o.gates()
            o.query(0)
            hg.project(2)
            spawn(o.compress(1))
            o.query(1)
            o.query(2)
            o.query(3)
            hg.project(3)
            o.hidden(0)
            o.hidden(1)
            drain()
            st["ticks"] = (3,)
            for h in range(4):
                d = store_parts(h, hres[:, h, :], st["xused"], hg.done["o", h])
            fence()
            scope.close()
            scope = ExitStack()
            attend(o, scope)
            fence()
            scope.close()
            outer.close()


        for step in plan:
            kind, args = step[0], step[1:]
            nm = None
            if kind == "scale":
                prescale()
            elif kind == "ffn_ln":
                nm = Norm(False)
                ffn(0.5, nm)
                layer_norm(nm, args[0], args[1])
            elif kind == "ffn_rms":
                nm = Norm(True)
                ffn(1.0, nm)
                rms_norm(nm, args[0])
            elif kind == "ffn_end":
                ffn(1.0, None)
            elif kind == "rms":
                nm = Norm(True)
                for k in range(KD):
                    nm.add(k, st["xr"][k])
                rms_norm(nm, args[0])
            elif kind == "mlstm":
                mlstm()
                nm = Norm(False)
                out_proj(nm)
                layer_norm(nm, args[0], True)
            elif kind == "window":
                window()
                nm = Norm(False)
                out_proj(nm)
                layer_norm(nm, args[0], True)
            elif kind == "nsa":
                nsa(args[0])
                nm = Norm(True)
                out_proj(nm)
                rms_norm(nm, args[1])
        assert tile_n[0] == n_units * UT, (tile_n[0], n_units * UT)
        outs = out.rearrange("(k p) t -> p k t", p=P)
        for k in range(KD):
            sp.wait([st["xr"][k]])
            sp.items.append(("dma", lambda e, k=k: e.dma_start(outs[:, k, :], xr[:, k, :]), "out"))
        sp.items.append(("wait", "out", 16 * KD))

        block = ctx.enter_context(nc.Block())

        @block.sync
        def _(e):
            for kind, a, b in sp.items:
                if kind == "wait":
                    e.wait_ge(sems[a], b)
                else:
                    a(e).then_inc(sems[b], 16)

        @block.tensor
        def _(e):
            pe.play(e, sems)

        @block.vector
        def _(e):
            dve.play(e, sems)

        @block.scalar
        def _(e):
            act.play(e, sems)

        @block.gpsimd
        def _(e):
            pool.play(e, sems)


PLAN = [("scale",), ("ffn_ln", 0, True), ("mlstm", 1), ("ffn_ln", 2, True), ("ffn_ln", 3, True), ("window", 4),
        ("ffn_ln", 5, False), ("rms", V_NM), ("nsa", 0, V_NF), ("ffn_rms", V_NM + 8), ("nsa", 1, V_NF + 8), ("ffn_end",)]


def columns(w, cols=None):
    w = np.asarray(w)
    if cols is None:
        cols = np.arange(w.shape[1])
    cols = np.asarray(cols)
    picked = w[:, np.maximum(cols, 0)]
    if (cols < 0).any():
        picked[:, cols < 0] = 0
    k, n = picked.shape
    return picked.reshape(k // P, P, n // P, P).transpose(2, 0, 1, 3).reshape(-1, P, P)


def head_pairs(order, dim=64):
    return np.concatenate([np.arange(h * dim, (h + 1) * dim) for h in order])


WIN_ORDER = [h for t in range(8) for h in ((t % 4) + 8 * (t // 4), (t % 4) + 4 + 8 * (t // 4))]
NSA_ORDER = [h for t in range(4) for h in (t, 4 + t)]


def stream(inp, plan):
    parts = []

    def ffn(w_in, w_out):
        w = columns(w_in).reshape(2, KF, KD, P, P)
        parts.append(w.transpose(1, 0, 2, 3, 4).reshape(-1, P, P))
        parts.append(columns(w_out))

    for step in plan:
        if step[0] == "ffn_ln":
            l, j = {0: (0, 0), 2: (0, 1), 3: (1, 0), 5: (1, 1)}[step[1]]
            ffn(inp["ffn_w_in"][l, j], inp["ffn_w_out"][l, j])
        elif step[0] in ("ffn_rms", "ffn_end"):
            l = 0 if step[0] == "ffn_rms" else 1
            ffn(inp["w_ffn_in_2"][l], inp["w_ffn_out_2"][l])
        elif step[0] == "mlstm":
            w = inp["ml_w_in"][0]
            g = np.full(P, -1)
            for q, at in enumerate((0, 64, 32, 96)):
                g[at:at + 4] = 3072 + 4 * q + np.arange(4)
            cols = [g]
            for h in range(4):
                cols += [P * h + np.arange(P), 512 + P * h + np.arange(P), 1024 + 2 * P * h + np.arange(2 * P)]
            parts.append(columns(w, np.concatenate(cols + [np.arange(2048, 3072)])))
            parts.append(columns(inp["ml_w_out"][0]))
        elif step[0] == "window":
            order = head_pairs(WIN_ORDER)
            parts.append(columns(inp["at_w_in"][0], np.concatenate([np.arange(1024, 1536), order])))
            parts.append(columns(inp["at_w_out"][0][order, :]))
        elif step[0] == "nsa":
            l = step[1]
            w = inp["w_in_2"][l]
            gate = np.full(P, -1)
            gate[:24] = 2048 + 512 + 768 + np.arange(24)
            order = head_pairs(NSA_ORDER)
            heads = [np.concatenate([np.arange(512 * i + P * h, 512 * i + P * h + P) for i in range(4)]) for h in range(4)]
            ck, cv, k0, v0, k1, v1 = (np.arange(2560 + P * i, 2560 + P * i + P) for i in range(6))
            q = (2048 + order).reshape(4, P)
            cols = [heads[0], ck, cv, k0, v0, heads[1], k1, v1, gate, q[0], heads[2], q[1], q[2], q[3], heads[3]]
            parts.append(columns(w, np.concatenate(cols)))
            parts.append(columns(inp["cmp_w1_k_2"][l]))
            parts.append(columns(inp["cmp_w1_v_2"][l]))
            rows = np.concatenate([np.arange(512), 512 + order])
            parts.append(columns(inp["w_out_2"][l][rows, :]))
    w = np.concatenate(parts)
    return np.ascontiguousarray(w.reshape(-1, UT, P, P).transpose(0, 2, 1, 3)).reshape(-1, P, UT * P)


def vectors(inp):
    v = np.zeros((P, V_N), np.float32)

    def put(at, a):
        a = np.asarray(a).reshape(-1, P)
        v[:, at:at + a.shape[0]] = a.T

    put(V_LNG, inp["ln_g"])
    put(V_LNB, inp["ln_b"])
    v[:, V_EPS] = LN_EPS
    v[:, V_EPS + 1] = RMS_EPS
    for q, at in enumerate((0, 64, 32, 96)):
        v[at:at + 4, V_GB] = inp["ml_gate_b"][0][4 * q:4 * q + 4]
    put(V_MNG, inp["ml_norm_g"])
    v[:, V_SINK:V_SINK + 16] = inp["at_sink"][0][WIN_ORDER][None, :]
    for l in range(2):
        put(V_LB + 4 * l, inp["hg_lb_logits_2"][l])
        v[:, V_HGN + l] = inp["hg_gnorm_2"][l]
        v[:, V_QG + l] = np.tile(inp["q_gain_2"][l], 2)
        for b in range(3):
            v[:, V_KG + 4 * l + b] = np.tile(inp["k_gain_2"][l, b], 2)
    put(V_NM, inp["norm_mix_2"])
    put(V_NF, inp["norm_ffn_2"])
    return v


def small_mats(inp):
    m = np.zeros((2, 2, P, 32 + 128), np.float32)
    for l in range(2):
        for i, n in enumerate("kv"):
            m[l, i, :, :32] = np.tile(inp[f"cmp_pe_{n}_2"][l].T, (2, 1))
            m[l, i, :, 32:] = inp[f"cmp_w2_{n}_2"][l].reshape(2, P, 64).transpose(1, 0, 2).reshape(P, 128)
    return m


def arrange(inp, plan, x):
    t = lay_tables()
    return {
        "in_x": np.ascontiguousarray(np.asarray(x).reshape(T, D).T),
        "in_w": stream(inp, plan),
        "in_vec": vectors(inp),
        "in_tab": np.concatenate([t[k] for k in SPANS], axis=1),
        "in_mat": small_mats(inp),
    }


def kernel(**inputs):
    import numpy as _np
    import concourse.bacc as _bacc
    from concourse import mybir as _mybir
    from concourse.bass_utils import run_bass_kernel_spmd as _run

    inp = {k: _np.asarray(v) for k, v in inputs.items()}
    arrays = arrange(inp, PLAN, inp["x"])
    nc = _bacc.Bacc("TRN2", target_bir_lowering=False, num_devices=1)
    args = [nc.dram_tensor(k, a.shape, _mybir.dt.float32, kind="ExternalInput").ap() for k, a in arrays.items()]
    args.append(nc.dram_tensor("out_0", [D, T], _mybir.dt.float32, kind="ExternalOutput").ap())
    build(nc, *args, PLAN)
    r = _run(nc, [arrays], core_ids=[0])
    return _np.ascontiguousarray(r.results[0]["out_0"].T).reshape(1, T, D)
```

```python
from contextlib import ExitStack

import numpy as np

import concourse.bass as bass
from concourse import mybir

P = 128
T = 512
D = 1024
KD = D // P
FF = 2816
KF = FF // P
ALPHA = 4 ** 0.25
LN_EPS = 1e-5
RMS_EPS = 1e-6
NEG = -1e30
UT = 8
NRAW = 5
NW = 4
NLD = 4
NC = 5
AHEAD = 2

ALU = mybir.AluOpType
ACT = mybir.ActivationFunctionType
AX = mybir.AxisListType.X
F32 = mybir.dt.float32
F32R = mybir.dt.float32r
U32 = mybir.dt.uint32

V_LNG, V_LNB = 0, 48
V_EPS = 96
V_GB = 100
V_MNG = 104
V_SINK = 112
V_LB = 128
V_HGN = 144
V_QG, V_KG = 146, 148
V_NM, V_NF = 156, 172
V_N = 192


def lay_tables():
    p = np.arange(P)[:, None]
    f = np.arange(P)[None, :]
    one = np.ones((P, P), np.float32)
    causal = np.where(f >= p, 0.0, NEG)
    acausal = np.where(f <= p, 0.0, NEG)
    t = {"ident": (p == f), "mean1024": one / 1024, "mean640": one / (NC * P)}
    for h in (16, 8, 4, 2, 1):
        t[f"lv{h}"] = (p // (2 * h) == f // (2 * h)) & (p % (2 * h) < h) & (f % (2 * h) >= h)
    t["mean128"] = one / 128
    t["keep"] = np.broadcast_to((np.arange(T) % P != 0)[None, :], (P, T))
    t["le"] = acausal
    rot = np.zeros((P, P))
    for i in range(P):
        if i % 64 < 32:
            rot[i + 32, i] = -1.0
        else:
            rot[i - 32, i] = 1.0
    t["rot"] = rot
    t["mean64"] = (p // 64 == f // 64) / 64.0
    ends = np.arange(31) * 16 + 31
    tok = np.arange(4)[None, :, None] * P + p[:, :, None]
    seen = np.zeros((P, 4, 32), bool)
    seen[:, :, :31] = ends[None, None, :] <= tok
    t["cneg"] = np.where(seen, 0.0, NEG).reshape(P, P)
    t["cone"] = seen.reshape(P, P).astype(np.float32)
    half = 32
    freqs = np.float32(10000.0) ** (-np.arange(half, dtype=np.float32) / np.float32(half))
    ang = np.arange(T, dtype=np.float32)[None, :] * freqs[np.arange(P) % half][:, None]
    t["cos"] = np.cos(ang.astype(np.float32))
    t["sin"] = np.sin(ang.astype(np.float32))
    t["mle"] = acausal
    t["mge"] = causal
    t["one"] = one
    t["mean256"] = one / 256
    kj = np.arange(3 * P)[None, :]
    rel = p - kj + P
    t["dist"] = np.where(np.abs(rel) <= P, np.abs(rel), 1e30)
    return {k: np.ascontiguousarray(v, np.float32) for k, v in t.items()}


def table_spans():
    at, spans = 0, {}
    for k, v in lay_tables().items():
        spans[k] = (at, v.shape[1])
        at += v.shape[1]
    return spans, at


SPANS, TABLE_N = table_spans()


class Queue:

    def __init__(self, sem):
        self.sem = sem
        self.n = 0
        self.items = []
        self.seen = {}

    def wait(self, waits):
        for w in waits:
            if w is None:
                continue
            if isinstance(w, (list, tuple)) and not (len(w) == 2 and isinstance(w[0], str)):
                self.wait(w)
                continue
            sem, value = w
            if self.seen.get(sem, 0) < value:
                self.seen[sem] = value
                self.items.append(("wait", sem, value))

    def put(self, fn, waits, signal=True):
        self.wait(waits)
        if not signal:
            self.items.append(("do", fn, None))
            return None
        self.n += 1
        self.items.append(("do", fn, self.sem))
        return (self.sem, self.n)

    def play(self, eng, sems):
        for kind, a, b in self.items:
            if kind == "wait":
                eng.wait_ge(sems[a], b)
            else:
                ins = a(eng)
                if b is not None:
                    ins.then_inc(sems[b], 1)


class Vec(Queue):
    def tt(self, out, a, b, op, *w):
        return self.put(lambda e: e.tensor_tensor(out, a, b, op), w)

    def ts(self, out, a, s1, op0, *w, s2=None, op1=None):
        if op1 is None:
            return self.put(lambda e: e.tensor_scalar(out, a, s1, None, op0), w)
        return self.put(lambda e: e.tensor_scalar(out, a, s1, s2, op0, op1), w)

    def stt(self, out, a, s, b, op0, op1, *w):
        return self.put(lambda e: e.scalar_tensor_tensor(out=out, in0=a, scalar=s, in1=b, op0=op0, op1=op1), w)

    def copy(self, out, a, *w):
        return self.put(lambda e: e.tensor_copy(out, a), w)

    def recip(self, out, a, *w):
        return self.put(lambda e: e.reciprocal(out, a), w)

    def scan(self, out, a, b, op0, op1, *w):
        return self.put(lambda e: e.tensor_tensor_scan(out, a, b, 0.0, op0, op1), w)

    def maxneg(self, out, a, *w):
        return self.put(lambda e: e.tensor_reduce(out, a, AX, ALU.max, negate=True), w)

    def pick(self, out, mask, a, *w):
        return self.put(lambda e: e.copy_predicated(out, mask, a), w)

    def fill(self, out, v, *w):
        return self.put(lambda e: e.memset(out, v), w)


class Act(Queue):
    def act(self, out, a, func, *w, scale=1.0, bias=0.0, total=None):
        if total is None:
            return self.put(lambda e: e.activation(out, a, func, bias=bias, scale=scale), w)
        return self.put(lambda e: e.activation(out, a, func, bias=bias, scale=scale, accum_out=total), w)

    def copy(self, out, a, *w):
        return self.put(lambda e: e.activation(out, a, ACT.Copy), w)


class Pe(Queue):
    def mm(self, out, l, r, start, stop, *w, signal=False):
        return self.put(lambda e: e.matmul(out, l, r, start=start, stop=stop), w, signal)

    def turn(self, out, a, ident, *w, signal=False):
        return self.put(lambda e: e.transpose(out, a, ident), w, signal)


class Buf:

    def __init__(self, ap):
        self.ap = ap
        self.free = []


def f32(ap):
    return ap.bitcast(F32)


def interleave(main, side, ratio):
    owed = 0.0
    for _ in main:
        owed += ratio
        while owed >= 1.0:
            owed -= 1.0
            if next(side, "end") == "end":
                owed = -1e9
    for _ in side:
        pass


def run_all(g):
    for _ in g:
        pass


def build(nc, xin, wst, vec, tab, mats_in, out, plan):
    with ExitStack() as ctx:
        def sem(name):
            return ctx.enter_context(nc.semaphore(name))

        def sb(name, shape, dt=F32, scope=ctx):
            return scope.enter_context(nc.sbuf_tensor(name, shape, dt))

        sems = {k: sem("s_" + k) for k in ("pe", "dve", "act", "pool", "out")}
        for i in range(NLD):
            sems[f"ld{i}"] = sem(f"s_ld{i}")
        for i in range(NRAW):
            sems[f"raw{i}"] = sem(f"s_raw{i}")
        pe, dve, act, pool = Pe("pe"), Vec("dve"), Act("act"), Vec("pool")
        sp = Queue("sp")

        ps = ctx.enter_context(nc.psum_tensor("ps", [P, 8, 512], F32))
        bank = [Buf(ps[:, i, :]) for i in range(8)]

        raw = [sb(f"raw{i}", [P, UT * P]) for i in range(NRAW)]
        whi = [sb(f"whi{i}", [P, UT * P], F32R) for i in range(NW)]
        wlo = [sb(f"wlo{i}", [P, UT * P], F32R) for i in range(NW)]
        xr = sb("xr", [P, KD, T])
        xh = sb("xh", [P, KD, T], F32R)
        xl = sb("xl", [P, KD, T], F32R)
        vc = sb("vc", [P, V_N])
        res = sb("res", [P, 3 * P])
        tmp = [Buf(sb(f"tmp{i}", [P, T])[:, :]) for i in range(5)]
        ident, mean1024, mean640 = (res[:, i * P:(i + 1) * P] for i in range(3))

        def table(tile, first, last=None):
            a = SPANS[first][0]
            z = sum(SPANS[last or first])
            return load(tile, tab[:, a:z])

        loads = [0]

        def load(dst, src, *w):
            i, n = loads[0] % NLD, loads[0] // NLD
            loads[0] += 1
            sp.wait([w, (f"ld{i}", 16 * n) if n else None])
            sp.items.append(("dma", lambda e: e.dma_start(dst, src), f"ld{i}"))
            return (f"ld{i}", 16 * (n + 1))

        n_units = wst.shape[0]
        unit = [0]
        prepared = [0]
        ready = {}
        spent = {}
        rawfree = {}

        def prep(u):
            if u >= n_units:
                return
            r, s = u % NRAW, u % NW
            sp.wait([rawfree.get(u - NRAW)])
            sp.items.append(("dma", lambda e: e.dma_start(raw[r][:, :], wst[u, :, :]), f"raw{r}"))
            landed = (f"raw{r}", 16 * (u // NRAW + 1))
            prepared[0] = u + 1
            return landed

        landed = {}
        fetched = [0]

        def fetch(u):
            while fetched[0] <= u and fetched[0] < n_units:
                landed[fetched[0]] = prep(fetched[0])
                fetched[0] += 1

        split_n = [0]

        def split(u):
            while split_n[0] <= u and split_n[0] < n_units:
                v = split_n[0]
                fetch(v + NRAW - 1)
                r, s = v % NRAW, v % NW
                a = act.copy(whi[s][:, :], raw[r][:, :], landed[v], spent.get(v - NW))
                d = dve.tt(wlo[s][:, :], raw[r][:, :], f32(whi[s][:, :]), ALU.subtract, landed[v], a, spent.get(v - NW))
                ready[v] = [a, d]
                rawfree[v] = d
                split_n[0] += 1

        tile_n = [0]

        def gemm(kt, hi, lo, out, waits, *w, first=True, last=True, n=None):
            tok = None
            for k in range(kt):
                u, j = divmod(tile_n[0], UT)
                need = []
                if j == 0 or k == 0:
                    split(u + AHEAD)
                    need = ready[u]
                s = u % NW
                wh, wl = whi[s][:, j * P:(j + 1) * P], wlo[s][:, j * P:(j + 1) * P]
                a = first and k == 0
                b = last and k == kt - 1
                pe.mm(out, wh, hi(k), a, False, need, waits(k), *(w if k == 0 else ()))
                pe.mm(out, wh, lo(k), False, False)
                tok = pe.mm(out, wl, hi(k), False, b, signal=(j == UT - 1 or k == kt - 1))
                if j == UT - 1:
                    spent[u] = tok
                tile_n[0] += 1
                if k % UT in st["ticks"]:
                    tick()
            return tok

        def pair(b0, b1):
            u = tile_n[0] // UT
            split(u + 1 + AHEAD)
            toks = [None, None]
            for k in range(KD):
                for i, b in enumerate((b0, b1)):
                    s = (u + i) % NW
                    wh, wl = whi[s][:, k * P:(k + 1) * P], wlo[s][:, k * P:(k + 1) * P]
                    pe.mm(b.ap, wh, xh[:, k, :], k == 0, False, ready[u + i], st["x"][k], b.free)
                    pe.mm(b.ap, wh, xl[:, k, :], False, False)
                    toks[i] = pe.mm(b.ap, wl, xh[:, k, :], False, k == KD - 1, signal=(k == KD - 1))
                if k in st["ticks"]:
                    tick()
            spent[u], spent[u + 1] = toks
            tile_n[0] += 2 * UT
            st["xused"] = toks[1]
            tick()
            return toks

        pending = []

        def spawn(g, now=False):
            if now:
                next(g, None)
            pending.append(g)

        def tick():
            for g in list(pending):
                if next(g, "end") == "end":
                    pending.remove(g)

        def drain():
            while pending:
                tick()

        def take(free):
            while not free:
                yield
            return free.pop(0)

        st = {"xr": [None] * KD, "x": [[] for _ in range(KD)], "xused": None, "ticks": (3,)}
        rot = [0]

        def next_bank(k=4):
            b = bank[rot[0] % k]
            rot[0] += 1
            return b

        def xk(k):
            return st["x"][k]

        def project(b):
            t = gemm(KD, lambda k: xh[:, k, :], lambda k: xl[:, k, :], b.ap, xk, b.free)
            st["xused"] = t
            tick()
            return t

        xs = xin.rearrange("(k p) t -> p k t", p=P)
        fetch(0)
        xt = [load(xr[:, 0:4, :], xs[:, 0:4, :]), load(xr[:, 4:8, :], xs[:, 4:8, :])]
        fetch(1)
        c0 = [load(vc[:, :], vec), table(res[:, :], "ident", "mean640")]
        for k in range(KD):
            a = act.copy(xh[:, k, :], xr[:, k, :], xt[k // 4])
            d = dve.tt(xl[:, k, :], xr[:, k, :], f32(xh[:, k, :]), ALU.subtract, a)
            st["x"][k] = [a, d]
            st["xr"][k] = d
            if k == 1:
                split(1)
        dve.wait([c0])
        act.wait([c0])
        pe.wait([c0])

        def prescale():
            for k in range(KD):
                st["xr"][k] = pool.ts(xr[:, k, :], xr[:, k, :], ALPHA, ALU.mult, st["xr"][k], s2=1.0, op1=ALU.mult)

        class Norm:

            def __init__(self, square):
                self.square = square
                self.acc, self.sq = tmp[4], tmp[3]
                self.tok = self.sqt = None
                self.b, self.b5, self.b6 = bank[4], bank[5], bank[6]
                self.centred = False

            def squared(self, k, t):
                z = xr[:, k, :]
                if self.sqt is None:
                    self.sqt = act.act(self.sq.ap, z, ACT.Square, t, self.sq.free)
                else:
                    s = tmp[k % 2]
                    a = act.act(s.ap, z, ACT.Square, t, s.free)
                    self.sqt = pool.tt(self.sq.ap, self.sq.ap, s.ap, ALU.add, a, self.sqt)
                    s.free = [self.sqt]

            def add(self, k, t):
                z = xr[:, k, :]
                if self.square:
                    if k < KD - 1:
                        self.squared(k, t)
                elif k < NC:
                    if k == 0:
                        self.tok = pool.put(lambda e: e.tensor_copy(self.acc.ap, z), [t, self.acc.free])
                    else:
                        self.tok = pool.tt(self.acc.ap, self.acc.ap, z, ALU.add, t, self.tok)
                    if k == NC - 1:
                        spawn(self.centre())
                else:
                    assert self.centred
                    self.rest.append(t)
                    if k < KD - 1:
                        self.squared(k, t)
                        spawn(self.summed(k, t))
                if k == KD - 2:
                    act.act(vc[:, V_N - 1:V_N], col(V_EPS), ACT.Sqrt)
                    spawn(self.gathered())

            def centre(self):
                yield
                m = pe.mm(self.b.ap, mean640, self.acc.ap, True, True, self.tok, self.b.free, signal=True)
                self.acc.free = [m]
                self.centred = True
                self.rest = []
                for k in range(KD):
                    d = st["xr"][k] = dve.tt(xr[:, k, :], xr[:, k, :], self.b.ap, ALU.subtract, m, st["xr"][k])
                    if k < NC:
                        self.squared(k, d)
                self.b.free = [d]

            def summed(self, k, t):
                pe.mm(self.b6.ap, mean1024, xr[:, k, :], k == NC, False, t, self.b6.free)
                yield

            def gathered(self):
                yield
                pe.mm(self.b5.ap, mean1024, self.sq.ap, True, False, self.sqt, self.b5.free)

        def layer_norm(nm, l, scale_next, then=None):
            drain()
            last = KD - 1
            t = st["xr"][last]
            s, e2, rc, b5, b6 = tmp[0], tmp[2], tmp[3], nm.b5, nm.b6
            m6 = pe.mm(b6.ap, mean1024, xr[:, last, :], False, True, t, signal=True)
            a = act.act(s.ap, xr[:, last, :], ACT.Square, t, s.free)
            m5 = pe.mm(b5.ap, mean1024, s.ap, False, True, a, signal=True)
            s.free = [m5]
            e = a = act.act(e2.ap, b6.ap, ACT.Square, m6, e2.free)
            cen = [None] * KD

            def centre(k):
                cen[k] = dve.tt(xr[:, k, :], xr[:, k, :], b6.ap, ALU.subtract, m6, e, st["xr"][k])

            centre(0)
            d = dve.tt(rc.ap, b5.ap, e2.ap, ALU.subtract, a, m5)
            b5.free = e2.free = [d]
            a = act.act(e2.ap, rc.ap, ACT.Sqrt, d, bias=vc[:, V_EPS:V_EPS + 1])
            centre(1)
            r = dve.recip(rc.ap, e2.ap, a)
            e2.free = [r]
            for k in range(KD):
                g, o = vc[:, V_LNG + 8 * l + k:V_LNG + 8 * l + k + 1], vc[:, V_LNB + 8 * l + k:V_LNB + 8 * l + k + 1]
                if cen[k] is None:
                    centre(k)
                s = tmp[k % 2]
                if then is not None:
                    n = dve.tt(xr[:, k, :], xr[:, k, :], rc.ap, ALU.mult, r, cen[k])
                    y = st["xr"][k] = act.act(xr[:, k, :], xr[:, k, :], ACT.Identity, n, scale=g, bias=o)
                    if k % 2:
                        q = pool.tt(s.ap, xr[:, k, :], xr[:, k, :], ALU.mult, y, s.free)
                    else:
                        q = act.act(s.ap, xr[:, k, :], ACT.Square, y, s.free)
                    m = pe.mm(b5.ap, mean1024, s.ap, k == 0, k == KD - 1, q, b5.free, signal=True)
                    s.free = [m]
                    continue
                n = dve.tt(s.ap, xr[:, k, :], rc.ap, ALU.mult, r, cen[k], s.free)
                a = act.act(xh[:, k, :], s.ap, ACT.Identity, n, st["xused"], scale=g, bias=o)
                if k < 2:
                    y = dve.ts(xr[:, k, :], s.ap, g, ALU.mult, n, s2=o, op1=ALU.add)
                else:
                    y = pool.ts(xr[:, k, :], s.ap, g, ALU.mult, n, s2=o, op1=ALU.add)
                s.free = [a, y]
                st["x"][k] = [a]
                cen[k] = (a, y)
                if k:
                    low(k - 1, cen)
            b6.free = [n]
            rc.free = [n]
            if then is not None:
                rms_apply(then, m, b5)
                return
            low(last, cen)
            if scale_next:
                prescale()

        def low(k, cen):
            a, y = cen[k]
            d = dve.tt(xl[:, k, :], xr[:, k, :], f32(xh[:, k, :]), ALU.subtract, y, a, st["xused"])
            st["x"][k] = [a, d]
            st["xr"][k] = d

        def rms_norm(nm, c):
            drain()
            last = KD - 1
            t = st["xr"][last]
            s, b5 = tmp[0], nm.b5
            a = act.act(s.ap, xr[:, last, :], ACT.Square, t, s.free)
            m = pe.mm(b5.ap, mean1024, s.ap, False, True, a, signal=True)
            s.free = [m]
            rms_apply(c, m, b5)

        def rms_apply(c, m, b5):
            sd, rc = tmp[2], tmp[3]
            a = act.act(sd.ap, b5.ap, ACT.Sqrt, m, sd.free, bias=vc[:, V_EPS + 1:V_EPS + 2])
            b5.free = [a]
            r = dve.recip(rc.ap, sd.ap, a, m)
            sd.free = [r]
            prev = None
            for k in range(KD + 1):
                if k < KD:
                    g = vc[:, c + k:c + k + 1]
                    s = tmp[k % 2]
                    n = dve.tt(s.ap, xr[:, k, :], rc.ap, ALU.mult, r, st["xr"][k], s.free)
                    a = act.act(xh[:, k, :], s.ap, ACT.Copy, n, st["xused"], scale=g)
                if prev is not None:
                    j, ps_, pg, pa = prev
                    d = dve.stt(xl[:, j, :], ps_.ap, pg, f32(xh[:, j, :]), ALU.mult, ALU.subtract, pa, st["xused"])
                    ps_.free = [d]
                    st["x"][j] = [pa, d]
                prev = (k, s, g, a)
            rc.free = [d]

        def residual(k, b, t, by, nm):
            d = dve.stt(xr[:, k, :], b.ap, by, xr[:, k, :], ALU.mult, ALU.add, t, st["xr"][k])
            b.free = [d]
            st["xr"][k] = d
            if nm is not None:
                nm.add(k, d)

        mem_free = []

        def ffn(by, nm):
            scope = ExitStack()
            hh = sb(f"hh{unit[0]}", [P, KF, T], F32R, scope)
            hl = sb(f"hl{unit[0]}", [P, KF, T], F32R, scope)
            unit[0] += 1
            free = list(mem_free)
            hready = []
            for j in range(KF):
                bg, bu = next_bank(), next_bank()
                tg, tu = pair(bg, bu)
                s, h = tmp[j % 2], tmp[2 + j % 2]
                a = act.act(s.ap, bg.ap, ACT.Silu, tg, s.free)
                d = dve.tt(h.ap, s.ap, bu.ap, ALU.mult, a, tu, h.free)
                bg.free, bu.free, s.free = [a], [d], [d]
                a = act.copy(hh[:, j, :], h.ap, d, free)
                d = dve.tt(hl[:, j, :], h.ap, f32(hh[:, j, :]), ALU.subtract, a, free)
                h.free = [d]
                hready.append([a, d])
            if nm is not None:
                st["ticks"] = (1, 3, 5)
            for f in range(KD):
                b = next_bank()
                t = gemm(KF, lambda k: hh[:, k, :], lambda k: hl[:, k, :], b.ap, lambda k: hready[k], b.free)
                residual(f, b, t, by, nm)
            st["ticks"] = (3,)
            mem_free[:] = [t]
            scope.close()

        def out_proj(nm):
            bs = [next_bank(), next_bank()]
            for f, t in enumerate(pair(*bs)):
                residual(f, bs[f], t, 1.0, nm)
            st["ticks"] = (1, 3, 5)
            for f in range(2, KD):
                b = next_bank()
                t = project(b)
                residual(f, b, t, 1.0, nm)
            st["ticks"] = (3,)

        def to_tokens(dst, src, b, *w):
            for i in range(4):
                t = pe.turn(b.ap[:, i * P:(i + 1) * P], src[:, i * P:(i + 1) * P], ident, *(list(w) + b.free if i == 0 else []), signal=(i == 3))
            c = dve.copy(dst, b.ap.rearrange("p (i f) -> p i f", i=4), t)
            b.free = [c]
            return t, c

        def fence(last=None, engines=None):
            if last is None:
                last = [(q.sem, q.n) for q in (pe, act, dve, pool) if q.n]
            for q in engines or (pe, act, dve, pool, sp):
                q.wait(list(last))

        def col(c, n=1, rows=slice(0, P)):
            return vc[rows, c:c + n]

        def over(ap, n):
            return ap[:, None, :].broadcast_to([ap.shape[0], n, ap.shape[1]])

        def along(ap, n):
            return ap[:, :, None].broadcast_to([ap.shape[0], ap.shape[1], n])

        def zeros(places):
            for x in places:
                t = pool.fill(x, 0.0, (pool.sem, pool.n))
            return t

        def store_parts(k, src, *w):
            a = act.copy(xh[:, k, :], src, *w)
            d = dve.tt(xl[:, k, :], src, f32(xh[:, k, :]), ALU.subtract, a, *w)
            st["x"][k] = [a, d]
            return d

        def mlstm():
            fence(mem_free)
            scope = ExitStack()

            def bufs(name, n, shape):
                return [Buf(sb(f"m{name}{i}", shape, F32, scope)) for i in range(n)]

            qb, kb, vb = bufs("q", 2, [P, T]), bufs("k", 2, [P, T]), bufs("v", 2, [P, 4, 2 * P])
            og = sb("mo", [P, 8, T], F32, scope)
            hs = sb("mh", [P, 8, T], F32, scope)
            tb = sb("mtb", [P, 4 * P], F32, scope)
            le, ge, one, mean256 = (tb[:, i * P:(i + 1) * P] for i in range(4))
            ct = table(tb[:, :], "mle", "mean256")
            rows = [sb(f"mr{i}", [64, T], F32, scope) for i in range(3)]
            nM, nm, fx = (r[:, :] for r in rows)
            at = sb("mat", [P, 4 * 64], F32, scope)
            nb, nkb, eb = bufs("n", 2, [P, T]), bufs("nk", 2, [P, T]), bufs("e", 2, [P, T])
            wt, pt = bufs("w", 2, [P, T]), bufs("p", 2, [P, T])
            banks, temps = bank[2:8], tmp[0:5]
            done = {}
            st["ticks"] = (2, 5)

            def gates(b, t):
                four = []
                for _ in range(4):
                    four.append((yield from take(temps)))
                g, f, e1, e2 = (x.ap for x in four)
                a = act.act(g, b.ap, ACT.Identity, t, [x.free for x in four], bias=col(V_GB))
                b.free = [a]
                d = dve.copy(f[0:64, :], g[64:128, :], a)
                yield
                a = act.act(e1[0:64, :], f[0:64, :], ACT.Abs, d)
                a = act.act(e2[0:64, :], e1[0:64, :], ACT.Exp, a, scale=-1.0)
                d = dve.ts(e2[0:64, :], e2[0:64, :], 1.0, ALU.add, a)
                a = act.act(e1[0:64, :], e2[0:64, :], ACT.Ln, d)
                d = dve.stt(f[0:64, :], f[0:64, :], 0.0, e1[0:64, :], ALU.min, ALU.subtract, a)
                d1 = dve.fill(e2[0:64, :], 1.0)
                yield
                dve.scan(e1[0:32, :], e2[0:32, :], f[0:32, :], ALU.mult, ALU.add, d, d1)
                d = dve.scan(e1[32:64, ::-1], e2[32:64, :], f[32:64, ::-1], ALU.mult, ALU.add)
                d = dve.tt(fx, g[0:64, :], e1[0:64, :], ALU.subtract, d)
                dve.scan(f[0:32, :], fx[0:32, :], fx[0:32, :], ALU.max, ALU.max, d)
                d = dve.scan(f[32:64, ::-1], fx[32:64, ::-1], fx[32:64, ::-1], ALU.max, ALU.max)
                d = dve.ts(nM, f[0:64, :], -1.0, ALU.mult, d, s2=1.0, op1=ALU.mult)
                r = dve.tt(nm, nM, e1[0:64, :], ALU.subtract, d)
                for x in four:
                    x.free = [r]
                temps.extend(four)
                yield
                yield
                b = yield from take(banks)
                for i in range(4):
                    t = pe.turn(b.ap[:, i * 64:(i + 1) * 64], fx[:, i * P:(i + 1) * P], ident[0:64, 0:64], r, b.free, signal=True)
                done["at"] = act.copy(at[:, :], b.ap[:, 0:256], t)
                b.free = [done["at"]]
                banks.append(b)
                done["rows"] = r
                spawn(bound(0, 0))

            def bound(h, r):
                n = 2 * h + r
                one_row = ident[0:64, 32 * r + h:32 * r + h + 1].broadcast_to([64, P])
                m, nk, e = nb[n % 2], nkb[n % 2], eb[n % 2]
                b = yield from take(banks)
                t = pe.mm(b.ap, one_row, nM, True, True, b.free, done["rows"], signal=True)
                a = act.copy(m.ap[:, :], b.ap, t, m.free)
                yield
                t = pe.mm(b.ap, one_row, nm, True, True, a, signal=True)
                a2 = act.act(e.ap[:, :], b.ap, ACT.Exp, t, e.free)
                b.free = [a2]
                banks.append(b)
                blocks = lambda x: x.rearrange("p (i f) -> p i f", i=4)
                d = dve.tt(blocks(nk.ap[:, :]), blocks(m.ap[:, :]), over(ge if r == 0 else le, 4), ALU.add, a, nk.free, ct)
                done["b", n] = (a, a2, d)

            def mix(h):
                need = [("q", h), ("k", h), ("v", h, 0), ("v", h, 1), "at"]
                while any(x not in done for x in need):
                    yield
                q, k, v = qb[h % 2], kb[h % 2], vb[h % 2]
                for r in range(2):
                    n = 2 * h + r
                    while ("b", n) not in done:
                        yield
                    if n < 7:
                        spawn(bound((n + 1) // 2, (n + 1) % 2))
                    a, a2, d = done["b", n]
                    m, e, nk = nb[n % 2], eb[n % 2], nkb[n % 2]
                    acc = None
                    for i, s in enumerate(range(4) if r == 0 else range(3, -1, -1)):
                        lo, hi = (s * P, T) if r == 0 else (0, (s + 1) * P)
                        b = yield from take(banks)
                        w, p = wt[i % 2], pt[i % 2]
                        t = pe.mm(b.ap[:, lo:hi], k.ap[:, s * P:(s + 1) * P], q.ap[:, lo:hi], True, True, b.free, done["q", h], done["k", h], signal=True)
                        bias = at[:, s * 64 + 32 * r + h:s * 64 + 32 * r + h + 1]
                        x = act.act(w.ap[:, s * P:(s + 1) * P], nk.ap[:, s * P:(s + 1) * P], ACT.Exp, d, done["at"], w.free, bias=bias)
                        olo, ohi = ((s + 1) * P, T) if r == 0 else (0, s * P)
                        if ohi > olo:
                            x = act.act(w.ap[:, olo:ohi], m.ap[:, olo:ohi], ACT.Exp, bias=bias)
                        y = dve.tt(p.ap[:, lo:hi], b.ap[:, lo:hi], w.ap[:, lo:hi], ALU.mult, x, t, p.free)
                        w.free = b.free = [y]
                        banks.append(b)
                        yield
                        if acc is None:
                            acc = []
                            for _ in range(3):
                                acc.append((yield from take(banks)))
                        for c in range(3):
                            l = one if c == 2 else v.ap[:, s, c * P:(c + 1) * P]
                            t = pe.mm(acc[c].ap[:, lo:hi], l, p.ap[:, lo:hi], i == 0, i == 3, y, ct, done["v", h, c % 2],
                                      acc[c].free if i == 0 else None, signal=(c == 2))
                        p.free = [t]
                    nk.free = m.free = [x]
                    if r == 1:
                        q.free = k.free = v.free = [t]
                    spawn(finish(h, r, acc, e, a2, t))
                    yield

            def finish(h, r, acc, e, a2, t):
                s1 = yield from take(temps)
                x = act.act(s1.ap, acc[2].ap, ACT.Abs, t, s1.free)
                acc[2].free = [x]
                banks.append(acc[2])
                y = dve.tt(s1.ap, s1.ap, e.ap[:, :], ALU.max, x, a2)
                e.free = [y]
                y = dve.recip(s1.ap, s1.ap, y)
                for c in range(2):
                    o = hs[:, 2 * h + c, :]
                    if r == 0:
                        y2 = dve.tt(o, acc[c].ap, s1.ap, ALU.mult, y)
                        done["h", 2 * h + c] = y2
                        acc[c].free = [y2]
                    else:
                        s = yield from take(temps)
                        y2 = dve.tt(s.ap, acc[c].ap, s1.ap, ALU.mult, y, s.free)
                        acc[c].free = [y2]
                        g = pool.tt(o, o, s.ap, ALU.add, y2, done["h", 2 * h + c])
                        s.free = [g]
                        temps.append(s)
                        done["h", 2 * h + c] = g
                s1.free = [y2]
                temps.append(s1)
                yield
                yield
                banks.extend(acc[0:2])
                if r == 0:
                    return
                yield
                b = yield from take(banks)
                w = [done["h", 2 * h], done["h", 2 * h + 1]]
                pe.mm(b.ap, mean256, hs[:, 2 * h, :], True, False, w, b.free)
                t = pe.mm(b.ap, mean256, hs[:, 2 * h + 1, :], False, True, signal=True)
                ss = []
                for c in range(2):
                    d = dve.tt(hs[:, 2 * h + c, :], hs[:, 2 * h + c, :], b.ap, ALU.subtract, t)
                    s = yield from take(temps)
                    ss.append(s)
                    a = act.act(s.ap, hs[:, 2 * h + c, :], ACT.Square, d, s.free)
                b.free = [d]
                yield
                for c in range(2):
                    t = pe.mm(b.ap, mean256, ss[c].ap, c == 0, c == 1, a, b.free, signal=True)
                s, s2 = ss
                s2.free = [t]
                temps.append(s2)
                a = act.act(s.ap, b.ap, ACT.Sqrt, t, bias=col(V_EPS))
                b.free = [a]
                banks.append(b)
                r = dve.recip(s.ap, s.ap, a)
                for c in range(2):
                    i = 2 * h + c
                    done["n", i] = dve.stt(hs[:, i, :], hs[:, i, :], col(V_MNG + i), s.ap, ALU.mult, ALU.mult, r)
                s.free = [done["n", i]]
                temps.append(s)

            def copied(b, t, dst, scale, key):
                done[key] = act.act(dst.ap[:, :], b.ap, ACT.Copy, t, dst.free, scale=scale)
                b.free = [done[key]]

            for h in range(4):
                bs = [next_bank(2), next_bank(2)]
                if h == 0:
                    tg, t = pair(*bs)
                    spawn(gates(bs[0], tg), now=True)
                    copied(bs[1], t, qb[0], 1.0, ("q", 0))
                    b = next_bank(2)
                    copied(b, project(b), kb[0], P ** -0.5, ("k", 0))
                else:
                    copied(bs[0], project(bs[0]), qb[h % 2], 1.0, ("q", h))
                    copied(bs[1], project(bs[1]), kb[h % 2], P ** -0.5, ("k", h))
                for c in range(2):
                    b = next_bank(2)
                    t = project(b)
                    v = vb[h % 2]
                    spawn(transposed(v, v.ap[:, :, c * P:(c + 1) * P], b, t, banks, temps, done, ("v", h, c)), now=True)
                if h:
                    while ("n", 2 * h - 1) not in done and len(pending) > 6:
                        tick()
                spawn(mix(h))
            for c in range(8):
                b = next_bank(2)
                t = project(b)
                a = act.act(og[:, c, :], b.ap, ACT.Sigmoid, t)
                b.free = [a]
                done["o", c] = a
                for x in range(c + 1):
                    if ("m", x) not in done and ("n", x) in done:
                        done["m", x] = pool.tt(hs[:, x, :], hs[:, x, :], og[:, x, :], ALU.mult, done["n", x], done["o", x])
            drain()
            for c in range(8):
                if ("m", c) not in done:
                    done["m", c] = dve.tt(hs[:, c, :], hs[:, c, :], og[:, c, :], ALU.mult, done["n", c], done["o", c])
                d = store_parts(c, hs[:, c, :], done["m", c], st["xused"])
            st["ticks"] = (3,)
            scope.close()
            mem_free[:] = [d, st["x"][7]]

        def window():
            fence(mem_free)
            scope = ExitStack()
            q = sb("wq", [P, 8, T], F32, scope)
            kz = sb("wk", [P, 2, 2, T], F32, scope)
            zero = zeros([kz[64 - 64 * g:128 - 64 * g, g, :, :] for g in range(2)])
            vt = sb("wv", [P, 4, 2 * P], F32, scope)
            dist = sb("wd", [P, 3 * P], F32, scope)
            ct = table(dist[:, :], "dist")
            sx = [Buf(sb(f"ws{i}", [P, 2, 3 * P], F32, scope)) for i in range(2)]
            pp = [Buf(sb(f"wp{i}", [P, 2, 3 * P], F32, scope)) for i in range(4)]
            pt = [Buf(sb(f"wt{i}", [P, 2, 3 * P], F32, scope)) for i in range(2)]
            nsink = sb("wns", [P, 16], F32, scope)
            small = [Buf(sb(f"wm{i}", [P, 16], F32, scope)) for i in range(3)]
            ns = dve.ts(nsink[:, :], col(V_SINK, 16), -1.0, ALU.mult, s2=1.0, op1=ALU.mult)
            bs = [next_bank(), next_bank()]
            ts = pair(*bs)
            for c in range(2):
                bs[c].free = [act.copy(kz[0:64, 0, c, :], bs[c].ap[0:64, :], ts[c]),
                              dve.copy(kz[64:128, 1, c, :], bs[c].ap[64:128, :], ts[c])]
            for c in range(2):
                b = next_bank()
                t = project(b)
                s = tmp[c % 2]
                a = act.copy(s.ap, b.ap, t, s.free)
                b.free = [a]
                t, d = to_tokens(vt[:, :, c * P:(c + 1) * P], s.ap, bank[4 + c % 2], a)
                s.free = [t]
            for c in range(8):
                b = next_bank()
                t = project(b)
                a = act.act(q[:, c, :], b.ap, ACT.Copy, t, scale=0.125)
                b.free = [a]
            pe.wait([a, d, zero])
            dve.wait([ct, ns])
            units = [(t, i) for t in range(8) for i in range(4)]
            stage = {}

            def first(n):
                t, i = units[n]
                j0, j1 = max(0, i - 1), min(3, i + 1)
                for g in range(2):
                    b = bank[2 * (n % 2) + g]
                    x = pe.mm(b.ap[:, 0:(j1 - j0 + 1) * P], q[:, t, i * P:(i + 1) * P],
                              kz[:, g, t // 4, j0 * P:(j1 + 1) * P], True, True, b.free, signal=True)
                stage[n] = x

            def second(n):
                t, i = units[n]
                j0, j1 = max(0, i - 1), min(3, i + 1)
                w = (j1 - j0 + 1) * P
                at = (j0 - i + 1) * P
                s, p, m = sx[n % 2], pp[n % 4], small[n % 3]
                for g in range(2):
                    slope = float(np.float32(2.0 ** (-8.0 * (WIN_ORDER[2 * t + g] + 1) / 16)))
                    b = bank[2 * (n % 2) + g]
                    d = dve.stt(s.ap[:, g, 0:w], dist[:, at:at + w], -slope, b.ap[:, 0:w], ALU.mult, ALU.add, stage[n], s.free)
                    b.free = [d]
                nm, sums, es = m.ap[:, 0:2], m.ap[:, 2:4], m.ap[:, 4:6]
                d = dve.maxneg(nm, s.ap[:, :, 0:w], d, m.free)
                d = dve.tt(nm, nm, nsink[:, 2 * t:2 * t + 2], ALU.min, d)
                d2 = dve.tt(es, nm, col(V_SINK + 2 * t, 2), ALU.add, d)
                for g in range(2):
                    a = act.act(p.ap[:, g, 0:w], s.ap[:, g, 0:w], ACT.Exp, d, p.free, bias=nm[:, g:g + 1], total=sums[:, g:g + 1])
                s.free = [a]
                stage[n] = act.act(es, es, ACT.Exp, d2)

            def scale(n):
                t, i = units[n]
                w = (min(3, i + 1) - max(0, i - 1) + 1) * P
                p, m = pp[n % 4], small[n % 3]
                sums, es = m.ap[:, 2:4], m.ap[:, 4:6]
                d = dve.tt(sums, sums, es, ALU.add, stage[n])
                d = dve.recip(sums, sums, d)
                d2 = pool.ts(p.ap[:, 0, 0:w], p.ap[:, 0, 0:w], sums[:, 0:1], ALU.mult, d, s2=1.0, op1=ALU.mult)
                d3 = pool.ts(p.ap[:, 1, 0:w], p.ap[:, 1, 0:w], sums[:, 1:2], ALU.mult, d, s2=1.0, op1=ALU.mult)
                m.free = [d2, d3]
                stage[n] = [d2, d3]

            def third(n):
                t, i = units[n]
                nk = min(3, i + 1) - max(0, i - 1) + 1
                p, y = pp[n % 4], pt[n % 2]
                for g in range(2):
                    b = bank[4 + g]
                    for j in range(nk):
                        x = pe.turn(b.ap[:, j * P:(j + 1) * P], p.ap[:, g, j * P:(j + 1) * P], ident, stage[n], b.free, signal=(j == nk - 1))
                z = act.copy(y.ap[:, :, 0:nk * P], ps[:, 4:6, 0:nk * P], x, y.free)
                bank[4].free = bank[5].free = [z]
                stage[n, 0] = stage[n, 1] = z
                p.free = [x]

            def fourth(n):
                t, i = units[n]
                j0, j1 = max(0, i - 1), min(3, i + 1)
                b, y = bank[6 + t % 2], pt[n % 2]
                for g in range(2):
                    for j in range(j0, j1 + 1):
                        at = (t // 4) * P + 64 * g
                        x = pe.mm(b.ap[64 * g:64 * g + 64, i * P:(i + 1) * P], vt[:, j, at:at + 64],
                                  y.ap[:, g, (j - j0) * P:(j - j0 + 1) * P], j == j0, j == j1, stage[n, g],
                                  b.free, signal=(g == 1 and j == j1))
                y.free = [x]
                if i == 3:
                    b.free = [store_parts(t, b.ap, x, st["xused"])]
                    b.free += st["x"][t]

            first(0)
            for n in range(len(units) + 4):
                if n + 1 < len(units):
                    first(n + 1)
                if n < len(units):
                    second(n)
                if 0 <= n - 1 < len(units):
                    scale(n - 1)
                if 0 <= n - 4:
                    fourth(n - 4)
                if 0 <= n - 3 < len(units):
                    third(n - 3)
            scope.close()
            mem_free[:] = b.free

        class Hgrn:
            def __init__(self, l, hres, scope, banks, temps):
                self.l, self.hres, self.banks, self.temps = l, hres, banks, temps

                def bufs(name, n, shape):
                    return [Buf(sb(f"h{name}{l}{i}", shape, F32, scope)) for i in range(n)]

                self.q, self.k, self.b = bufs("q", 2, [P, T]), bufs("k", 2, [P, T]), bufs("b", 2, [P, T])
                self.v = bufs("v", 2, [P, 4, P])
                self.x, self.qe, self.ke = bufs("x", 3, [P, T]), bufs("qe", 2, [P, T]), bufs("ke", 2, [P, T])
                self.ad, self.ao = bufs("ad", 2, [P, T]), bufs("ao", 1, [P, 6 * P])
                tb = sb(f"htb{l}", [P, 6 * P + T], F32, scope)
                self.lbs = lbs = sb(f"hlb{l}", [P, 48], F32, scope)
                self.ct = table(tb[:, :], "lv16", "keep")
                self.keep = tb[:, 6 * P:]
                self.mask = {h: tb[:, i * P:(i + 1) * P].bitcast(U32) for i, h in enumerate((16, 8, 4, 2, 1))}
                self.mask[0] = ident.bitcast(U32)
                self.mean128 = tb[:, 5 * P:6 * P]
                l0, l1 = col(V_LB, 4), col(V_LB + 4, 4)
                self.c = c = [lbs[:, 4 * i:4 * i + 4] for i in range(8)]
                d = dve.tt(c[0], l0, l1, ALU.max)
                d = dve.tt(c[1], l0, c[0], ALU.subtract, d)
                d = dve.tt(c[2], l1, c[0], ALU.subtract, d)
                a = act.act(lbs[:, 4:12], lbs[:, 4:12], ACT.Exp, d)
                d = dve.tt(c[3], c[1], c[2], ALU.add, a)
                d = dve.recip(c[3], c[3], d)
                d = dve.tt(c[4], c[1], c[3], ALU.mult, d)
                d = dve.tt(c[5], c[2], c[3], ALU.mult, d)
                d = dve.tt(c[5], c[4], c[5], ALU.add, d)
                d = dve.tt(c[6], c[4 + l], c[4], ALU.subtract, d)
                self.lb_ok = dve.ts(c[7], c[6], -1.0, ALU.mult, d, s2=1.0, op1=ALU.add)
                self.chain = [dve.fill(x.ap[:, :], 0.0) for x in self.ad]
                self.off = [None] * 4
                self.count = [0] * 4
                self.done = {}

            def project(self, h):
                q, k, bb, v = self.q[h % 2], self.k[h % 2], self.b[h % 2], self.v[h % 2]
                bs = [next_bank(2), next_bank(2)]
                ts = pair(*bs) if h == 0 else (project(bs[0]), project(bs[1]))
                b, t = bs[0], ts[0]
                a = act.act(q.ap[:, :], b.ap, ACT.Silu, t, q.free)
                self.done["q", h] = a
                b.free = [a]
                b, t = bs[1], ts[1]
                a = act.act(bb.ap[:, :], b.ap, ACT.Sigmoid, t, bb.free)
                b.free = [a]
                d = dve.ts(bb.ap[:, :], bb.ap[:, :], self.c[7][:, h:h + 1], ALU.mult, a, self.lb_ok, s2=self.c[6][:, h:h + 1], op1=ALU.add)
                self.done["k", h] = dve.ts(k.ap[:, :], bb.ap[:, :], -1.0, ALU.mult, d, k.free, s2=1.0, op1=ALU.add)
                b = next_bank(2)
                t = project(b)
                a = act.act(bb.ap[:, :], bb.ap[:, :], ACT.Ln, self.done["k", h])
                self.done["b", h] = dve.scan(bb.ap[:, :], self.keep, bb.ap[:, :], ALU.mult, ALU.add, a, self.ct)
                spawn(transposed(v, v.ap[:, :, :], b, t, self.banks, self.temps, self.done, ("v", h)), now=True)
                b = next_bank(2)
                t = project(b)
                self.done["g", h] = act.act(self.hres[:, h, :], b.ap, ACT.Silu, t)
                b.free = [self.done["g", h]]
                spawn(self.mix(h))

            def mix(self, h):
                for half in (64, 32, 16, 8, 4, 2, 1):
                    x = yield from take(self.x)
                    spawn(self.level(h, half, x))
                    yield
                spawn(self.level(h, 0, None))
                yield
                x = yield from take(self.x)
                x2 = yield from take(self.x)
                spawn(self.between(h, x, x2))
                while self.count[h] < 9 or ("v", h) not in self.done:
                    yield
                spawn(self.values(h))

            def level(self, h, half, x):
                v = lambda y: y.rearrange("p (i f) -> p i f", f=2 * half)
                v4 = lambda y: y.rearrange("p (i f) -> p i f", f=P)
                bh, q, k = self.b[h % 2], self.q[h % 2], self.k[h % 2]
                pd = self.ad[h % 2]
                if half:
                    d = dve.tt(v(x.ap[:, :]), v(bh.ap[:, :]), along(v(bh.ap[:, :])[:, :, half - 1], 2 * half), ALU.subtract, self.done["b", h], x.free)
                    act.act(v(x.ap[:, :])[:, :, 0:half], v(x.ap[:, :])[:, :, 0:half], ACT.Exp, d, scale=-1.0)
                    a = act.act(v(x.ap[:, :])[:, :, half:], v(x.ap[:, :])[:, :, half:], ACT.Exp)
                    yield
                    qq = yield from take(self.qe)
                    ek = yield from take(self.ke)
                    d1 = dve.tt(qq.ap[:, :], q.ap[:, :], x.ap[:, :], ALU.mult, a, self.done["q", h], qq.free)
                    d2 = pool.tt(ek.ap[:, :], k.ap[:, :], x.ap[:, :], ALU.mult, a, self.done["k", h], ek.free)
                    x.free = [d1, d2]
                    self.x.append(x)
                    kx, qx, w = ek.ap, qq.ap, [d1, d2]
                else:
                    kx, qx, w = k.ap, q.ap, [self.done["q", h], self.done["k", h]]
                yield
                yield
                pb = yield from take(self.banks)
                if half >= 32:
                    for i in range(T // (2 * half)):
                        lo = 2 * half * i
                        r = lo % P
                        t = pe.mm(pb.ap[r:r + half, lo + half:lo + 2 * half], kx[:, lo:lo + half], qx[:, lo + half:lo + 2 * half],
                                  True, True, w, pb.free, signal=True)
                else:
                    for i in range(4):
                        t = pe.mm(pb.ap[:, i * P:(i + 1) * P], kx[:, i * P:(i + 1) * P], qx[:, i * P:(i + 1) * P],
                                  True, True, w, pb.free, signal=(i == 3))
                if half:
                    qq.free = ek.free = [t]
                    self.qe.append(qq)
                    self.ke.append(ek)
                yield
                free = pd.free if self.count[h] == 0 else None
                if half >= 32:
                    for r in range(0, P, 2 * half):
                        y = dve.copy(v4(pd.ap[:, :])[r:r + half, :, r + half:r + 2 * half], v4(pb.ap)[r:r + half, :, r + half:r + 2 * half],
                                     t, free, self.chain[h % 2])
                        self.chain[h % 2] = y
                else:
                    y = dve.pick(v4(pd.ap[:, :]), over(self.mask[half], 4), v4(pb.ap), t, free, self.chain[h % 2], self.ct)
                    self.chain[h % 2] = y
                pb.free = [y]
                self.banks.append(pb)
                self.count[h] += 1

            def between(self, h, x, x2):
                v4 = lambda y: y.rearrange("p (i f) -> p i f", f=P)
                bh, q, k, po, lbs = self.b[h % 2], self.q[h % 2], self.k[h % 2], self.ao[0], self.lbs
                ends = v4(bh.ap[:, :])[:, 0:3, P - 1]
                d = dve.tt(v4(x.ap[:, :])[:, 0:3, :], along(ends, P), v4(bh.ap[:, :])[:, 0:3, :], ALU.subtract, x.free, self.done["b", h])
                a0 = act.act(x.ap[:, 0:384], x.ap[:, 0:384], ACT.Exp, d)
                act.act(x2.ap[:, 0:384], bh.ap[:, P:T], ACT.Exp, x2.free, self.done["b", h])
                a = act.act(lbs[:, 32:35], ends, ACT.Exp, self.done.get("lbs"))
                yield
                qq = yield from take(self.qe)
                ek = yield from take(self.ke)
                d1 = pool.tt(ek.ap[:, 0:384], k.ap[:, 0:384], x.ap[:, 0:384], ALU.mult, a0, ek.free)
                d2 = dve.tt(qq.ap[:, 0:384], q.ap[:, P:T], x2.ap[:, 0:384], ALU.mult, a, qq.free)
                d3 = pool.ts(ek.ap[:, 384:T], ek.ap[:, 0:P], lbs[:, 33:34], ALU.mult, d1, a, s2=1.0, op1=ALU.mult)
                d4 = dve.ts(qq.ap[:, 384:T], qq.ap[:, 256:384], lbs[:, 34:35], ALU.mult, d2, s2=1.0, op1=ALU.mult)
                x.free = x2.free = [d3, d4]
                self.x += [x, x2]
                self.done["lbs"] = [d3, d4]
                yield
                yield
                b0 = yield from take(self.banks)
                b1 = yield from take(self.banks)
                K = lambda i: ek.ap[:, i * P:(i + 1) * P]
                Q = lambda i: qq.ap[:, i * P:(i + 1) * P]
                pairs = [(0, 0, K(0), Q(0)), (0, 1, K(3), Q(1)), (0, 2, K(3), Q(3)), (1, 0, K(1), Q(1)), (1, 1, K(1), Q(3)), (1, 2, K(2), Q(2))]
                for bi, at, kx, qx in pairs:
                    o = (b0, b1)[bi]
                    t = pe.mm(o.ap[:, at * P:(at + 1) * P], kx, qx, True, True, d3, d4, o.free, signal=True)
                qq.free = ek.free = [t]
                self.qe.append(qq)
                self.ke.append(ek)
                yield
                y1 = act.copy(po.ap[:, 0:384], b0.ap[:, 0:384], t, po.free)
                self.off[h] = act.copy(po.ap[:, 384:768], b1.ap[:, 0:384], t)
                b0.free, b1.free = [y1], [self.off[h]]
                self.banks += [b0, b1]
                self.count[h] += 1

            def values(self, h):
                pd, po, vt = self.ad[h % 2], self.ao[0], self.v[h % 2]
                ob = yield from take(self.banks)
                off = {0: (0, 384), 1: (384, 640), 2: (640, 768)}
                w = [self.chain[h % 2], self.off[h], self.done["v", h]]
                for j in range(4):
                    v = vt.ap[:, j, :]
                    t = pe.mm(ob.ap[:, j * P:(j + 1) * P], v, pd.ap[:, j * P:(j + 1) * P], j == 0, j == 3, w, ob.free, signal=True)
                    if j < 3:
                        t = pe.mm(ob.ap[:, (j + 1) * P:T], v, po.ap[:, off[j][0]:off[j][1]], False, False, signal=True)
                for x in (pd, po, vt, self.q[h % 2], self.k[h % 2], self.b[h % 2]):
                    x.free = [t]
                self.b[h % 2].free = self.q[h % 2].free = self.k[h % 2].free = [t, self.done["lbs"]]
                yield
                s = yield from take(self.temps)
                r = yield from take(self.temps)
                a = act.act(s.ap, ob.ap, ACT.Square, t, s.free)
                yield
                mb = yield from take(self.banks)
                t2 = pe.mm(mb.ap, self.mean128, s.ap, True, True, a, mb.free, self.ct, signal=True)
                yield
                a = act.act(r.ap, mb.ap, ACT.Sqrt, t2, r.free, bias=col(V_EPS + 1))
                mb.free = [a]
                self.banks.append(mb)
                d = dve.recip(r.ap, r.ap, a)
                d = dve.tt(s.ap, ob.ap, r.ap, ALU.mult, d, t2)
                ob.free = [d]
                self.banks.append(ob)
                r.free = [d]
                d = dve.stt(self.hres[:, h, :], s.ap, col(V_HGN + self.l), self.hres[:, h, :], ALU.mult, ALU.mult, d, self.done["g", h])
                s.free = [d]
                self.temps += [r, s]
                self.done["o", h] = d

        def transposed(dbuf, dst, b, t, banks, temps, done, key):
            s = yield from take(temps)
            a = act.copy(s.ap, b.ap, t, s.free)
            b.free = [a]
            yield
            yield
            pb = yield from take(banks)
            for i in range(4):
                t = pe.turn(pb.ap[:, i * P:(i + 1) * P], s.ap[:, i * P:(i + 1) * P], ident, a, pb.free, signal=(i == 3))
            s.free = [t]
            temps.append(s)
            yield
            c = dve.copy(dst, pb.ap.rearrange("p (i f) -> p i f", i=4), t, dbuf.free)
            pb.free = [c]
            banks.append(pb)
            done[key] = c

        class Attention:
            def __init__(self, l, scope, early, banks, temps):
                self.l, self.banks, self.temps = l, banks, temps
                self.q = sb(f"nq{l}", [P, 4, T], F32, scope)
                self.kz = sb(f"nk{l}", [P, 2, 2, T], F32, scope)
                self.vt = sb(f"nv{l}", [P, 2, 4, P], F32, scope)
                tb = sb(f"ntb{l}", [P, 5 * P + 2 * T], F32, scope)
                self.mats = sb(f"nm{l}", [P, 2, 160], F32, scope)
                self.kc = sb(f"nkc{l}", [P, 2, 32], F32, scope)
                self.zero = zeros([x for g in range(2) for x in (self.kz[64 - 64 * g:128 - 64 * g, g, :, :], self.kc[64 - 64 * g:128 - 64 * g, g, :])])
                self.vcm = sb(f"nvc{l}", [32, P], F32, scope)
                self.gt = sb(f"ng{l}", [P, 4, 24], F32, scope)
                self.st1 = sb(f"ns{l}", [P, 80], F32, scope)
                self.le, self.rotm, self.mean64, self.cneg, self.cone = (tb[:, i * P:(i + 1) * P] for i in range(5))
                self.ct = [table(tb[:, :], "le", "sin"), load(self.mats[:, :, :], mats_in[l].rearrange("c p n -> p c n"))]
                self.cos, self.sin = tb[:, 5 * P:5 * P + T], tb[:, 5 * P + T:]
                self.xx = sb(f"nx{l}", [P, 16, 62], F32, early)
                self.xxh = sb(f"nxh{l}", [P, 16, 62], F32R, early)
                self.xxl = sb(f"nxl{l}", [P, 16, 62], F32R, early)
                self.hid = sb(f"nh{l}", [P, 2, 62], F32, early)
                self.cc = sb(f"nc{l}", [P, 2, T], F32, early)
                self.qg = dve.ts(self.st1[:, 0:1], col(V_QG + l), 0.125, ALU.mult, s2=1.0, op1=ALU.mult)
                self.done = {}

            def head_norm(self, dst, src, gain, c, s, n, t, b, home, key):
                s0 = yield from take(self.temps)
                s1 = yield from take(self.temps)
                a = act.act(s0.ap[:, 0:n], src, ACT.Square, t, s0.free)
                yield
                yield
                b2 = yield from take(self.banks)
                m = pe.mm(b2.ap[:, 0:n], self.mean64, s0.ap[:, 0:n], True, True, a, b2.free, self.ct, signal=True)
                yield
                a = act.act(s1.ap[:, 0:n], b2.ap[:, 0:n], ACT.Sqrt, m, s1.free, bias=col(V_EPS + 1))
                b2.free = [a]
                self.banks.append(b2)
                d = dve.recip(s1.ap[:, 0:n], s1.ap[:, 0:n], a)
                d = dve.stt(s0.ap[:, 0:n], src, gain, s1.ap[:, 0:n], ALU.mult, ALU.mult, d, m, self.qg)
                b.free = [d]
                if home is not None:
                    home.append(b)
                yield
                yield
                yield
                b3 = yield from take(self.banks)
                m = pe.mm(b3.ap[:, 0:n], self.rotm, s0.ap[:, 0:n], True, True, d, b3.free, signal=True)
                d1 = pool.tt(s0.ap[:, 0:n], s0.ap[:, 0:n], c, ALU.mult, m, self.ct)
                yield
                d2 = dve.tt(s1.ap[:, 0:n], b3.ap[:, 0:n], s, ALU.mult, m, self.ct)
                b3.free = [d2]
                self.banks.append(b3)
                if isinstance(dst, list):
                    d = [dve.tt(dst[g], s0.ap[64 * g:64 * g + 64, 0:n], s1.ap[64 * g:64 * g + 64, 0:n], ALU.add, d1, d2) for g in range(2)]
                else:
                    d = dve.tt(dst, s0.ap[:, 0:n], s1.ap[:, 0:n], ALU.add, d1, d2)
                s0.free = s1.free = [d]
                self.temps += [s0, s1]
                self.done[key] = d

            def compress(self, c):
                while ("cfree", c) not in self.done:
                    yield
                used = self.done["cfree", c]
                d = self.done["c", c]
                for g in range(2):
                    rg = slice(64 * g, 64 * g + 64)
                    src = self.cc[rg, c, :].rearrange("p (n c) -> p c n", c=16)
                    pos = self.mats[rg, c, 0:32]
                    for par in range(2):
                        for up in range(2):
                            o = self.xx[64 * par:64 * par + 64, 8 * up:8 * up + 8, 31 * g:31 * g + 31]
                            y = dve.tt(o, src[:, par::2, up:up + 31], along(pos[:, 16 * up + par:16 * up + 16:2], 31), ALU.add, d, used, self.ct)
                    yield
                a = act.copy(self.xxh[:, :, :], self.xx[:, :, :], y, used)
                y = dve.tt(self.xxl[:, :, :], self.xx[:, :, :], f32(self.xxh[:, :, :]), ALU.subtract, a, used)
                self.done["x", c] = [a, y]

            def plain(self, c):
                b = next_bank(2)
                t = project(b)
                self.done["c", c] = act.copy(self.cc[:, c, :], b.ap, t)
                b.free = [self.done["c", c]]

            def key(self, c):
                b = next_bank(2)
                t = project(b)
                spawn(self.freed(b, [self.kz[64 * g:64 * g + 64, g, c, :] for g in range(2)], col(V_KG + 4 * self.l + 1 + c), t, ("k", c)), now=True)

            def query(self, c):
                b = next_bank(2)
                t = project(b)
                spawn(self.freed(b, self.q[:, c, :], self.st1[:, 0:1], t, ("q", c)), now=True)

            def freed(self, b, dst, gain, t, key):
                s = yield from take(self.temps)
                a = act.copy(s.ap, b.ap, t, s.free)
                b.free = [a]
                yield from self.head_norm(dst, s.ap, gain, self.cos, self.sin, T, a, s, self.temps, key)

            def value(self, c):
                b = next_bank(2)
                t = project(b)
                spawn(transposed(Buf(None), self.vt[:, c, :, :], b, t, self.banks, self.temps, self.done, ("v", c)), now=True)

            def gates(self):
                b = next_bank(2)
                t = project(b)
                spawn(self.gate_task(b, t), now=True)

            def gate_task(self, b, t):
                s = yield from take(self.temps)
                a = act.act(s.ap[0:32, :], b.ap[0:32, :], ACT.Sigmoid, t, s.free)
                b.free = [a]
                yield
                pb = yield from take(self.banks)
                for i in range(4):
                    t = pe.turn(pb.ap[:, i * 32:(i + 1) * 32], s.ap[0:32, i * P:(i + 1) * P], ident[0:32, 0:32], a, pb.free, signal=(i == 3))
                s.free = [t]
                self.temps.append(s)
                yield
                self.done["gt"] = dve.copy(self.gt[:, :, :], pb.ap[:, 0:P].rearrange("p (i f) -> p i f", f=32)[:, :, 0:24], t)
                pb.free = [self.done["gt"]]
                self.banks.append(pb)

            def hidden(self, c):
                while ("x", c) not in self.done:
                    tick()
                w = self.done["x", c]
                b = next_bank(2)
                o = b.ap[0:62, 0:2 * P]
                for k in range(16):
                    u, j = divmod(tile_n[0], UT)
                    if j == 0:
                        split(u + AHEAD)
                    s = u % NW
                    wh, wl = whi[s][:, j * P:(j + 2) * P], wlo[s][:, j * P:(j + 2) * P]
                    pe.mm(o, self.xxh[:, k, :], wh, k == 0, False, w, ready[u], b.free)
                    pe.mm(o, self.xxh[:, k, :], wl, False, False)
                    t = pe.mm(o, self.xxl[:, k, :], wh, False, k == 15, signal=(j == UT - 2))
                    if j == UT - 2:
                        spent[u] = t
                        tick()
                    tile_n[0] += 2
                h = act.act(self.cc[0:62, c, 0:2 * P], o, ACT.Silu, t, w)
                b.free = [h]
                self.done["cfree", 1] = t
                spawn(self.second_layer(c, h))

            def second_layer(self, c, h):
                yield
                b = yield from take(self.banks)
                for hh in range(2):
                    t = pe.turn(b.ap[:, 64 * hh:64 * hh + 62], self.cc[0:62, c, hh * P:(hh + 1) * P], ident[0:62, 0:62], h, b.free, signal=True)
                yield
                h = act.copy(self.hid[:, :, :], b.ap[:, 0:P].rearrange("p (h f) -> p h f", h=2)[:, :, 0:62], t, self.done.get("hid"))
                b.free = [h]
                self.banks.append(b)
                yield
                b = yield from take(self.banks)
                w2 = self.mats[:, c, 32:160].rearrange("p (h f) -> p h f", h=2)
                for g in range(2):
                    for hh in range(2):
                        t = pe.mm(b.ap[64 * g:64 * g + 64, 0:31], w2[:, hh, :], self.hid[:, hh, 31 * g:31 * g + 31], hh == 0, hh == 1, h, b.free, self.ct, signal=True)
                self.done["hid"] = t
                if c == 0:
                    yield from self.head_norm([self.kc[64 * g:64 * g + 64, g, 0:31] for g in range(2)], b.ap[:, 0:31], col(V_KG + 4 * self.l), self.cos[:, 31::16], self.sin[:, 31::16], 31, t, b, self.banks, "kc")
                    return
                yield
                s = yield from take(self.temps)
                a = act.copy(s.ap[:, 0:31], b.ap[:, 0:31], t, s.free)
                b.free = [a]
                self.banks.append(b)
                yield
                b = yield from take(self.banks)
                t = pe.turn(b.ap[0:31, 0:P], s.ap[:, 0:31], ident, a, b.free, signal=True)
                s.free = [t]
                self.temps.append(s)
                yield
                self.done["vcm"] = dve.copy(self.vcm[0:31, :], b.ap[0:31, 0:P], t)
                b.free = [self.done["vcm"]]
                self.banks.append(b)

        def attend(o, scope):
            l, q, kz, vt, kc, vcm, gt, st1, le, cneg, cone = o.l, o.q, o.kz, o.vt, o.kc, o.vcm, o.gt, o.st1, o.le, o.cneg, o.cone
            pc = sb(f"npc{l}", [P, 32, 31], F32, scope)
            pct = sb(f"npt{l}", [32, 32, P], F32, scope)
            pp = [Buf(sb(f"np{l}{i}", [P, 2, T], F32, scope)) for i in range(4)]
            pt = [Buf(sb(f"nt{l}{i}", [P, 2, T], F32, scope)) for i in range(2)]
            small = [Buf(sb(f"nsm{l}{i}", [P, 16], F32, scope)) for i in range(3)]
            gt_ok = o.done["gt"]

            nmx, sm = st1[:, 8:40], st1[:, 40:72]
            need = [o.done["q", i] for i in range(4)] + [o.done["kc"], o.zero]
            scores, turned = [], []
            for hf in range(2):
                b = bank[6 + hf]
                for t in range(4):
                    for i in range(4):
                        at = 4 * t + i
                        x = pe.mm(b.ap[:, 32 * at:32 * at + 31], q[:, t, i * P:(i + 1) * P], kc[:, hf, 0:31], True, True, b.free, need, signal=True)
                scores.append(x)
            for hf in range(2):
                b, x = bank[6 + hf], scores[hf]
                p3 = pc[:, 16 * hf:16 * hf + 16, :]
                s3 = b.ap.rearrange("p (u n) -> p u n", n=32)[:, :, 0:31]
                cn = cneg.rearrange("p (i n) -> p i n", n=32)[:, :, 0:31]
                for u in range(4):
                    y = dve.tt(p3[:, 4 * u:4 * u + 4, :], s3[:, 4 * u:4 * u + 4, :], cn, ALU.add, x)
                b.free = [y]
                m, s = nmx[:, 16 * hf:16 * hf + 16], sm[:, 16 * hf:16 * hf + 16]
                y = dve.maxneg(m, p3, y)
                y = dve.tt(p3, p3, along(m, 31), ALU.add, y)
                a = act.act(p3, p3, ACT.Exp, y)
                y = dve.put(lambda e, s=s, p3=p3: e.tensor_reduce(s, p3, AX, ALU.add), [a])
                y = dve.recip(s, s, y)
                for u in range(4):
                    head = 4 * hf + u
                    w = dve.tt(s[:, 4 * u:4 * u + 4], s[:, 4 * u:4 * u + 4], gt[:, :, 3 * head], ALU.mult, y, gt_ok)
                y = dve.tt(p3, p3, along(s, 31), ALU.mult, w)
                c1 = cone.rearrange("p (i n) -> p i n", n=32)[:, :, 0:31]
                for u in range(4):
                    y2 = dve.tt(p3[:, 4 * u:4 * u + 4, :], p3[:, 4 * u:4 * u + 4, :], c1, ALU.mult, y)
                turned.append((p3, y2))

            def turn_compressed():
                for hf, (p3, y2) in enumerate(turned):
                    for u in range(4):
                        b = bank[4 + u]
                        for i in range(4):
                            x = pe.turn(b.ap[0:31, i * P:(i + 1) * P], p3[:, 4 * u + i, :], ident, y2, b.free, signal=True)
                        z = act.copy(pct[0:31, 16 * hf + 4 * u:16 * hf + 4 * u + 4, :], b.ap[0:31, :].rearrange("p (i f) -> p i f", i=4), x)
                        b.free = [z]
                return z

            units = [(t, g, i) for t in range(4) for i in (0, 1, 2, 3) for g in range(2)]
            stage = {}
            done_vcm = o.done["vcm"]
            keys = [o.done["k", c] for c in range(2)]
            values = [o.done["v", c] for c in range(2)]

            def first(n):
                t, g, i = units[n]
                for br in range(2):
                    b = bank[2 * (n % 2) + br]
                    stage[n] = pe.mm(b.ap[:, 0:(i + 1) * P], q[:, t, i * P:(i + 1) * P],
                                     kz[:, g, br, 0:(i + 1) * P], True, True, b.free, keys, signal=True)

            def second(n):
                t, g, i = units[n]
                head = t + 4 * g
                w = (i + 1) * P
                two = ps[:, 2 * (n % 2):2 * (n % 2) + 2, :]
                pair = (bank[2 * (n % 2)], bank[2 * (n % 2) + 1])
                p, m = pp[n % 4], small[n % 3]
                nm, sums = m.ap[:, 0:2], m.ap[:, 2:4]
                d = dve.tt(two[:, :, i * P:w], two[:, :, i * P:w], over(le, 2), ALU.add, stage[n])
                d = dve.maxneg(nm, two[:, :, 0:w], d, m.free)
                for br in range(2):
                    a = act.act(p.ap[:, br, 0:w], two[:, br, 0:w], ACT.Exp, d, p.free, bias=nm[:, br:br + 1], total=sums[:, br:br + 1])
                for b in pair:
                    b.free = [a]
                stage[n] = a

            def scale(n):
                t, g, i = units[n]
                head = t + 4 * g
                w = (i + 1) * P
                p, m = pp[n % 4], small[n % 3]
                sums = m.ap[:, 2:4]
                d = dve.recip(sums, sums, stage[n])
                d = dve.tt(sums, sums, gt[:, i, 3 * head + 1:3 * head + 3], ALU.mult, d)
                d2 = pool.ts(p.ap[:, 0, 0:w], p.ap[:, 0, 0:w], sums[:, 0:1], ALU.mult, d, s2=1.0, op1=ALU.mult)
                d3 = pool.ts(p.ap[:, 1, 0:w], p.ap[:, 1, 0:w], sums[:, 1:2], ALU.mult, d, s2=1.0, op1=ALU.mult)
                m.free = [d2, d3]
                stage[n] = [d2, d3]

            def third(n):
                t, g, i = units[n]
                p, y = pp[n % 4], pt[n % 2]
                for br in range(2):
                    b = bank[4 + br]
                    for j in range(i + 1):
                        x = pe.turn(b.ap[:, j * P:(j + 1) * P], p.ap[:, br, j * P:(j + 1) * P], ident, stage[n], b.free, signal=(j == i))
                    w = (i + 1) * P
                    z = (dve if br else act).copy(y.ap[:, br, 0:w], b.ap[:, 0:w], x, y.free)
                    b.free = [z]
                    stage[n, br] = z
                p.free = [x]

            def fourth(n):
                t, g, i = units[n]
                b, y = bank[6 + t % 2], pt[n % 2]
                o = b.ap[64 * g:64 * g + 64, i * P:(i + 1) * P]
                pe.mm(o, vcm[0:31, 64 * g:64 * g + 64], pct[0:31, 16 * g + 4 * t + i, :], True, False, b.free, stage["pct"], done_vcm)
                for br in range(2):
                    for j in range(i + 1):
                        end = br == 1 and j == i
                        x = pe.mm(o, vt[:, br, j, 64 * g:64 * g + 64], y.ap[:, br, j * P:(j + 1) * P], False, end, stage[n, br], values, signal=end)
                y.free = [x]
                if i == 3 and g == 1:
                    b.free = [store_parts(4 + t, b.ap, x, st["xused"])]
                    b.free += st["x"][4 + t]

            for n in range(len(units) + 3):
                if n < len(units):
                    first(n)
                    second(n)
                if 0 <= n - 1 < len(units):
                    scale(n - 1)
                if n == 2:
                    stage["pct"] = turn_compressed()
                if 0 <= n - 3:
                    fourth(n - 3)
                if 0 <= n - 2 < len(units):
                    third(n - 2)

        def nsa(l):
            fence(mem_free)
            outer = ExitStack()
            banks, temps = bank[2:8], tmp[0:5]
            scope = ExitStack()
            o = Attention(l, outer, scope, banks, temps)
            hres = sb(f"hres{l}", [P, 4, T], F32, scope)
            hg = Hgrn(l, hres, scope, banks, temps)
            o.done["cfree", 0] = None
            st["ticks"] = (2, 5)
            hg.project(0)
            o.plain(0)
            o.plain(1)
            spawn(o.compress(0))
            o.key(0)
            o.value(0)
            hg.project(1)
            o.key(1)
            o.value(1)
            o.gates()
            hg.project(2)
            spawn(o.compress(1))
            o.query(0)
            o.query(1)
            hg.project(3)
            o.hidden(0)
            o.query(2)
            o.query(3)

            def stored():
                for h in range(4):
                    while ("o", h) not in hg.done:
                        yield
                    store_parts(h, hres[:, h, :], st["xused"], hg.done["o", h])
                    yield

            spawn(stored())
            o.hidden(1)
            drain()
            st["ticks"] = (3,)
            fence(engines=(act, dve, pool))
            scope.close()
            scope = ExitStack()
            attend(o, scope)
            mem_free[:] = [(q.sem, q.n) for q in (pe, act, dve, pool)]
            scope.close()
            outer.close()


        for step in plan:
            kind, args = step[0], step[1:]
            nm = None
            if kind == "scale":
                prescale()
            elif kind == "ffn_ln":
                nm = Norm(False)
                ffn(0.5, nm)
                layer_norm(nm, args[0], args[1], *args[2:])
            elif kind == "ffn_rms":
                nm = Norm(True)
                ffn(1.0, nm)
                rms_norm(nm, args[0])
            elif kind == "ffn_end":
                ffn(1.0, None)
            elif kind == "rms":
                nm = Norm(True)
                for k in range(KD):
                    nm.add(k, st["xr"][k])
                rms_norm(nm, args[0])
            elif kind == "mlstm":
                mlstm()
                nm = Norm(False)
                out_proj(nm)
                layer_norm(nm, args[0], True)
            elif kind == "window":
                window()
                nm = Norm(False)
                out_proj(nm)
                layer_norm(nm, args[0], True)
            elif kind == "nsa":
                nsa(args[0])
                nm = Norm(True)
                out_proj(nm)
                rms_norm(nm, args[1])
        assert tile_n[0] == n_units * UT, (tile_n[0], n_units * UT)
        outs = out.rearrange("(k p) t -> p k t", p=P)
        for k in range(KD):
            sp.wait([st["xr"][k]])
            sp.items.append(("dma", lambda e, k=k: e.dma_start(outs[:, k, :], xr[:, k, :]), "out"))
        sp.items.append(("wait", "out", 16 * KD))

        block = ctx.enter_context(nc.Block())

        @block.sync
        def _(e):
            for kind, a, b in sp.items:
                if kind == "wait":
                    e.wait_ge(sems[a], b)
                else:
                    a(e).then_inc(sems[b], 16)

        @block.tensor
        def _(e):
            pe.play(e, sems)

        @block.vector
        def _(e):
            dve.play(e, sems)

        @block.scalar
        def _(e):
            act.play(e, sems)

        @block.gpsimd
        def _(e):
            pool.play(e, sems)


PLAN = [("scale",), ("ffn_ln", 0, True), ("mlstm", 1), ("ffn_ln", 2, True), ("ffn_ln", 3, True), ("window", 4),
        ("ffn_ln", 5, False, V_NM), ("nsa", 0, V_NF), ("ffn_rms", V_NM + 8), ("nsa", 1, V_NF + 8), ("ffn_end",)]


def columns(w, cols=None):
    w = np.asarray(w)
    if cols is None:
        cols = np.arange(w.shape[1])
    cols = np.asarray(cols)
    picked = w[:, np.maximum(cols, 0)]
    if (cols < 0).any():
        picked[:, cols < 0] = 0
    k, n = picked.shape
    return picked.reshape(k // P, P, n // P, P).transpose(2, 0, 1, 3).reshape(-1, P, P)


def head_pairs(order, dim=64):
    return np.concatenate([np.arange(h * dim, (h + 1) * dim) for h in order])


WIN_ORDER = [h for t in range(8) for h in ((t % 4) + 8 * (t // 4), (t % 4) + 4 + 8 * (t // 4))]
NSA_ORDER = [h for t in range(4) for h in (t, 4 + t)]


def stream(inp, plan):
    parts = []

    def ffn(w_in, w_out):
        w = columns(w_in).reshape(2, KF, KD, P, P)
        parts.append(w.transpose(1, 0, 2, 3, 4).reshape(-1, P, P))
        parts.append(columns(w_out))

    for step in plan:
        if step[0] == "ffn_ln":
            l, j = {0: (0, 0), 2: (0, 1), 3: (1, 0), 5: (1, 1)}[step[1]]
            ffn(inp["ffn_w_in"][l, j], inp["ffn_w_out"][l, j])
        elif step[0] in ("ffn_rms", "ffn_end"):
            l = 0 if step[0] == "ffn_rms" else 1
            ffn(inp["w_ffn_in_2"][l], inp["w_ffn_out_2"][l])
        elif step[0] == "mlstm":
            w = inp["ml_w_in"][0]
            g = np.full(P, -1)
            for q, at in enumerate((0, 64, 32, 96)):
                g[at:at + 4] = 3072 + 4 * q + np.arange(4)
            cols = [g]
            for h in range(4):
                cols += [P * h + np.arange(P), 512 + P * h + np.arange(P), 1024 + 2 * P * h + np.arange(2 * P)]
            parts.append(columns(w, np.concatenate(cols + [np.arange(2048, 3072)])))
            parts.append(columns(inp["ml_w_out"][0]))
        elif step[0] == "window":
            order = head_pairs(WIN_ORDER)
            parts.append(columns(inp["at_w_in"][0], np.concatenate([np.arange(1024, 1536), order])))
            parts.append(columns(inp["at_w_out"][0][order, :]))
        elif step[0] == "nsa":
            l = step[1]
            w = inp["w_in_2"][l]
            gate = np.full(P, -1)
            gate[:24] = 2048 + 512 + 768 + np.arange(24)
            order = head_pairs(NSA_ORDER)
            heads = [np.concatenate([np.arange(512 * i + P * h, 512 * i + P * h + P) for i in range(4)]) for h in range(4)]
            ck, cv, k0, v0, k1, v1 = (np.arange(2560 + P * i, 2560 + P * i + P) for i in range(6))
            q = (2048 + order).reshape(4, P)
            cols = [heads[0], ck, cv, k0, v0, heads[1], k1, v1, gate, heads[2], q[0], q[1], heads[3]]
            parts.append(columns(w, np.concatenate(cols)))
            for n in "kv":
                parts.append(columns(inp[f"cmp_w1_{n}_2"][l]).reshape(2, 16, P, P).transpose(1, 0, 2, 3).reshape(-1, P, P))
                if n == "k":
                    parts.append(columns(w, np.concatenate([q[2], q[3]])))
            rows = np.concatenate([np.arange(512), 512 + order])
            parts.append(columns(inp["w_out_2"][l][rows, :]))
    w = np.concatenate(parts)
    return np.ascontiguousarray(w.reshape(-1, UT, P, P).transpose(0, 2, 1, 3)).reshape(-1, P, UT * P)


def vectors(inp):
    v = np.zeros((P, V_N), np.float32)

    def put(at, a):
        a = np.asarray(a).reshape(-1, P)
        v[:, at:at + a.shape[0]] = a.T

    put(V_LNG, inp["ln_g"])
    put(V_LNB, inp["ln_b"])
    v[:, V_EPS] = LN_EPS
    v[:, V_EPS + 1] = RMS_EPS
    for q, at in enumerate((0, 64, 32, 96)):
        v[at:at + 4, V_GB] = inp["ml_gate_b"][0][4 * q:4 * q + 4]
    put(V_MNG, inp["ml_norm_g"])
    v[:, V_SINK:V_SINK + 16] = inp["at_sink"][0][WIN_ORDER][None, :]
    for l in range(2):
        put(V_LB + 4 * l, inp["hg_lb_logits_2"][l])
        v[:, V_HGN + l] = inp["hg_gnorm_2"][l]
        v[:, V_QG + l] = np.tile(inp["q_gain_2"][l], 2)
        for b in range(3):
            v[:, V_KG + 4 * l + b] = np.tile(inp["k_gain_2"][l, b], 2)
    put(V_NM, inp["norm_mix_2"])
    put(V_NF, inp["norm_ffn_2"])
    return v


def small_mats(inp):
    m = np.zeros((2, 2, P, 32 + 128), np.float32)
    for l in range(2):
        for i, n in enumerate("kv"):
            m[l, i, :, :32] = np.tile(inp[f"cmp_pe_{n}_2"][l].T, (2, 1))
            m[l, i, :, 32:] = inp[f"cmp_w2_{n}_2"][l].reshape(2, P, 64).transpose(1, 0, 2).reshape(P, 128)
    return m


def arrange(inp, plan, x):
    t = lay_tables()
    return {
        "in_x": np.ascontiguousarray(np.asarray(x).reshape(T, D).T),
        "in_w": stream(inp, plan),
        "in_vec": vectors(inp),
        "in_tab": np.concatenate([t[k] for k in SPANS], axis=1),
        "in_mat": small_mats(inp),
    }


def kernel(**inputs):
    import numpy as _np
    import concourse.bacc as _bacc
    from concourse import mybir as _mybir
    from concourse.bass_utils import run_bass_kernel_spmd as _run

    inp = {k: _np.asarray(v) for k, v in inputs.items()}
    arrays = arrange(inp, PLAN, inp["x"])
    nc = _bacc.Bacc("TRN2", target_bir_lowering=False, num_devices=1)
    args = [nc.dram_tensor(k, a.shape, _mybir.dt.float32, kind="ExternalInput").ap() for k, a in arrays.items()]
    args.append(nc.dram_tensor("out_0", [D, T], _mybir.dt.float32, kind="ExternalOutput").ap())
    build(nc, *args, PLAN)
    r = _run(nc, [arrays], core_ids=[0])
    return _np.ascontiguousarray(r.results[0]["out_0"].T).reshape(1, T, D)
```
